# Optimizing a Trainium2 kernel written in Bass

```python
import math
import jax, jax.numpy as jnp
from jax import lax
import numpy as np

D_MODEL = 1024
BATCH = 1
SEQ = 512
DEPTH = 2

N_A_LAYERS = max(1, DEPTH // 2)
N_B_LAYERS = DEPTH - N_A_LAYERS

A_HEADS = D_MODEL // 128
A_HEAD_DIM = 64
A_V_DIM = 2 * A_HEAD_DIM
A_QK_WIDTH = A_HEADS * 2 * A_HEAD_DIM
A_V_WIDTH = A_HEADS * A_V_DIM
LAMBDA_INIT_BASE = 0.8
LAMBDA_INIT_AMP = 0.6
LAMBDA_INIT_RATE = 0.3

ROPE_THETA = 500000.0
ROT_DIM = A_HEAD_DIM // 4

B_HEADS = D_MODEL // 64
B_HEAD_DIM = 64
B_WIDTH = B_HEADS * B_HEAD_DIM

D_FF = -(-8 * D_MODEL // (3 * 256)) * 256

Q_BLOCK = 128
EPS = 1e-6


def rms_norm(x, g):
    x32 = x.astype(jnp.float32)
    y = x32 * lax.rsqrt(jnp.mean(x32 * x32, axis=-1, keepdims=True) + EPS)
    return (y * g.astype(jnp.float32)).astype(x.dtype)

def rope_tables(seq):
    pos = jnp.arange(seq, dtype=jnp.float32)
    inv_freq = ROPE_THETA ** (-jnp.arange(0, ROT_DIM, 2, dtype=jnp.float32) / ROT_DIM)
    ang = pos[:, None] * inv_freq[None, :]
    return jnp.cos(ang), jnp.sin(ang)

def apply_partial_rope(t, cos, sin):
    half = ROT_DIM // 2
    t1 = t[..., :half].astype(jnp.float32)
    t2 = t[..., half:ROT_DIM].astype(jnp.float32)
    r1 = t1 * cos - t2 * sin
    r2 = t2 * cos + t1 * sin
    return jnp.concatenate([r1.astype(t.dtype), r2.astype(t.dtype), t[..., ROT_DIM:]], axis=-1)

def to_blocks(t):
    b, h, s, d = t.shape
    return t.reshape(b, h, s // Q_BLOCK, Q_BLOCK, d).transpose(2, 0, 1, 3, 4)

def from_blocks(o):
    nb, b, h, qb, d = o.shape
    return o.transpose(1, 0, 3, 2, 4).reshape(b, nb * qb, h, d)

def diff_attention(h, w_qkv, w_o, lq1, lk1, lq2, lk2, subln_g, lambda_init, cos, sin):
    b, s, _ = h.shape
    qkv = h @ w_qkv
    q, k, v = jnp.split(qkv, [A_QK_WIDTH, 2 * A_QK_WIDTH], axis=-1)
    q = q.reshape(b, s, 2 * A_HEADS, A_HEAD_DIM).transpose(0, 2, 1, 3)
    k = k.reshape(b, s, 2 * A_HEADS, A_HEAD_DIM).transpose(0, 2, 1, 3)
    v = v.reshape(b, s, A_HEADS, A_V_DIM).transpose(0, 2, 1, 3)
    q = apply_partial_rope(q, cos, sin)
    k = apply_partial_rope(k, cos, sin)
    f32 = jnp.float32
    lam = (jnp.exp(jnp.sum(lq1.astype(f32) * lk1.astype(f32)))
           - jnp.exp(jnp.sum(lq2.astype(f32) * lk2.astype(f32))) + lambda_init)
    scale = A_HEAD_DIM ** -0.5
    kpos = jnp.arange(s)
    n_blocks = s // Q_BLOCK

    def block(args):
        qb, start = args
        sc = jnp.einsum('bhqd,bhkd->bhqk', qb, k).astype(f32) * scale
        qpos = start + jnp.arange(Q_BLOCK)
        mask = kpos[None, :] <= qpos[:, None]
        p = jax.nn.softmax(jnp.where(mask, sc, -jnp.inf), axis=-1)
        p = p.reshape(b, A_HEADS, 2, Q_BLOCK, s)
        a = p[:, :, 0] - lam * p[:, :, 1]
        return jnp.einsum('bhqk,bhkd->bhqd', a.astype(v.dtype), v)

    o = lax.map(block, (to_blocks(q), jnp.arange(n_blocks) * Q_BLOCK))
    o = from_blocks(o)
    o = rms_norm(o, subln_g) * (1.0 - lambda_init)
    return o.reshape(b, s, A_V_WIDTH).astype(h.dtype) @ w_o

def stick_breaking_attention(h, w_q, w_o, k, v):
    b, s, _ = h.shape
    q = (h @ w_q).reshape(b, s, B_HEADS, B_HEAD_DIM).transpose(0, 2, 1, 3)
    f32 = jnp.float32
    scale = B_HEAD_DIM ** -0.5
    kpos = jnp.arange(s)
    n_blocks = s // Q_BLOCK

    def block(args):
        qb, start = args
        z = jnp.einsum('bhqd,bhkd->bhqk', qb, k).astype(f32) * scale
        qpos = start + jnp.arange(Q_BLOCK)
        mask = kpos[None, :] < qpos[:, None]
        log_beta = jax.nn.log_sigmoid(z)
        log_1m = jnp.where(mask, jax.nn.log_sigmoid(-z), 0.0)
        between = lax.cumsum(log_1m, axis=3, reverse=True) - log_1m
        a = jnp.where(mask, jnp.exp(log_beta + between), 0.0)
        return jnp.einsum('bhqk,bhkd->bhqd', a.astype(v.dtype), v)

    o = lax.map(block, (to_blocks(q), jnp.arange(n_blocks) * Q_BLOCK))
    o = from_blocks(o).reshape(b, s, B_WIDTH)
    return o @ w_o

def swiglu(h, w_gate_up, w_down):
    gate, up = jnp.split(h @ w_gate_up, 2, axis=-1)
    return (jax.nn.silu(gate) * up) @ w_down

def first_inputs(seed: int = 0) -> dict:
    key = jax.random.key(seed)
    ks = jax.random.split(key, 24)
    f32 = jnp.float32

    def w(k, shape, fan_in):
        return jax.random.normal(k, shape, f32) * (fan_in ** -0.5)

    def gain(k, shape):
        return 1.0 + 0.02 * jax.random.normal(k, shape, f32)

    return {
        'x': jax.random.normal(ks[0], (BATCH, SEQ, D_MODEL), f32),
        'a_w_qkv': w(ks[1], (N_A_LAYERS, D_MODEL, 2 * A_QK_WIDTH + A_V_WIDTH), D_MODEL),
        'a_w_o': w(ks[2], (N_A_LAYERS, A_V_WIDTH, D_MODEL), A_V_WIDTH),
        'a_lambda_q1': 0.1 * jax.random.normal(ks[3], (N_A_LAYERS, A_HEAD_DIM), f32),
        'a_lambda_k1': 0.1 * jax.random.normal(ks[4], (N_A_LAYERS, A_HEAD_DIM), f32),
        'a_lambda_q2': 0.1 * jax.random.normal(ks[5], (N_A_LAYERS, A_HEAD_DIM), f32),
        'a_lambda_k2': 0.1 * jax.random.normal(ks[6], (N_A_LAYERS, A_HEAD_DIM), f32),
        'a_subln_g': gain(ks[7], (N_A_LAYERS, A_V_DIM)),
        'kv_norm_g': gain(ks[8], (D_MODEL,)),
        'kv_w': w(ks[9], (D_MODEL, 2 * B_WIDTH), D_MODEL),
        'b_w_q': w(ks[10], (N_B_LAYERS, D_MODEL, B_WIDTH), D_MODEL),
        'b_w_o': w(ks[11], (N_B_LAYERS, B_WIDTH, D_MODEL), B_WIDTH),
        'mix_pre_g': gain(ks[12], (DEPTH, D_MODEL)),
        'mix_post_g': gain(ks[13], (DEPTH, D_MODEL)),
        'ffn_pre_g': gain(ks[14], (DEPTH, D_MODEL)),
        'ffn_post_g': gain(ks[15], (DEPTH, D_MODEL)),
        'ffn_w_gate_up': w(ks[16], (DEPTH, D_MODEL, 2 * D_FF), D_MODEL),
        'ffn_w_down': w(ks[17], (DEPTH, D_FF, D_MODEL), D_FF),
    }

def first_block(x, a_w_qkv, a_w_o, a_lambda_q1, a_lambda_k1, a_lambda_q2, a_lambda_k2,
              a_subln_g, kv_norm_g, kv_w, b_w_q, b_w_o, mix_pre_g, mix_post_g,
              ffn_pre_g, ffn_post_g, ffn_w_gate_up, ffn_w_down):
    b, s, _ = x.shape
    cos, sin = rope_tables(s)
    shared_k = None
    shared_v = None
    for layer in range(DEPTH):
        h = rms_norm(x, mix_pre_g[layer])
        if layer < N_A_LAYERS:
            lambda_init = LAMBDA_INIT_BASE - LAMBDA_INIT_AMP * math.exp(-LAMBDA_INIT_RATE * layer)
            m = diff_attention(h, a_w_qkv[layer], a_w_o[layer],
                               a_lambda_q1[layer], a_lambda_k1[layer],
                               a_lambda_q2[layer], a_lambda_k2[layer],
                               a_subln_g[layer], lambda_init, cos, sin)
        else:
            if shared_k is None:
                kv = rms_norm(x, kv_norm_g) @ kv_w
                kk, vv = jnp.split(kv, 2, axis=-1)
                shared_k = kk.reshape(b, s, B_HEADS, B_HEAD_DIM).transpose(0, 2, 1, 3)
                shared_v = vv.reshape(b, s, B_HEADS, B_HEAD_DIM).transpose(0, 2, 1, 3)
            j = layer - N_A_LAYERS
            m = stick_breaking_attention(h, b_w_q[j], b_w_o[j], shared_k, shared_v)
        x = x + rms_norm(m, mix_post_g[layer])
        f = swiglu(rms_norm(x, ffn_pre_g[layer]), ffn_w_gate_up[layer], ffn_w_down[layer])
        x = x + rms_norm(f, ffn_post_g[layer])
    return x


CHUNK = 64
MEM_LEN = 256
POOL_GROUPS = 4
POOL_WINDOWS = (2, 4, 8, 16)
POOL_WIDTH = D_MODEL // 2
POOL_GC = POOL_WIDTH // POOL_GROUPS
N_HEADS = 8
HEAD_DIM = 64
ATTN_WIDTH = N_HEADS * HEAD_DIM
IDX_HEADS = 8
IDX_DIM = 64
TOPK_MAX = 256
ATTN_SCALE = HEAD_DIM ** -0.5
IDX_W_SCALE = (IDX_DIM ** -0.5) * (IDX_HEADS ** -0.5)
MEM_HEADS = 4
MEM_HEAD_DIM = 128
MEM_WIDTH = MEM_HEADS * MEM_HEAD_DIM
MEM_SCALE = MEM_HEAD_DIM ** -0.5
N_BRANCH = 3
REL_BUCKETS = 32
REL_MAX_DIST = 1024
NEG = -1e30
IN_SPLITS = (POOL_WIDTH, POOL_WIDTH,
             ATTN_WIDTH, ATTN_WIDTH, ATTN_WIDTH, ATTN_WIDTH,
             IDX_HEADS * IDX_DIM, IDX_DIM, IDX_HEADS,
             MEM_WIDTH, MEM_WIDTH,
             N_BRANCH * D_MODEL)
IN_COLS = sum(IN_SPLITS)


def rms_norm_2(x, g):
    x32 = x.astype(jnp.float32)
    y = x32 * lax.rsqrt(jnp.mean(x32 * x32, axis=-1, keepdims=True) + EPS)
    return (y * g.astype(jnp.float32)).astype(x.dtype)

def rel_bucket(rel):
    half = REL_BUCKETS // 2
    max_exact = half // 2
    ret = jnp.where(rel > 0, half, 0)
    n = jnp.abs(rel)
    nf = jnp.maximum(n, 1).astype(jnp.float32)
    large = max_exact + (jnp.log(nf / max_exact) / math.log(REL_MAX_DIST / max_exact)
                         * (half - max_exact)).astype(jnp.int32)
    large = jnp.minimum(large, half - 1)
    return ret + jnp.where(n < max_exact, n, large)

def multi_scale_pool(u, pool_w, pool_scale):
    b, s, _ = u.shape
    ug = u.reshape(b, s, POOL_GROUPS, POOL_GC).astype(jnp.float32)
    cs = jnp.cumsum(ug, axis=1)
    cs = jnp.concatenate([jnp.zeros_like(cs[:, :1]), cs], axis=1)
    t = jnp.arange(s, dtype=jnp.int32)[:, None]
    win = jnp.asarray(POOL_WINDOWS, jnp.int32)[None, :]
    start = jnp.maximum(t + 1 - win, 0)
    grp = jnp.arange(POOL_GROUPS, dtype=jnp.int32)[None, :]
    lo = cs[:, start, grp, :]
    count = (t + 1 - start).astype(jnp.float32)[None, :, :, None]
    pooled = (cs[:, 1:] - lo) / count - ug
    mixed = jnp.einsum('bsgc,gcd->bsgd', pooled.astype(u.dtype), pool_w)
    return mixed.reshape(b, s, POOL_WIDTH) * pool_scale

def dsa_attention(q, k, v, iq, ik, iw, rel_bias):
    b, s = q.shape[:2]
    topk = min(TOPK_MAX, s // 4)
    nb = s // Q_BLOCK
    key_pos = jnp.arange(s, dtype=jnp.int32)
    ik32 = ik.astype(jnp.float32)
    gather = jax.vmap(lambda arr, idx: arr[idx])

    def to_blocks(a):
        return jnp.moveaxis(a.reshape((b, nb, Q_BLOCK) + a.shape[2:]), 1, 0)

    def block(args):
        qb, iqb, iwb, qpos = args
        limit = (qpos // CHUNK + 1) * CHUNK
        sc = jnp.einsum('bqhd,bsd->bqhs', iqb.astype(jnp.float32), ik32)
        index_score = jnp.einsum('bqhs,bqh->bqs', jax.nn.relu(sc),
                                 iwb.astype(jnp.float32) * IDX_W_SCALE)
        admissible = key_pos[None, :] < limit[:, None]
        index_score = jnp.where(admissible[None], index_score, NEG)
        _, idx = lax.top_k(index_score, topk)
        k_sel = gather(k, idx)
        v_sel = gather(v, idx)
        logits = jnp.einsum('bqhd,bqkhd->bqhk', qb, k_sel).astype(jnp.float32) * ATTN_SCALE
        bias = rel_bias[rel_bucket(idx - qpos[None, :, None])]
        logits = logits + jnp.moveaxis(bias, -1, 2).astype(jnp.float32)
        valid = idx < limit[None, :, None]
        logits = jnp.where(valid[:, :, None, :], logits, NEG)
        p = jax.nn.softmax(logits, axis=-1).astype(v.dtype)
        return jnp.einsum('bqhk,bqkhd->bqhd', p, v_sel)

    out = lax.map(block, (to_blocks(q), to_blocks(iq), to_blocks(iw),
                          key_pos.reshape(nb, Q_BLOCK)))
    return jnp.moveaxis(out, 0, 1).reshape(b, s, N_HEADS * HEAD_DIM)

def memory_attention(q, mem_k, mem_v):
    b, s = q.shape[:2]
    logits = jnp.einsum('bshd,bmhd->bhsm', q, mem_k).astype(jnp.float32) * MEM_SCALE
    p = jax.nn.softmax(logits, axis=-1).astype(mem_v.dtype)
    return jnp.einsum('bhsm,bmhd->bshd', p, mem_v).reshape(b, s, MEM_WIDTH)

def second_inputs(seed: int = 0) -> dict:
    key = jax.random.key(seed)
    ks = jax.random.split(key, 14)
    f32 = jnp.float32
    nrm = lambda k, shape, scale: jax.random.normal(k, shape, f32) * scale
    return {
        "x": nrm(ks[0], (BATCH, SEQ, D_MODEL), 1.0),
        "mem": nrm(ks[1], (BATCH, MEM_LEN, D_MODEL), 1.0),
        "norm_g": 1.0 + nrm(ks[2], (DEPTH, D_MODEL), 0.02),
        "w_in": nrm(ks[3], (DEPTH, D_MODEL, IN_COLS), D_MODEL ** -0.5),
        "pool_w": nrm(ks[4], (DEPTH, POOL_GROUPS, POOL_GC, POOL_GC), POOL_GC ** -0.5),
        "pool_scale": 1.0 + nrm(ks[5], (DEPTH, POOL_WIDTH), 0.02),
        "mem_norm_g": 1.0 + nrm(ks[6], (DEPTH, D_MODEL), 0.02),
        "w_mem_kv": nrm(ks[7], (DEPTH, D_MODEL, 2 * MEM_WIDTH), D_MODEL ** -0.5),
        "w_branch": nrm(ks[8], (DEPTH, N_BRANCH, POOL_WIDTH, D_MODEL), POOL_WIDTH ** -0.5),
        "w_out": nrm(ks[9], (DEPTH, D_MODEL, D_MODEL), D_MODEL ** -0.5),
        "rel_bias": nrm(ks[10], (REL_BUCKETS, N_HEADS), 0.5),
        "final_g": 1.0 + nrm(ks[11], (D_MODEL,), 0.02),
    }

def second_block(x, mem, norm_g, w_in, pool_w, pool_scale, mem_norm_g, w_mem_kv,
              w_branch, w_out, rel_bias, final_g):
    b, s, _ = x.shape
    split_points = np.cumsum(np.asarray(IN_SPLITS))[:-1].tolist()
    for l in range(DEPTH):
        h = rms_norm_2(x, norm_g[l])
        proj = h @ w_in[l]
        (pool_u, pool_z, aq, ak, av, az, iq, ik, iw, mq, mz, gates) = jnp.split(
            proj, split_points, axis=-1)

        y_pool = multi_scale_pool(pool_u, pool_w[l], pool_scale[l]) * jax.nn.silu(pool_z)

        y_attn = dsa_attention(
            aq.reshape(b, s, N_HEADS, HEAD_DIM), ak.reshape(b, s, N_HEADS, HEAD_DIM),
            av.reshape(b, s, N_HEADS, HEAD_DIM), iq.reshape(b, s, IDX_HEADS, IDX_DIM),
            ik, iw, rel_bias) * jax.nn.silu(az)

        mkv = rms_norm_2(mem, mem_norm_g[l]) @ w_mem_kv[l]
        mk, mv = jnp.split(mkv, 2, axis=-1)
        mm = mem.shape[1]
        y_mem = memory_attention(
            mq.reshape(b, s, MEM_HEADS, MEM_HEAD_DIM),
            mk.reshape(b, mm, MEM_HEADS, MEM_HEAD_DIM),
            mv.reshape(b, mm, MEM_HEADS, MEM_HEAD_DIM)) * jax.nn.silu(mz)

        g = jax.nn.sigmoid(gates).reshape(b, s, N_BRANCH, D_MODEL)
        merged = (g[:, :, 0] * (y_pool @ w_branch[l, 0])
                  + g[:, :, 1] * (y_attn @ w_branch[l, 1])
                  + g[:, :, 2] * (y_mem @ w_branch[l, 2]))
        x = x + merged @ w_out[l]
    return rms_norm_2(x, final_g)


def setup_inputs(seed=0):
    out = dict(first_inputs(seed))
    for name, value in second_inputs(seed + 1).items():
        if name != "x":
            out[name + "_2"] = value
    return out


def reference(
    x, a_w_qkv, a_w_o, a_lambda_q1, a_lambda_k1, a_lambda_q2, a_lambda_k2, a_subln_g, kv_norm_g,
    kv_w, b_w_q, b_w_o, mix_pre_g, mix_post_g, ffn_pre_g, ffn_post_g, ffn_w_gate_up, ffn_w_down,
    mem_2, norm_g_2, w_in_2, pool_w_2, pool_scale_2, mem_norm_g_2, w_mem_kv_2, w_branch_2,
    w_out_2, rel_bias_2, final_g_2,
):
    x = first_block(
        x, a_w_qkv, a_w_o, a_lambda_q1, a_lambda_k1, a_lambda_q2, a_lambda_k2, a_subln_g,
        kv_norm_g, kv_w, b_w_q, b_w_o, mix_pre_g, mix_post_g, ffn_pre_g, ffn_post_g,
        ffn_w_gate_up, ffn_w_down,
    )
    return second_block(
        x, mem_2, norm_g_2, w_in_2, pool_w_2, pool_scale_2, mem_norm_g_2, w_mem_kv_2,
        w_branch_2, w_out_2, rel_bias_2, final_g_2,
    )


_drawn_inputs = setup_inputs


def setup_inputs(seed=0):
    import zlib

    import numpy as np

    out = dict(_drawn_inputs(seed))
    spreads = {}
    factors = {'a_lambda_q2': 8.0,
     'kv_norm_g': 4.777,
     'ffn_post_g': 3.307,
     'mem_2': 2.706,
     'norm_g_2': 8.0,
     'pool_scale_2': 8.0,
     'mem_norm_g_2': 8.0,
     'rel_bias_2': 3.841}
    for name, (base, spread) in spreads.items():
        noise = np.random.default_rng([zlib.crc32(name.encode()), seed]).standard_normal(out[name].shape)
        drawn = base * np.exp(spread * noise) if base else spread * noise
        out[name] = __import__('jax').numpy.asarray(drawn.astype(out[name].dtype))
    for name, factor in factors.items():
        out[name] = (out[name] * factor).astype(out[name].dtype)
    return out
```

```python
import math

import numpy as np

import concourse.bass as bass
from concourse import mybir
from concourse.alu_op_type import AluOpType as ALU

F32 = mybir.dt.float32
F32R = mybir.dt.float32r
ACT = mybir.ActivationFunctionType
AX = mybir.AxisListType

P = 128
SEQ = 512
D = 1024
KD = D // P
QT = SEQ // P
D_FF = 2816
FF_TILES = D_FF // P
A_PAIRS = 8
NEG = -1e30
EPS = 1e-6
LAMBDA_INIT = 0.8 - 0.6 * math.exp(-0.3 * 0)
BLOCK_TILES = 8
RAW_SLOTS = 4
W_SLOTS = 2

GAINS = ["mix_pre0", "mix_post0", "ffn_pre0", "ffn_post0", "kv", "mix_pre1", "mix_post1", "ffn_pre1", "ffn_post1",
         "norm0", "norm1", "mem_norm0", "mem_norm1", "final"]
GAIN_AT = {name: KD * n for n, name in enumerate(GAINS)}
POOL_SCALE_AT = KD * len(GAINS)
SUBLN_AT = POOL_SCALE_AT + 2 * 4
LAMBDA_AT = SUBLN_AT + 1
N_PARAMS = LAMBDA_AT + 4

IDENT_AT, ROT_AT, CAUSAL_AT, STRICT_AT = 0, P, 2 * P, 3 * P
COUNT_AT = 4 * P
POOL_EDGE = 16
POOL_GROUPS = 4
N_TABLES = COUNT_AT + POOL_GROUPS * POOL_EDGE

LAYERS = 2
H_TILES = 4
IDX_PAIRS = 4
TOPK = 128
CHUNK = 64
MEM = 256
MEM_CHUNKS = MEM // P
TAKEN = -3e38
IDX_SCALE = 64 ** -0.5 * 8 ** -0.5
MEM_SCALE = 128 ** -0.5
REL_SPAN = SEQ + P
N_REL_HEADS = 8


class Tally:

    def __init__(self, n=0):
        self.n, self.turn, self.per = n, None, 0

    def at(self, ahead=0):
        if self.turn is None:
            return self.n + ahead
        return self.turn * self.per + (self.n + ahead)

    def next(self):
        self.n += 1
        return self.at()


class Turns:

    def __init__(self, eng, n, grow):
        self.eng, self.n, self.grow = eng, n, grow

    def __enter__(self):
        self.loop = self.eng.Fori(0, self.n)
        i = self.loop.__enter__()
        self.start = [(t, t.n) for t, _ in self.grow]
        for t, per in self.grow:
            t.turn, t.per = i, per
        return i

    def __exit__(self, *error):
        self.loop.__exit__(*error)
        if error[0] is None:
            grown = [t.n - n for t, n in self.start]
            assert grown == [per for _, per in self.grow], (grown, [per for _, per in self.grow])
            for (t, n), (_, per) in zip(self.start, self.grow):
                t.n, t.turn = n + per * self.n, None


def build(nc, ap):
    w_stream, n_blocks = ap["weights"], ap["weights"].shape[0]
    place = {"at": 16512}

    def region(start):
        place["at"] = start

    def sb(name, shape, dt=F32):
        size = 4 * int(np.prod(shape[1:]))
        t = nc.alloc_sbuf_tensor_at(name, shape, dt, offset=place["at"])
        place["at"] += size + (-size) % 32
        return t

    x = sb("x", [P, KD, SEQ])
    h_hi, h_lo = sb("h_hi", [P, KD, SEQ], F32R), sb("h_lo", [P, KD, SEQ], F32R)
    raw = sb("raw", [P, RAW_SLOTS, BLOCK_TILES * P])
    w_hi, w_lo = (sb(n, [P, W_SLOTS, BLOCK_TILES, P], F32R) for n in ("w_hi", "w_lo"))
    params = sb("params", [P, N_PARAMS])
    tables = sb("tables", [P, N_TABLES])
    ones = sb("ones", [P, P])
    eps = sb("eps", [P, 1])
    rstd, rstd_m = sb("rstd", [P, SEQ]), sb("rstd_m", [P, SEQ])
    negmax, rowsum, rinv = sb("negmax", [P, 2, 2]), sb("rowsum", [P, 2, 2]), sb("rinv", [P, 2])
    lam_prod, lam_exp, neg_lam = sb("lam_prod", [64, 2]), sb("lam_exp", [P, 2]), sb("neg_lam", [P, 1])
    sub_gain = sb("sub_gain", [P, 1])
    squares = sb("squares", [P, 2, SEQ])
    sum_at = place["at"]
    square_sum = sb("square_sum", [P, SEQ])
    region(sum_at)
    o_raw = sb("o_raw", [P, SEQ])
    stage_at = place["at"]

    plain, rot_sin = sb("plain", [P, 2, SEQ]), sb("rot_sin", [P, SEQ])
    o_sq, o_rstd = sb("o_sq", [P, SEQ]), sb("o_rstd", [P, SEQ])
    rope = sb("rope", [P, 2, SEQ])
    rel = sb("rel", [32, N_REL_HEADS + REL_SPAN])
    rel_rows = sb("rel_rows", [N_REL_HEADS, REL_SPAN])
    region(stage_at)
    g_hi, g_lo = sb("g_hi", [P, KD, SEQ], F32R), sb("g_lo", [P, KD, SEQ], F32R)
    q_now, k_now = sb("q_now", [P, 2, SEQ]), sb("k_now", [P, 2, SEQ])
    v_t = sb("v_t", [P, SEQ])
    v_now = sb("v_now", [P, 2, QT, P])
    probs = sb("probs", [P, 2, 2, SEQ])
    a_t = sb("a_t", [P, 2, QT, SEQ])
    softplus, decay = sb("softplus", [P, 2, SEQ]), sb("decay", [P, 2, 2, SEQ])
    o_hi, o_lo = sb("o_hi", [P, KD, SEQ], F32R), sb("o_lo", [P, KD, SEQ], F32R)
    end_a = place["at"]
    region(stage_at)
    m_attn = sb("m_attn", [P, KD, SEQ])
    region(stage_at)
    act_hi, act_lo = sb("act_hi", [P, FF_TILES, SEQ], F32R), sb("act_lo", [P, FF_TILES, SEQ], F32R)
    m_ffn = sb("m_ffn", [P, KD, SEQ])
    gate_s, up_s = sb("gate_s", [P, 2, SEQ]), sb("up_s", [P, 2, SEQ])
    region(stage_at)
    bias = sb("bias", [P, N_REL_HEADS, SEQ])
    y_attn = sb("y_attn_hi", [P, H_TILES, SEQ], F32R), sb("y_attn_lo", [P, H_TILES, SEQ], F32R)
    work_at = place["at"]
    aq, ak = sb("aq", [P, H_TILES, SEQ]), sb("ak", [P, H_TILES, SEQ])
    av = sb("av", [P, QT, H_TILES * P])
    iq, ik = sb("iq", [P, H_TILES, SEQ]), sb("ik", [P, SEQ])
    turn_in = sb("turn_in", [P, SEQ])
    chosen = sb("chosen", [P, QT, SEQ])
    az = sb("az", [P, H_TILES, SEQ])
    iw = sb("iw", [P, QT, 8])
    region(work_at + 56 * 1024)
    weights2 = sb("weights2", [P, 2, 2, SEQ])
    a2_at = place["at"]
    a2_t = sb("a2_t", [P, 2, QT, SEQ])
    y_now = sb("y_now", [P, SEQ])
    top8 = sb("top8", [P, 8])
    end_d = place["at"]
    region(a2_at)
    relu_s, index = sb("relu_s", [P, 2, 2, SEQ]), sb("index", [P, SEQ])
    region(work_at)
    y_mem = sb("y_mem_hi", [P, H_TILES, SEQ], F32R), sb("y_mem_lo", [P, H_TILES, SEQ], F32R)
    mem_hi, mem_lo = sb("mem_hi", [P, KD, MEM], F32R), sb("mem_lo", [P, KD, MEM], F32R)
    mem = sb("mem", [P, KD, MEM])
    mk, mv = sb("mk", [P, H_TILES, MEM]), sb("mv", [P, MEM_CHUNKS, H_TILES * P])
    mq = sb("mq", [P, H_TILES, SEQ])
    mz_at = place["at"]
    assert mz_at <= work_at + 56 * 1024
    region(work_at + 32768)
    mz = sb("mz", [P, H_TILES, SEQ])
    region(work_at + 16384)
    y_pool = sb("y_pool_hi", [P, H_TILES, SEQ], F32R), sb("y_pool_lo", [P, H_TILES, SEQ], F32R)
    pool_w = sb("pool_w", [P, POOL_GROUPS, P])
    pool_u, pool_a, pool_b = (sb(n, [P, POOL_EDGE + SEQ]) for n in ("pool_u", "pool_a", "pool_b"))
    pooled, pool_z = sb("pooled", [P, SEQ]), sb("pool_z", [P, SEQ])
    edge = sb("edge", [P, POOL_EDGE])
    region(work_at + 32768)
    sum_hi, sum_lo = sb("sum_hi", [P, KD, SEQ], F32R), sb("sum_lo", [P, KD, SEQ], F32R)
    gates, merged = sb("gates", [P, 2, 3, SEQ]), sb("merged", [P, 2, SEQ])
    part = sb("part", [P, SEQ])
    end_m = place["at"]
    assert max(end_d, end_m) <= nc.sbuf_usable_end, (end_d, end_m)
    region(work_at)
    result = sb("result", [P, KD, SEQ])

    lin = nc.alloc_psum_tensor("lin", [P, 2, SEQ], F32)
    score = nc.alloc_psum_tensor("score", [P, 2, 2, SEQ], F32)
    turn = nc.alloc_psum_tensor("turn", [P, SEQ], F32)
    outp = nc.alloc_psum_tensor("outp", [P, SEQ], F32)

    ident = tables[:, IDENT_AT:IDENT_AT + P]
    rot = tables[:, ROT_AT:ROT_AT + P]
    cos, sin = rope[:, 0, :], rope[:, 1, :]

    def gain(name, f):
        return params[:, GAIN_AT[name] + f:GAIN_AT[name] + f + 1]

    def sem(name):
        return nc.alloc_semaphore(name)

    raw_loaded = [sem(f"raw_loaded{i}") for i in range(RAW_SLOTS)]
    x_loaded, params_loaded, out_stored = sem("x_loaded"), sem("params_loaded"), sem("out_stored")
    hi_split, w_split, w_used = sem("hi_split"), sem("w_split"), sem("w_used")
    lin_written, lin_read = sem("lin_written"), sem("lin_read")
    score_written, exp_done, mixed = sem("score_written"), sem("exp_done"), sem("mixed")
    negmax_done, qk_ready = sem("negmax_done"), sem("qk_ready")
    turn_written, turn_read = sem("turn_written"), sem("turn_read")
    out_written, out_read = sem("out_written"), sem("out_read")
    logs_done, sticks_done, weights_done = sem("logs_done"), sem("sticks_done"), sem("weights_done")
    sub_rstd, sub_scaled, hi_done, lo_done = sem("sub_rstd"), sem("sub_scaled"), sem("hi_done"), sem("lo_done")
    silu_done, act_ready = sem("silu_done"), sem("act_ready")
    square_done = sem("square_done")
    stat_written, rstd_done = sem("stat_written"), sem("rstd_done")
    x_ready, h_ready = sem("x_ready"), sem("h_ready")
    const_done, sum_added = sem("const_done"), sem("sum_added")
    rel_written, rel_copied, rel_stored, bias_loaded = (
        sem(n) for n in ("rel_written", "rel_copied", "rel_stored", "bias_loaded"))
    relu_done, index_done, biased = sem("relu_done"), sem("index_done"), sem("biased")
    y_ready, mem_loaded, mem_exp, pool_ready = sem("y_ready"), sem("mem_loaded"), sem("mem_exp"), sem("pool_ready")
    gated, pool_loaded = sem("gated"), sem("pool_loaded")
    lam_ready, lam_summed, lam_done = sem("lam_ready"), sem("lam_summed"), sem("lam_done")
    v_step, a_step = sem("v_step"), sem("a_step")

    rel_tensor = nc.dram_tensor("rel_rows_dram", [N_REL_HEADS, REL_SPAN], F32)
    rel_dram = rel_tensor.ap()
    toeplitz = bass.AP(tensor=rel_dram.tensor, offset=0, ap=[[1, P], [REL_SPAN, N_REL_HEADS], [1, SEQ]])

    block = nc.Block()
    block.__enter__()

    @block.sync
    def _(sp):
        sp.dma_start(x[:], ap["x_t"].rearrange("c p n -> p c n")).then_inc(x_loaded, 16)
        sp.dma_start(params[:], ap["params"]).then_inc(params_loaded, 16)
        sp.dma_start(tables[:], ap["tables"]).then_inc(params_loaded, 16)
        sp.dma_start(rope[:], ap["rope"]).then_inc(params_loaded, 16)
        sp.dma_start(rel[:], ap["rel"]).then_inc(params_loaded, 16)

        def load(b, slot, count):
            sp.dma_start(raw[:, slot, :], w_stream[bass.ds(b, 1)].rearrange("a p n -> (a p) n")).then_inc(
                raw_loaded[slot], 16)

        for b in range(RAW_SLOTS):
            load(b, b, 16)
        with sp.Fori(1, n_blocks // RAW_SLOTS) as i:
            for slot in range(RAW_SLOTS):
                sp.wait_ge(w_split, RAW_SLOTS * i + (slot - RAW_SLOTS + 1))
                load(RAW_SLOTS * i + slot, slot, 16)
        for f in range(KD):
            sp.wait_ge(x_ready, KD * 4 + f + 1)
            sp.dma_start(ap["out_t"][f], result[:, f, :]).then_inc(out_stored, 16)
        sp.wait_ge(out_stored, 16 * KD)

    @block.gpsimd
    def _(pool):
        one = ones[:, 0:1].broadcast_to([P, BLOCK_TILES * P])
        pool.wait_ge(const_done, 1)
        with pool.Fori(0, n_blocks // RAW_SLOTS) as i:
            for slot in range(RAW_SLOTS):
                pool.wait_ge(raw_loaded[slot], 16 * i + 16)
                pool.wait_ge(w_used, RAW_SLOTS * i + (slot + 1))
                hi = w_hi[:, slot % W_SLOTS].rearrange("p c n -> p (c n)")
                lo = w_lo[:, slot % W_SLOTS].rearrange("p c n -> p (c n)")
                pool.tensor_tensor(hi, raw[:, slot, :], one, ALU.mult).then_inc(hi_split, 1)
                pool.wait_ge(hi_split, RAW_SLOTS * i + (slot + 1))
                pool.tensor_tensor(lo, raw[:, slot, :], hi.bitcast(F32), ALU.subtract).then_inc(w_split, 1)


    @block.tensor
    def _(pe):
        blocks, tiles = Tally(), Tally()
        lin_freed = Tally(0)
        scores_free, probs_in, turns_done, outs = Tally(), Tally(), Tally(), Tally()
        h_seen = {"n": 0}
        stats = Tally()
        pe.sem_inc(w_used, 1)
        pe.wait_ge(params_loaded, 64)
        pe.wait_ge(const_done, 2)

        def passes(out, slot, tile, hi, lo, first, last, signal_used):
            a = pe.matmul(out, w_hi[:, slot, tile, :], hi, start=first, stop=False)
            if signal_used:
                a.then_inc(w_used, 1)
            pe.matmul(out, w_hi[:, slot, tile, :], lo, start=False, stop=False)
            return pe.matmul(out, w_lo[:, slot, tile, :], hi, start=False, stop=last)

        def linear(hi, lo, chunks, ready=None, width=SEQ):
            pe.wait_ge(lin_read, tiles.at(1))
            bank = tiles.n % 2
            for c in range(chunks):
                if c % BLOCK_TILES == 0:
                    slot = blocks.n % W_SLOTS
                    pe.wait_ge(w_split, blocks.at(1))
                    blocks.next()
                if ready is not None:
                    pe.wait_ge(h_ready, h_base["n"] + ready * (c + 1))
                mm = passes(lin[:, bank, 0:width], slot, c % BLOCK_TILES, hi[:, c, :], lo[:, c, :], c == 0,
                            c == chunks - 1, c % BLOCK_TILES == 0)
            mm.then_inc(lin_written, 1)
            tiles.next()

        def rotate(which):
            pe.wait_ge(lin_read, tiles.at(2))
            bank = tiles.n % 2
            pe.matmul(lin[:, bank, :], rot, plain[:, which, :], start=True, stop=True).then_inc(lin_written, 1)
            tiles.next()

        def turn_v(parity):
            pe.wait_ge(lin_read, tiles.at(2))
            pe.wait_ge(turn_read, turns_done.at(1))
            for t in range(QT):
                mm = pe.transpose(turn[:, t * P:(t + 1) * P], v_t[:, t * P:(t + 1) * P], ident)
            mm.then_inc(turn_written, 1)
            turns_done.next()

        def scores(parity, t, free, mask_at):
            n = P * (t + 1)
            pe.wait_ge(free, scores_free.at(1))
            for e in range(2):
                half = slice(64 * e, 64 * e + 64)
                out = score[:, scores_free.n % 2, e, 0:n]
                pe.matmul(out, q_now[half, parity, t * P:(t + 1) * P], k_now[half, parity, 0:n], start=True,
                          stop=True)
                mm = pe.matmul(out[:, n - P:n], ident, tables[:, mask_at:mask_at + P], start=False, stop=True,
                               skip_group_check=True)
            mm.then_inc(score_written, 1)
            scores_free.next()

        def turn_probs(t, e, ready):
            pe.wait_ge(ready, probs_in.at(1))
            pe.wait_ge(turn_read, turns_done.at(1))
            for c in range(t + 1):
                mm = pe.transpose(turn[:, c * P:(c + 1) * P], probs[:, t % 2, e, c * P:(c + 1) * P], ident)
            mm.then_inc(turn_written, 1)
            turns_done.next()

        def stat(source, ready, count):
            pe.wait_ge(ready, count)
            pe.wait_ge(out_read, outs.at(1))
            pe.matmul(outp[:], ones[:], source, start=True, stop=True).then_inc(out_written, 1)
            outs.next()

        qk = Tally()

        def a_period(parity, prev=True, cur=True, nxt=True):
            other = 1 - parity
            if cur:
                qk.n += 2
                pe.wait_ge(qk_ready, qk.at())
                scores(parity, 3, exp_done, CAUSAL_AT)
            if prev:
                turn_probs(0, 0, mixed)
                probs_in.next()
            if nxt:
                first_linear() if not cur else linear(h_hi, h_lo, KD)
            if prev:
                a_values(other)
            if cur:
                scores(parity, 2, exp_done, CAUSAL_AT)
                turn_probs(3, 0, mixed)
                probs_in.next()
            if nxt:
                rotate(0)
                linear(h_hi, h_lo, KD)
            if prev:
                pe.wait_ge(out_read, outs.at(1))
                pe.matmul(outp[:], ones[:], o_sq[:], start=True, stop=True).then_inc(out_written, 1)
                outs.next()
            if cur:
                scores(parity, 1, exp_done, CAUSAL_AT)
                turn_probs(2, 0, mixed)
                probs_in.next()
            if nxt:
                rotate(1)
                linear(h_hi, h_lo, KD)
            if cur:
                scores(parity, 0, exp_done, CAUSAL_AT)
                turn_probs(1, 0, mixed)
                probs_in.next()
            if nxt:
                turn_v(other)

        def a_values(parity):
            pe.wait_ge(turn_read, turns_done.at(1))
            pe.wait_ge(out_read, outs.at(1))
            for c in range(QT):
                mm = pe.matmul(outp[:, c * P:SEQ], v_now[:, parity, c, :], a_t[:, 0, c, c * P:SEQ], start=(c == 0),
                               stop=(c == QT - 1), skip_group_check=True)
            mm.then_inc(out_written, 1)
            outs.next()

        def b_values(parity):
            pe.wait_ge(turn_read, turns_done.at(1))
            pe.wait_ge(out_read, outs.at(1))
            for e in range(2):
                half = slice(64 * e, 64 * e + 64)
                for c in range(QT):
                    mm = pe.matmul(outp[half, c * P:SEQ], v_now[:, parity, c, half], a_t[:, e, c, c * P:SEQ],
                                   start=(c == 0), stop=(c == QT - 1), skip_group_check=True)
            mm.then_inc(out_written, 1)
            outs.next()

        def b_period(parity, prev=True, cur=True, nxt=True):
            other = 1 - parity
            if cur:
                pe.wait_ge(lin_read, tiles.at(2))
                scores(parity, 3, sticks_done, STRICT_AT)
            if prev:
                turn_probs(0, 0, weights_done)
                turn_probs(0, 1, weights_done)
                probs_in.next()
            if nxt:
                first_linear(2) if not cur else linear(h_hi, h_lo, KD)
            if prev:
                b_values(other)
            if cur:
                scores(parity, 2, sticks_done, STRICT_AT)
                turn_probs(3, 0, weights_done)
                turn_probs(3, 1, weights_done)
                probs_in.next()
            if nxt:
                linear(g_hi, g_lo, KD)
            if cur:
                scores(parity, 1, sticks_done, STRICT_AT)
                turn_probs(2, 0, weights_done)
                turn_probs(2, 1, weights_done)
                probs_in.next()
            if nxt:
                linear(g_hi, g_lo, KD)
            if cur:
                scores(parity, 0, sticks_done, STRICT_AT)
                turn_probs(1, 0, weights_done)
                turn_probs(1, 1, weights_done)
                probs_in.next()
            if nxt:
                turn_v(other)

        h_base, sums = {"n": 0}, Tally(2)

        def first_linear(copies=1):
            linear(h_hi, h_lo, KD, copies)
            h_base["n"] += copies * KD
            norm_stats()

        def norm_stats(width=SEQ):
            sums.n += KD
            pe.wait_ge(sum_added, sums.at())
            pe.wait_ge(out_read, outs.at(1))
            pe.matmul(outp[:, 0:width], ones[:], square_sum[:, 0:width], start=True, stop=True).then_inc(
                out_written, 1)
            outs.next()

        def ffn():
            def both():
                linear(h_hi, h_lo, KD)
                linear(h_hi, h_lo, KD)

            first_linear()
            linear(h_hi, h_lo, KD)
            both()
            with Turns(pe, FF_TILES // 2 - 1, [(blocks, 4), (tiles, 4)]) as i:
                for u in range(2):
                    both()
            pe.wait_ge(lo_done, lo_base["n"] + FF_TILES)
            lo_base["n"] += FF_TILES
            with Turns(pe, KD // 2, [(blocks, 6), (tiles, 2)]):
                for u in range(2):
                    linear(act_hi, act_lo, FF_TILES)

        lo_base = {"n": 0}

        def project_out():
            pe.wait_ge(lo_done, lo_base["n"] + KD)
            lo_base["n"] += KD
            with Turns(pe, KD // 2, [(blocks, 2), (tiles, 2)]):
                for u in range(2):
                    linear(o_hi, o_lo, KD)

        for half in range(2):
            mm = pe.matmul(score[0:N_REL_HEADS, 1, half, 0:REL_SPAN // 2], rel[:, 0:N_REL_HEADS],
                           rel[:, N_REL_HEADS + half * (REL_SPAN // 2):N_REL_HEADS + (half + 1) * (REL_SPAN // 2)],
                           start=True, stop=True)
        mm.then_inc(rel_written, 1)
        pe.wait_ge(rel_copied, 1)
        pe.wait_ge(lam_ready, 1)
        pe.matmul(score[:, 0, 0, 0:2], ones[0:64, :], lam_prod[:], start=True, stop=True).then_inc(lam_summed, 1)
        pe.wait_ge(lam_done, 1)
        a_period(1, False, False, True)
        a_period(0, False, True, True)
        with Turns(pe, 3, [(blocks, 6), (tiles, 10), (scores_free, 8), (probs_in, 8), (turns_done, 10), (outs, 4),
                           (qk, 4)]):
            a_period(1)
            a_period(0)
        a_period(1, True, True, False)
        a_period(0, True, False, False)
        project_out()
        norm_stats()
        ffn()
        norm_stats()
        scores_free.n = probs_in.n = 0
        pe.wait_ge(exp_done, 2 + QT * A_PAIRS)
        b_period(1, False, False, True)
        b_period(0, False, True, True)
        with Turns(pe, 3, [(blocks, 6), (tiles, 6), (scores_free, 8), (probs_in, 8), (turns_done, 18), (outs, 2)]):
            b_period(1)
            b_period(0)
        b_period(1, True, True, False)
        b_period(0, True, False, False)
        project_out()
        norm_stats()
        ffn()
        norm_stats()

        relus, biases, mem_exps, mixes, ys = Tally(), Tally(), Tally(), Tally(QT * A_PAIRS), Tally(lo_base["n"])

        def turn_tile(source, chunks):
            pe.wait_ge(lin_read, tiles.at(2))
            pe.wait_ge(turn_read, turns_done.at(1))
            for t in range(chunks):
                mm = pe.transpose(turn[:, t * P:(t + 1) * P], source[:, t * P:(t + 1) * P], ident)
            mm.then_inc(turn_written, 1)
            turns_done.next()

        def index_scores(t):
            n = P * (t + 1)
            for pair in range(IDX_PAIRS):
                pe.wait_ge(relu_done, relus.at(1))
                for e in range(2):
                    half = slice(64 * e, 64 * e + 64)
                    mm = pe.matmul(score[:, relus.n % 2, e, 0:n], iq[half, pair, t * P:(t + 1) * P], ik[half, 0:n],
                                   start=True, stop=True)
                mm.then_inc(score_written, 1)
                relus.next()

        def sparse_scores(pair, t):
            n = P * (t + 1)
            pe.wait_ge(biased, biases.at(1))
            for e in range(2):
                half = slice(64 * e, 64 * e + 64)
                mm = pe.matmul(score[:, biases.n % 2, e, 0:n], aq[half, pair, t * P:(t + 1) * P], ak[half, pair, 0:n],
                               start=True, stop=True)
            mm.then_inc(score_written, 1)
            biases.next()

        def sparse_turn(t, slot):
            pe.wait_ge(mixed, mixes.next())
            for e in range(2):
                pe.wait_ge(turn_read, turns_done.at(1))
                for c in range(t + 1):
                    mm = pe.transpose(turn[:, c * P:(c + 1) * P], weights2[:, slot, e, c * P:(c + 1) * P], ident)
                mm.then_inc(turn_written, 1)
                turns_done.next()

        def sparse_values(pair):
            pe.wait_ge(turn_read, turns_done.at(1))
            pe.wait_ge(out_read, outs.at(1))
            for e in range(2):
                half = slice(64 * e, 64 * e + 64)
                for c in range(QT):
                    mm = pe.matmul(outp[half, c * P:SEQ], av[:, c, pair * P + 64 * e:pair * P + 64 * e + 64],
                                   a2_t[:, e, c, c * P:SEQ], start=(c == 0), stop=(c == QT - 1),
                                   skip_group_check=True)
            mm.then_inc(out_written, 1)
            outs.next()

        def mem_scores(pair, t):
            pe.wait_ge(mem_exp, mem_exps.at(1))
            for e in range(2):
                head = 2 * pair + e
                mm = pe.matmul(score[:, mem_exps.n % 2, e, 0:MEM], mq[:, head, t * P:(t + 1) * P], mk[:, head, :],
                               start=True, stop=True)
            mm.then_inc(score_written, 1)
            mem_exps.next()

        def mem_turn(slot):
            pe.wait_ge(mixed, mixes.next())
            pe.wait_ge(turn_read, turns_done.at(1))
            for e in range(2):
                for c in range(MEM_CHUNKS):
                    at = (MEM_CHUNKS * e + c) * P
                    mm = pe.transpose(turn[:, at:at + P], weights2[:, slot, e, c * P:(c + 1) * P], ident)
            mm.then_inc(turn_written, 1)
            turns_done.next()

        def mem_values(pair):
            pe.wait_ge(turn_read, turns_done.at(1))
            for e in range(2):
                pe.wait_ge(out_read, outs.at(1))
                for c in range(MEM_CHUNKS):
                    mm = pe.matmul(outp[:], mv[:, c, (2 * pair + e) * P:(2 * pair + e + 1) * P], a2_t[:, e, c, :],
                                   start=(c == 0), stop=(c == MEM_CHUNKS - 1))
                mm.then_inc(out_written, 1)
                outs.next()

        def branch(y, tile_base, first_slot, second_slot, b):
            pe.wait_ge(lin_read, tiles.at(1))
            for c in range(H_TILES):
                at = H_TILES * b + c
                if at % BLOCK_TILES == 0:
                    pe.wait_ge(w_split, blocks.next())
                slot = (blocks.n - 1) % W_SLOTS
                mm = passes(lin[:, tiles.n % 2, :], slot, at % BLOCK_TILES, y[0][:, c, :], y[1][:, c, :], c == 0,
                            c == H_TILES - 1, at % BLOCK_TILES == 0)
            mm.then_inc(lin_written, 1)
            tiles.next()

        def two_layer():
            first_linear()
            for f in range(1, H_TILES + 2):
                linear(h_hi, h_lo, KD)
            turn_tile(turn_in, QT)
            for t, source in ((3, None), (2, None), (1, turn_in)):
                index_scores(t)
                if source is None:
                    with Turns(pe, H_TILES // 2, [(blocks, 2), (tiles, 2)]):
                        for u in range(2):
                            linear(h_hi, h_lo, KD)
                else:
                    for u in range(H_TILES):
                        linear(h_hi, h_lo, KD)
                        turn_tile(turn_in, QT)
            with Turns(pe, H_TILES // 2, [(blocks, 2), (tiles, 2)]):
                for u in range(2):
                    linear(h_hi, h_lo, KD)
            pe.wait_ge(lin_read, tiles.at(2))
            pe.wait_ge(relu_done, relus.at(2))
            steps = [(pair, t) for pair in range(H_TILES) for t in (3, 2, 1, 0)]
            for n, (pair, t) in enumerate(steps):
                sparse_scores(pair, t)
                if n:
                    sparse_turn(steps[n - 1][1], (n - 1) % 2)
                if n and t == 3:
                    sparse_values(pair - 1)
            sparse_turn(0, 1)
            sparse_values(H_TILES - 1)
            with Turns(pe, H_TILES, [(blocks, 2), (tiles, 2)]):
                for u in range(2):
                    linear(h_hi, h_lo, KD)
            linear(mem_hi, mem_lo, KD, 1, MEM)
            h_base["n"] += KD
            norm_stats(MEM)
            for f in range(1, H_TILES):
                linear(mem_hi, mem_lo, KD, None, MEM)
            for f in range(H_TILES):
                linear(mem_hi, mem_lo, KD, None, MEM)
                turn_tile(weights2[:, 0, 0, :], MEM_CHUNKS)
            pe.wait_ge(lin_read, tiles.at(2))
            pe.wait_ge(biased, biases.at(2))
            steps = [(pair, t) for pair in range(H_TILES // 2) for t in (3, 2, 1, 0)]
            for n, (pair, t) in enumerate(steps):
                mem_scores(pair, t)
                if n:
                    mem_turn((n - 1) % 2)
                if n and t == 3:
                    mem_values(pair - 1)
            mem_turn(1)
            mem_values(H_TILES // 2 - 1)
            pe.wait_ge(pool_loaded, pool_loads.next() * 16)
            for g in range(POOL_GROUPS):
                linear(h_hi, h_lo, KD)
                linear(h_hi, h_lo, KD)
                pe.wait_ge(pool_ready, pools.next())
                pe.wait_ge(lin_read, tiles.at(1))
                pe.matmul(lin[:, tiles.n % 2, :], pool_w[:, g, :], pooled[:], start=True, stop=True).then_inc(
                    lin_written, 1)
                tiles.next()
            ys.n += 3 * H_TILES
            pe.wait_ge(lo_done, ys.at())
            with Turns(pe, KD // 2, [(blocks, 10), (tiles, 12)]):
                for u in range(2):
                    for b in range(3):
                        linear(h_hi, h_lo, KD)
                    for b, y in enumerate((y_pool, y_attn, y_mem)):
                        branch(y, 0, 0, 0, b)
            ys.n += KD
            pe.wait_ge(lo_done, ys.at())
            with Turns(pe, KD // 2, [(blocks, 2), (tiles, 2)]):
                for u in range(2):
                    linear(sum_hi, sum_lo, KD)

        pools, pool_loads = Tally(), Tally()
        for layer in range(LAYERS):
            two_layer()
        norm_stats()

    @block.scalar
    def _(act):
        step = Tally()
        act.sem_inc(turn_read, 1)
        act.sem_inc(out_read, 1)
        act.sem_inc(exp_done, 2)
        turned, outs, negs, exps = Tally(), Tally(), Tally(), Tally()
        scored, sticks, subs, lins = Tally(), Tally(), Tally(), Tally()
        sq_in, his = Tally(), Tally()

        def then_wait(ins):
            ins.then_inc(a_step, 1)
            act.wait_ge(a_step, step.next())

        def soft_exp(t):
            n = P * (t + 1)
            act.wait_ge(negmax_done, negs.next())
            slot = (negs.n - 1) % 2
            for e in range(2):
                i = act.activation(probs[:, t % 2, e, 0:n], score[:, slot, e, 0:n], ACT.Exp,
                                   bias=negmax[:, slot, e:e + 1], accum_out=rowsum[:, slot, e:e + 1])
            i.then_inc(exp_done, 1)

        def keep_turned(t, e):
            act.wait_ge(turn_written, turned.next())
            act.activation(a_t[:, e, 0:t + 1, t * P:(t + 1) * P],
                           turn[:, 0:(t + 1) * P].rearrange("p (c n) -> p c n", n=P), ACT.Copy).then_inc(turn_read, 1)

        def keep_values(parity):
            act.wait_ge(turn_written, turned.next())
            act.activation(v_now[:, parity].rearrange("p c n -> p (c n)"), turn[:], ACT.Copy).then_inc(turn_read, 1)

        def to_rstd(out, width, signal, tally_out):
            act.wait_ge(out_written, tally_out.next())
            act.activation(out, outp[:, 0:out.shape[1]], ACT.Ln, bias=eps[:, 0:1], scale=1.0 / width).then_inc(out_read, 1)
            act.wait_ge(out_read, tally_out.at(1))
            act.activation(out, out, ACT.Exp, scale=-0.5).then_inc(signal, 1)

        def a_period(parity, pair, prev=True, cur=True, nxt=True):
            other = 1 - parity
            if cur:
                soft_exp(3)
            if prev:
                keep_turned(0, 0)
                act.wait_ge(out_written, outs.next())
                act.activation(o_raw[:], outp[:], ACT.Copy)
                act.activation(o_sq[:], outp[:], ACT.Square).then_inc(out_read, 1)
            if cur:
                soft_exp(2)
                keep_turned(3, 0)
            if prev:
                to_rstd(o_rstd[:], P, sub_rstd, outs)
            if cur:
                soft_exp(1)
                keep_turned(2, 0)
            if prev:
                act.wait_ge(sub_scaled, subs.next())
                act.activation(o_hi[:, bass.ds(pair - 1, 1), :], o_sq[:], ACT.Copy,
                               scale=sub_gain[:, 0:1]).then_inc(hi_done, 1)
            if cur:
                soft_exp(0)
                keep_turned(1, 0)
            if nxt:
                keep_values(other)

        def b_logs(t):
            n = P * (t + 1)
            act.wait_ge(score_written, scored.next())
            z, out = score[:, (scored.n - 1) % 2, :, 0:n], decay[:, t % 2, :, 0:n]
            then_wait(act.activation(out, z, ACT.Abs))
            then_wait(act.activation(out, out, ACT.Exp, scale=-1.0))
            act.activation(out, out, ACT.Ln, bias=ones[:, 0:1]).then_inc(logs_done, 1)

        def b_weights(t):
            n = P * (t + 1)
            act.wait_ge(sticks_done, sticks.next())
            act.activation(probs[:, t % 2, :, 0:n], decay[:, t % 2, :, 0:n], ACT.Exp).then_inc(weights_done, 1)

        def b_period(parity, pair, prev=True, cur=True, nxt=True):
            other = 1 - parity
            if cur:
                b_logs(3)
            if prev:
                keep_turned(0, 0)
                keep_turned(0, 1)
                act.wait_ge(out_written, outs.next())
                act.activation(o_hi[:, bass.ds(pair - 1, 1), :], outp[:], ACT.Copy).then_inc(hi_done, 1)
                act.activation(o_raw[:], outp[:], ACT.Copy).then_inc(out_read, 1)
            if cur:
                for t in (3, 2, 1):
                    b_logs(t - 1)
                    b_weights(t)
                    keep_turned(t, 0)
                    keep_turned(t, 1)
            if nxt:
                keep_values(other)
            if cur:
                b_weights(0)

        sq = Tally()

        def out_squares(m):
            def one(f, k):
                act.wait_ge(lin_read, lins.next())
                act.wait_ge(sum_added, sq.at(1))
                act.activation(squares[:, k, :], m[:, bass.ds(f, 1), :], ACT.Square).then_inc(square_done, 1)
                sq.next()

            with Turns(act, KD // 2, [(lins, 2), (sq, 2)]) as i:
                for k in range(2):
                    one(2 * i + k, k)

        xs = Tally()

        def norm_in(names, ready=x_ready, counts=None, source=x, width=SEQ):
            counts = xs if counts is None else counts
            for f in range(KD):
                if ready is not None:
                    act.wait_ge(ready, counts.next())
                act.wait_ge(sum_added, sq.at(1))
                act.activation(squares[:, f % 2, 0:width], source[:, f, :], ACT.Square).then_inc(square_done, 1)
                sq.next()
                for name, hi in names:
                    act.activation(hi[:, f, :], source[:, f, :], ACT.Copy, scale=gain(name, f)).then_inc(hi_done, 1)

        def ffn():
            def one(j, u, first):
                act.wait_ge(lin_read, lins.next())
                act.activation(gate_s[:, u, :], gate_s[:, u, :], ACT.Silu).then_inc(silu_done, 1)
                lins.next()
                act.wait_ge(act_ready, acts.next())
                act.activation(act_hi[:, bass.ds(j, 1), :], up_s[:, u, :], ACT.Copy).then_inc(hi_done, 1)

            for u in range(2):
                one(u, u, True)
            with Turns(act, FF_TILES // 2 - 1, [(lins, 4), (acts, 2)]) as i:
                for u in range(2):
                    one(2 * i + (u + 2), u, False)

        acts = Tally()

        act.sem_inc(sum_added, 2)
        act.wait_ge(const_done, 2)
        act.wait_ge(params_loaded, 64)
        act.wait_ge(rel_written, 1)
        for half in range(2):
            i = act.activation(rel_rows[:, half * (REL_SPAN // 2):(half + 1) * (REL_SPAN // 2)],
                               score[0:N_REL_HEADS, 1, half, 0:REL_SPAN // 2], ACT.Copy)
        i.then_inc(rel_copied, 1)
        act.wait_ge(rel_copied, 1)
        act.dma_start(rel_dram, rel_rows[:]).then_inc(rel_stored, 16)
        act.wait_ge(lam_summed, 1)
        act.activation(lam_exp[:], score[:, 0, 0, 0:2], ACT.Exp).then_inc(lam_done, 1)
        act.wait_ge(x_loaded, 16)
        norm_in([("mix_pre0", h_hi)], ready=None)
        to_rstd(rstd[:], D, rstd_done, outs)
        lins.n = 2
        a_period(1, None, False, False, True)
        a_period(0, 0, False, True, True)
        with Turns(act, 3, [(negs, 8), (turned, 10), (outs, 4), (subs, 2)]) as i:
            a_period(1, 2 * i + 1)
            a_period(0, 2 * i + 2)
        a_period(1, 7, True, True, False)
        a_period(0, 8, True, False, False)
        lins.n += 5 * A_PAIRS
        act.wait_ge(rel_stored, 16)
        out_squares(m_attn)
        to_rstd(rstd_m[:], D, rstd_done, outs)
        norm_in([("ffn_pre0", h_hi)])
        to_rstd(rstd[:], D, rstd_done, outs)
        ffn()
        out_squares(m_ffn)
        to_rstd(rstd_m[:], D, rstd_done, outs)
        norm_in([("mix_pre1", h_hi), ("kv", g_hi)])
        to_rstd(rstd[:], D, rstd_done, outs)
        scored.n = QT * A_PAIRS
        sticks.n = 2
        b_period(1, None, False, False, True)
        b_period(0, 0, False, True, True)
        with Turns(act, 3, [(step, 16), (scored, 8), (sticks, 8), (turned, 18), (outs, 2)]) as i:
            b_period(1, 2 * i + 1)
            b_period(0, 2 * i + 2)
        b_period(1, 7, True, True, False)
        b_period(0, 8, True, False, False)
        lins.n += 3 * A_PAIRS
        out_squares(m_attn)
        to_rstd(rstd_m[:], D, rstd_done, outs)
        norm_in([("ffn_pre1", h_hi)])
        to_rstd(rstd[:], D, rstd_done, outs)
        ffn()
        out_squares(m_ffn)
        to_rstd(rstd_m[:], D, rstd_done, outs)
        act.sem_inc(relu_done, 2)
        act.sem_inc(mem_exp, 2)
        act.dma_start(bias[:], toeplitz).then_inc(bias_loaded, 16)
        norm_in([("norm0", h_hi)])
        to_rstd(rstd[:], D, rstd_done, outs)
        scored.n = 2 * QT * A_PAIRS
        ready_y = Tally()

        def index_relu(t):
            n = P * (t + 1)
            for pair in range(IDX_PAIRS):
                act.wait_ge(score_written, scored.next())
                act.wait_ge(index_done, relued.at(1))
                act.activation(relu_s[:, relued.n % 2, :, 0:n], score[:, relued.n % 2, :, 0:n], ACT.Relu).then_inc(
                    relu_done, 1)
                relued.next()

        relued = Tally()

        def keep(out, chunks, cols=P):
            act.wait_ge(turn_written, turned.next())
            act.activation(out, turn[:, 0:chunks * P].rearrange("p (c n) -> p c n", n=P)[:, :, 0:cols],
                           ACT.Copy).then_inc(turn_read, 1)

        def sparse_exp(t, slot):
            n = P * (t + 1)
            act.wait_ge(negmax_done, negs.next())
            for e in range(2):
                i = act.activation(weights2[:, slot, e, 0:n], weights2[:, slot, e, 0:n], ACT.Exp,
                                   bias=negmax[:, slot, e:e + 1], accum_out=rowsum[:, slot, e:e + 1])
            i.then_inc(exp_done, 1)

        def sparse_keep(t):
            for e in range(2):
                keep(a2_t[:, e, 0:t + 1, t * P:(t + 1) * P], t + 1)

        def take_out():
            act.wait_ge(out_written, outs.next())
            act.activation(o_raw[:], outp[:], ACT.Copy).then_inc(out_read, 1)

        def y_hi(y, f):
            act.wait_ge(y_ready, ready_y.next())
            act.activation(y[0][:, f, :], y_now[:], ACT.Copy).then_inc(hi_done, 1)

        def mem_soft(slot):
            act.wait_ge(negmax_done, negs.next())
            for e in range(2):
                i = act.activation(weights2[:, slot, e, 0:MEM], score[:, slot, e, 0:MEM], ACT.Exp,
                                   bias=negmax[:, slot, e:e + 1], accum_out=rowsum[:, slot, e:e + 1])
            i.then_inc(mem_exp, 1)

        def mem_keep(t):
            act.wait_ge(turn_written, turned.next())
            act.activation(a2_t[:, :, 0:MEM_CHUNKS, t * P:(t + 1) * P],
                           turn[:].rearrange("p (e c n) -> p e c n", e=2, n=P), ACT.Copy).then_inc(turn_read, 1)

        def two_layer(layer):
            lins.n += H_TILES + 2
            keep(iw[:], QT, 8)
            for t in (3, 2, 1):
                index_relu(t)
                lins.n += H_TILES
                if t == 1:
                    for f in range(H_TILES):
                        keep(av[:, :, f * P:(f + 1) * P], QT)
            for f in range(H_TILES):
                act.wait_ge(lin_read, lins.next())
                act.activation(az[:, f, :], az[:, f, :], ACT.Silu).then_inc(silu_done, 1)
            steps = [(pair, t) for pair in range(H_TILES) for t in (3, 2, 1, 0)]
            for n, (pair, t) in enumerate(steps):
                sparse_exp(t, n % 2)
                if n:
                    sparse_keep(steps[n - 1][1])
                if n and t == 3:
                    take_out()
                if n > 4 and t == 2:
                    y_hi(y_attn, pair - 1)
            sparse_keep(0)
            take_out()
            y_hi(y_attn, H_TILES - 1)
            scored.n += QT * H_TILES
            act.dma_start(mem[:], ap["mem_t"].rearrange("c p n -> p c n")).then_inc(mem_loaded, 16)
            act.wait_ge(mem_loaded, 16 * (layer + 1))
            norm_in([(f"mem_norm{layer}", mem_hi)], None, None, mem, MEM)
            return

        def two_layer_rest(layer):
            to_rstd(rstd_m[:, 0:MEM], D, rstd_done, outs)
            for f in range(H_TILES):
                lins.next()
                act.wait_ge(lin_read, lins.next())
                act.activation(mz[:, f, :], mz[:, f, :], ACT.Silu).then_inc(silu_done, 1)
            lins.n += 2 * H_TILES
            for f in range(H_TILES):
                keep(mv[:, :, f * P:(f + 1) * P], MEM_CHUNKS)
            steps = [(pair, t) for pair in range(H_TILES // 2) for t in (3, 2, 1, 0)]
            for n, (pair, t) in enumerate(steps):
                mem_soft(n % 2)
                if n:
                    mem_keep(steps[n - 1][1])
                if n and t == 3:
                    for e in range(2):
                        take_out()
                        y_hi(y_mem, 2 * (pair - 1) + e)
            mem_keep(0)
            for e in range(2):
                take_out()
                y_hi(y_mem, H_TILES - 2 + e)
            scored.n += QT * H_TILES // 2
            act.dma_start(pool_w[:], ap["pool_w"][layer]).then_inc(pool_loaded, 16)
            for g in range(POOL_GROUPS):
                lins.next()
                act.wait_ge(lin_read, lins.next())
                act.activation(pool_z[:], pool_z[:], ACT.Silu).then_inc(silu_done, 1)
                act.wait_ge(lin_read, lins.next())
                act.activation(y_pool[0][:, g, :], y_now[:], ACT.Copy).then_inc(hi_done, 1)
            def merge(f, u):
                for b in range(3):
                    act.wait_ge(lin_read, lins.next())
                    act.activation(gates[:, u, b, :], gates[:, u, b, :], ACT.Sigmoid).then_inc(silu_done, 1)
                lins.n += 3
                act.wait_ge(gated, ready_sum.next())
                act.activation(sum_hi[:, bass.ds(f, 1), :], merged[:, u, :], ACT.Copy).then_inc(hi_done, 1)

            with Turns(act, KD // 2, [(lins, 12), (ready_sum, 2)]) as i:
                for u in range(2):
                    merge(2 * i + u, u)
            norm_in([(f"norm{layer + 1}", h_hi)] if layer + 1 < LAYERS else [], lin_read, lins)
            to_rstd(rstd[:], D, rstd_done, outs)

        ready_sum = Tally()
        for layer in range(LAYERS):
            two_layer(layer)
            two_layer_rest(layer)

    @block.vector
    def _(dve):
        step = Tally()
        dve.sem_inc(lin_read, 2)
        dve.sem_inc(sticks_done, 2)

        def do(ins):
            ins.then_inc(v_step, 1)
            step.next()

        def settle():
            dve.wait_ge(v_step, step.at())

        lins, reads = Tally(), Tally(2)
        exps, scored, logs, silus, his, sqs, sums, rs, subs, qks = (Tally() for _ in range(10))

        def evacuate(out, factor, source_scale=1.0, width=SEQ):
            dve.wait_ge(lin_written, lins.next())
            bank = (lins.n - 1) % 2
            dve.scalar_tensor_tensor(out, lin[:, bank, 0:width], source_scale, factor, ALU.mult,
                                     ALU.mult).then_inc(lin_read, 1)
            reads.next()

        def rope(which, out):
            dve.wait_ge(lin_written, lins.next())
            bank = (lins.n - 1) % 2
            dve.tensor_tensor(rot_sin[:], lin[:, bank, :], sin, ALU.mult).then_inc(lin_read, 1)
            reads.next()
            do(dve.tensor_tensor(out, plain[:, which, :], cos, ALU.mult))
            dve.wait_ge(lin_read, reads.at())
            settle()
            dve.tensor_tensor(out, out, rot_sin[:], ALU.add).then_inc(qk_ready, 1)

        def maxima(t):
            n = P * (t + 1)
            dve.wait_ge(score_written, scored.next())
            slot = (scored.n - 1) % 2
            dve.tensor_reduce(negmax[:, slot, :], score[:, slot, :, 0:n], AX.X, ALU.max,
                              negate=True).then_inc(negmax_done, 1)

        def combine(t):
            n = P * (t + 1)
            dve.wait_ge(exp_done, exps.next())
            slot = (exps.n - 1) % 2
            do(dve.reciprocal(rinv[:], rowsum[:, slot, :]))
            settle()
            do(dve.tensor_scalar(probs[:, t % 2, 1, 0:n], probs[:, t % 2, 1, 0:n], rinv[:, 1:2], neg_lam[:, 0:1],
                                 ALU.mult, ALU.mult))
            settle()
            dve.scalar_tensor_tensor(probs[:, t % 2, 0, 0:n], probs[:, t % 2, 0, 0:n], rinv[:, 0:1],
                                     probs[:, t % 2, 1, 0:n], ALU.mult, ALU.add).then_inc(mixed, 1)

        def a_period(parity, pair, prev=True, cur=True, nxt=True):
            other = 1 - parity
            if cur:
                maxima(3)
            if nxt:
                evacuate(plain[:, 0, :], rstd[:], 0.125)
            if cur:
                combine(3)
                maxima(2)
            if nxt:
                rope(0, q_now[:, other, :])
                evacuate(plain[:, 1, :], rstd[:])
            if cur:
                combine(2)
            if prev:
                dve.wait_ge(sub_rstd, subs.next())
                dve.tensor_tensor(o_sq[:], o_raw[:], o_rstd[:], ALU.mult).then_inc(sub_scaled, 1)
            if cur:
                maxima(1)
            if nxt:
                rope(1, k_now[:, other, :])
                evacuate(v_t[:], rstd[:])
            if cur:
                combine(1)
            if prev:
                dve.wait_ge(hi_done, his.next())
                dve.scalar_tensor_tensor(o_lo[:, bass.ds(pair - 1, 1), :], o_sq[:], sub_gain[:, 0:1],
                                         o_hi[:, bass.ds(pair - 1, 1), :].bitcast(F32), ALU.mult,
                                         ALU.subtract).then_inc(lo_done, 1)
            if cur:
                maxima(0)
                combine(0)

        def b_sticks(t):
            n = P * (t + 1)
            dve.wait_ge(logs_done, logs.next())
            z = score[:, (logs.n - 1) % 2, :, 0:n]
            sums_at = decay[:, t % 2, :, 0:n]
            do(dve.scalar_tensor_tensor(softplus[:, :, 0:n], z, 0.0, sums_at, ALU.max, ALU.add))
            settle()
            for e in range(2):
                back = softplus[:, e, 0:n][:, ::-1]
                do(dve.tensor_tensor_scan(sums_at[:, e, :][:, ::-1], back, back, 0.0, ALU.add, ALU.bypass))
            settle()
            dve.tensor_tensor(sums_at, z, sums_at, ALU.subtract).then_inc(sticks_done, 1)

        def b_period(parity, pair, prev=True, cur=True, nxt=True):
            other = 1 - parity
            if cur:
                b_sticks(3)
            if nxt:
                evacuate(q_now[:, other, :], rstd[:], 0.125)
            if cur:
                b_sticks(2)
            if nxt:
                evacuate(k_now[:, other, :], rstd[:])
            if prev:
                dve.wait_ge(hi_done, his.next())
                dve.wait_ge(out_read, outr.next())
                dve.tensor_tensor(o_lo[:, bass.ds(pair - 1, 1), :], o_raw[:],
                                  o_hi[:, bass.ds(pair - 1, 1), :].bitcast(F32), ALU.subtract).then_inc(lo_done, 1)
            if cur:
                b_sticks(1)
            if nxt:
                evacuate(v_t[:], rstd[:])
            if cur:
                b_sticks(0)

        outr = Tally()

        def add_square(first, k, width=SEQ):
            dve.wait_ge(square_done, sqs.next())
            total, new = square_sum[:, 0:width], squares[:, k, 0:width]
            if first:
                i = dve.tensor_copy(total, new)
            else:
                i = dve.tensor_tensor(total, total, new, ALU.add)
            i.then_inc(sum_added, 1)
            dve.wait_ge(sum_added, added.next())

        added = Tally(2)

        def out_tiles(m):
            def tile(f, k):
                dve.wait_ge(lin_written, lins.next())
                dve.tensor_copy(m[:, bass.ds(f, 1), :], lin[:, k, :]).then_inc(lin_read, 1)
                reads.next()

            tile(0, 0)
            tile(1, 1)
            add_square(True, 0)
            with Turns(dve, KD // 2 - 1, [(lins, 2), (reads, 2), (sqs, 2), (added, 2)]) as i:
                tile(2 * i + 2, 0)
                add_square(False, 1)
                tile(2 * i + 3, 1)
                add_square(False, 0)
            add_square(False, 1)

        def norm_in(names, m=None, post=None):
            if m is not None:
                dve.wait_ge(rstd_done, rs.next())
            for f in range(KD):
                if m is not None:
                    do(dve.scalar_tensor_tensor(m[:, f, :], m[:, f, :], gain(post, f), rstd_m[:], ALU.mult, ALU.mult))
                    settle()
                    dve.tensor_tensor(x[:, f, :], x[:, f, :], m[:, f, :], ALU.add).then_inc(x_ready, 1)
                    dve.wait_ge(x_ready, xs.next())
                if f:
                    finish(names, f - 1)
            if names:
                finish(names, KD - 1)

        xs = Tally()

        def finish(names, f, source=x, width=SEQ):
            if not names:
                return
            add_square(f == 0, f % 2, width)
            for name, hi, lo in names:
                if name is None:
                    continue
                dve.wait_ge(hi_done, his.next())
                dve.scalar_tensor_tensor(lo[:, f, :], source[:, f, :], gain(name, f), hi[:, f, :].bitcast(F32), ALU.mult,
                                         ALU.subtract).then_inc(h_ready, 1)

        def ffn():
            def one(j, u, lagging):
                evacuate(gate_s[:, u, :], rstd[:])
                if lagging:
                    low(j - 1, 1 - u)
                evacuate(up_s[:, u, :], rstd[:])
                dve.wait_ge(silu_done, silus.next())
                dve.wait_ge(lin_read, reads.at())
                dve.tensor_tensor(up_s[:, u, :], gate_s[:, u, :], up_s[:, u, :], ALU.mult).then_inc(act_ready, 1)
                dve.wait_ge(act_ready, acts.next())

            def low(j, u):
                dve.wait_ge(hi_done, his.next())
                dve.tensor_tensor(act_lo[:, bass.ds(j, 1), :], up_s[:, u, :],
                                  act_hi[:, bass.ds(j, 1), :].bitcast(F32), ALU.subtract).then_inc(lo_done, 1)

            one(0, 0, False)
            one(1, 1, True)
            with Turns(dve, FF_TILES // 2 - 1, [(lins, 4), (reads, 4), (silus, 2), (acts, 2), (his, 2)]) as i:
                for u in range(2):
                    one(2 * i + (u + 2), u, True)
            low(FF_TILES - 1, 1)

        acts = Tally()
        dve.memset(ones[:], 1.0).then_inc(const_done, 1)
        dve.memset(eps[:], EPS).then_inc(const_done, 1)
        dve.wait_ge(params_loaded, 64)
        lam = params[0:64, LAMBDA_AT:LAMBDA_AT + 4]
        dve.tensor_tensor(lam_prod[:], lam[:, 0:2], lam[:, 2:4], ALU.mult).then_inc(lam_ready, 1)
        dve.wait_ge(lam_done, 1)
        do(dve.tensor_tensor(neg_lam[:], lam_exp[:, 1:2], lam_exp[:, 0:1], ALU.subtract))
        settle()
        do(dve.tensor_scalar(neg_lam[:], neg_lam[:], -LAMBDA_INIT, None, ALU.add))
        do(dve.tensor_scalar(sub_gain[:], params[:, SUBLN_AT:SUBLN_AT + 1], 1.0 - LAMBDA_INIT, None, ALU.mult))
        dve.wait_ge(x_loaded, 16)
        norm_in([("mix_pre0", h_hi, h_lo)])
        dve.wait_ge(rstd_done, rs.next())
        a_period(1, None, False, False, True)
        exps.n = 2
        a_period(0, 0, False, True, True)
        with Turns(dve, 3, [(step, 20), (lins, 10), (reads, 10), (exps, 8), (scored, 8), (subs, 2), (his, 2)]) as i:
            a_period(1, 2 * i + 1)
            a_period(0, 2 * i + 2)
        a_period(1, 7, True, True, False)
        a_period(0, 8, True, False, False)
        out_tiles(m_attn)
        norm_in([("ffn_pre0", h_hi, h_lo)], m_attn, "mix_post0")
        dve.wait_ge(rstd_done, rs.next())
        ffn()
        out_tiles(m_ffn)
        norm_in([("mix_pre1", h_hi, h_lo), ("kv", g_hi, g_lo)], m_ffn, "ffn_post0")
        dve.wait_ge(rstd_done, rs.next())
        outr.n = 1 + 1 + 2 * A_PAIRS + 4
        b_period(1, None, False, False, True)
        b_period(0, 0, False, True, True)
        with Turns(dve, 3, [(step, 24), (lins, 6), (reads, 6), (logs, 8), (his, 2), (outr, 2)]) as i:
            b_period(1, 2 * i + 1)
            b_period(0, 2 * i + 2)
        b_period(1, 7, True, True, False)
        b_period(0, 8, True, False, False)
        out_tiles(m_attn)
        norm_in([("ffn_pre1", h_hi, h_lo)], m_attn, "mix_post1")
        dve.wait_ge(rstd_done, rs.next())
        ffn()
        out_tiles(m_ffn)
        norm_in([("norm0", h_hi, h_lo)], m_ffn, "ffn_post1")
        dve.wait_ge(rstd_done, rs.next())
        dve.sem_inc(index_done, 2)
        dve.sem_inc(biased, 2)
        scored.n = 2 * QT * A_PAIRS
        relus, ready_y = Tally(2), Tally()
        mem_exps = Tally(2)
        outr.n += 4

        def index_sum(t):
            n = P * (t + 1)
            for pair in range(IDX_PAIRS):
                dve.wait_ge(relu_done, relus.next())
                slot = (relus.n - 1) % 2
                for e in range(2):
                    head = 2 * pair + e
                    weight = iw[:, t, head:head + 1]
                    if head == 0:
                        i = dve.tensor_scalar(index[:, 0:n], relu_s[:, slot, e, 0:n], weight, None, ALU.mult)
                    else:
                        i = dve.scalar_tensor_tensor(index[:, 0:n], relu_s[:, slot, e, 0:n], weight, index[:, 0:n],
                                                     ALU.mult, ALU.add)
                    if e:
                        i.then_inc(index_done, 1)
                        dve.wait_ge(index_done, indexed.next())
                    else:
                        do(i)
                        settle()
            do(dve.memset(index[0:CHUNK, n - CHUNK:n], NEG))
            settle()

        indexed = Tally(2)

        def top_rounds(t, rounds):
            n = P * (t + 1)
            for _ in range(rounds):
                do(dve.max(top8[:], index[:, 0:n]))
                settle()
                do(dve.match_replace(index[:, 0:n], top8[:], index[:, 0:n], TAKEN))
                settle()

        def choose(t):
            n = P * (t + 1)
            do(dve.tensor_scalar(chosen[:, t, 0:n], index[:, 0:n], TAKEN / 2, NEG, ALU.is_ge, ALU.mult))
            settle()

        def sparse_front(pair, t, slot):
            n = P * (t + 1)
            biases_back = bias[:, 2 * pair:2 * pair + 2, P * t + P - n:P * t + P][:, :, ::-1]
            dve.wait_ge(score_written, scored.next())
            w = weights2[:, slot, :, 0:n]
            dve.tensor_tensor(w, score[:, slot, :, 0:n], biases_back,
                              ALU.add).then_inc(biased, 1)
            dve.wait_ge(biased, biases.next())
            do(dve.tensor_tensor(w, w, chosen[:, t:t + 1, 0:n].broadcast_to([P, 2, n]), ALU.add))
            settle()
            dve.tensor_reduce(negmax[:, slot, :], w, AX.X, ALU.max, negate=True).then_inc(negmax_done, 1)

        biases = Tally(2)

        mixes = Tally(QT * A_PAIRS)

        def normalise(n, slot):
            dve.wait_ge(mixed, mixes.at())
            do(dve.reciprocal(rinv[:], rowsum[:, slot, :]))
            settle()
            for e in range(2):
                i = dve.tensor_scalar(weights2[:, slot, e, 0:n], weights2[:, slot, e, 0:n], rinv[:, e:e + 1], None,
                                      ALU.mult)
            i.then_inc(mixed, 1)
            mixes.next()

        def sparse_back(t, slot):
            dve.wait_ge(exp_done, exps.next())
            normalise(P * (t + 1), slot)

        def y_of(factor, y, f):
            dve.wait_ge(out_read, outr.next())
            dve.wait_ge(lo_done, lows.at())
            dve.tensor_tensor(y_now[:], o_raw[:], factor, ALU.mult).then_inc(y_ready, 1)
            y_low(y, f)

        def y_low(y, f):
            dve.wait_ge(hi_done, his.next())
            dve.tensor_tensor(y[1][:, f, :], y_now[:], y[0][:, f, :].bitcast(F32), ALU.subtract).then_inc(lo_done, 1)
            lows.next()

        lows = Tally(2 * (KD + FF_TILES))

        def mem_front(slot):
            dve.wait_ge(score_written, scored.next())
            dve.tensor_reduce(negmax[:, slot, :], score[:, slot, :, 0:MEM], AX.X, ALU.max,
                              negate=True).then_inc(negmax_done, 1)

        def two_layer(layer):
            for f in range(H_TILES):
                evacuate(iq[:, f, :], rstd[:])
            evacuate(ik[:], rstd[:])
            evacuate(turn_in[:], rstd[:], IDX_SCALE)
            dve.wait_ge(turn_read, iw_turned[layer])
            for t, out, factor in ((3, aq, 0.125), (2, ak, 1.0)):
                index_sum(t)
                for f in range(H_TILES):
                    evacuate(out[:, f, :], rstd[:], factor)
                    top_rounds(t, TOPK // 8 // H_TILES)
                choose(t)
            index_sum(1)
            for f in range(H_TILES):
                evacuate(turn_in[:], rstd[:])
                top_rounds(1, TOPK // 8 // H_TILES)
            choose(1)
            do(dve.memset(chosen[:, 0, 0:P], 0.0))
            settle()
            do(dve.memset(chosen[0:CHUNK, 0, P - CHUNK:P], NEG))
            for f in range(H_TILES):
                evacuate(az[:, f, :], rstd[:])
            silus.n += H_TILES
            dve.wait_ge(silu_done, silus.at())
            dve.wait_ge(bias_loaded, 16)
            scored.n += 3 * IDX_PAIRS
            steps = [(pair, t) for pair in range(H_TILES) for t in (3, 2, 1, 0)]
            for n, (pair, t) in enumerate(steps):
                sparse_front(pair, t, n % 2)
                if n:
                    sparse_back(steps[n - 1][1], (n - 1) % 2)
                if n > 4 and t == 2:
                    y_of(az[:, pair - 1, :], y_attn, pair - 1)
            sparse_back(0, 1)
            y_of(az[:, H_TILES - 1, :], y_attn, H_TILES - 1)
            dve.wait_ge(mem_loaded, 16 * (layer + 1))
            for f in range(KD):
                finish([(f"mem_norm{layer}", mem_hi, mem_lo)], f, mem, MEM)
            for f in range(H_TILES):
                evacuate(mq[:, f, :], rstd[:], MEM_SCALE)
                evacuate(mz[:, f, :], rstd[:])
            dve.wait_ge(rstd_done, rs.next())
            outr.n += 1
            for f in range(H_TILES):
                evacuate(mk[:, f, :], rstd_m[:, 0:MEM], 1.0, MEM)
            for f in range(H_TILES):
                evacuate(weights2[:, 0, 0, 0:MEM], rstd_m[:, 0:MEM], 1.0, MEM)
            silus.n += H_TILES
            dve.wait_ge(silu_done, silus.at())
            steps = [(pair, t) for pair in range(H_TILES // 2) for t in (3, 2, 1, 0)]
            for n, (pair, t) in enumerate(steps):
                mem_front(n % 2)
                if n:
                    dve.wait_ge(mem_exp, mem_exps.next())
                    normalise(MEM, (n - 1) % 2)
                if n and t == 3:
                    for e in range(2):
                        y_of(mz[:, 2 * (pair - 1) + e, :], y_mem, 2 * (pair - 1) + e)
            dve.wait_ge(mem_exp, mem_exps.next())
            normalise(MEM, 1)
            for e in range(2):
                y_of(mz[:, H_TILES - 2 + e, :], y_mem, H_TILES - 2 + e)
            for t in (pool_u, pool_a, pool_b):
                do(dve.memset(t[:, 0:POOL_EDGE], 0.0))
            settle()
            body = slice(POOL_EDGE, POOL_EDGE + SEQ)
            for g in range(POOL_GROUPS):
                evacuate(pool_u[:, body], rstd[:])
                dve.wait_ge(lin_read, reads.at())
                source = pool_u
                for level in range(g + 1):
                    out = pool_b if source is pool_a else pool_a
                    back = slice(POOL_EDGE - 2 ** level, POOL_EDGE + SEQ - 2 ** level)
                    do(dve.tensor_tensor(out[:, body], source[:, body], source[:, back], ALU.add))
                    settle()
                    source = out
                inverse = tables[:, COUNT_AT + POOL_EDGE * g:COUNT_AT + POOL_EDGE * (g + 1)]
                do(dve.tensor_tensor(edge[:], source[:, POOL_EDGE:2 * POOL_EDGE], inverse, ALU.mult))
                do(dve.scalar_tensor_tensor(pooled[:], source[:, body], 0.5 ** (g + 1), pool_u[:, body], ALU.mult,
                                            ALU.subtract))
                settle()
                dve.tensor_tensor(pooled[:, 0:POOL_EDGE], edge[:], pool_u[:, POOL_EDGE:2 * POOL_EDGE],
                                  ALU.subtract).then_inc(pool_ready, 1)
                evacuate(pool_z[:], rstd[:])
                dve.wait_ge(silu_done, silus.next())
                dve.wait_ge(lin_written, lins.next())
                dve.wait_ge(lo_done, lows.at())
                scale_at = POOL_SCALE_AT + POOL_GROUPS * layer + g
                dve.scalar_tensor_tensor(y_now[:], lin[:, (lins.n - 1) % 2, :], params[:, scale_at:scale_at + 1],
                                         pool_z[:], ALU.mult, ALU.mult).then_inc(lin_read, 1)
                reads.next()
                y_low(y_pool, g)

            def merge(f, u):
                for b in range(3):
                    evacuate(gates[:, u, b, :], rstd[:])
                for b in range(3):
                    dve.wait_ge(silu_done, silus.next())
                    dve.wait_ge(lin_written, lins.next())
                    out = merged[:, u, :] if b == 0 else part[:]
                    dve.tensor_tensor(out, lin[:, (lins.n - 1) % 2, :], gates[:, u, b, :], ALU.mult).then_inc(
                        lin_read, 1)
                    dve.wait_ge(lin_read, reads.next())
                    if b:
                        i = dve.tensor_tensor(merged[:, u, :], merged[:, u, :], part[:], ALU.add)
                        if b == 1:
                            do(i)
                            settle()
                        else:
                            i.then_inc(gated, 1)
                            dve.wait_ge(gated, gate_n.next())
                dve.wait_ge(hi_done, his.next())
                dve.tensor_tensor(sum_lo[:, bass.ds(f, 1), :], merged[:, u, :],
                                  sum_hi[:, bass.ds(f, 1), :].bitcast(F32), ALU.subtract).then_inc(lo_done, 1)
                lows.next()

            with Turns(dve, KD // 2, [(lins, 12), (reads, 12), (silus, 6), (gate_n, 2), (his, 2), (step, 2),
                                             (lows, 2)]) as i:
                for u in range(2):
                    merge(2 * i + u, u)
            names = [(f"norm{layer + 1}", h_hi, h_lo)] if layer + 1 < LAYERS else [(None, None, None)]
            for f in range(KD):
                dve.wait_ge(lin_written, lins.next())
                dve.tensor_tensor(x[:, f, :], x[:, f, :], lin[:, (lins.n - 1) % 2, :], ALU.add).then_inc(lin_read, 1)
                dve.wait_ge(lin_read, reads.next())
                if f:
                    finish(names, f - 1)
            finish(names, KD - 1)
            dve.wait_ge(rstd_done, rs.next())
            outr.n += 1

        gate_n = Tally()
        turns_at = 1 + 5 * A_PAIRS + 9 * A_PAIRS
        per_layer = 1 + H_TILES + 2 * QT * H_TILES + H_TILES + QT * H_TILES // 2
        iw_turned = [turns_at + 1 + per_layer * layer for layer in range(LAYERS)]
        for layer in range(LAYERS):
            two_layer(layer)
        for f in range(KD):
            dve.scalar_tensor_tensor(result[:, f, :], x[:, f, :], gain("final", f), rstd[:], ALU.mult,
                                     ALU.mult).then_inc(x_ready, 1)

    block.__exit__(None, None, None)


def layout(inputs):
    def tiles(w):
        k, n = w.shape
        return w.reshape(k // P, P, n // P, P).transpose(2, 0, 1, 3)

    def blocks(t):
        f, c = t.shape[:2]
        full = -(-c // BLOCK_TILES) * BLOCK_TILES
        if full != c:
            t = np.concatenate([t, np.zeros((f, full - c, P, P), t.dtype)], axis=1)
        return t.reshape(f * full // BLOCK_TILES, BLOCK_TILES, P, P).transpose(0, 2, 1, 3).reshape(-1, P, BLOCK_TILES * P)

    def woven(*parts):
        return np.stack(parts, axis=1).reshape(-1, *parts[0].shape[1:])

    def ffn(layer):
        both = tiles(inputs["ffn_w_gate_up"][layer])
        return [blocks(woven(both[:FF_TILES], both[FF_TILES:])), blocks(tiles(inputs["ffn_w_down"][layer]))]

    qkv = tiles(inputs["a_w_qkv"][0])
    kv = tiles(inputs["kv_w"])
    stream = [blocks(woven(qkv[0:8], qkv[8:16], qkv[16:24])), blocks(tiles(inputs["a_w_o"][0]))] + ffn(0)
    stream += [blocks(woven(tiles(inputs["b_w_q"][0]), kv[0:8], kv[8:16])), blocks(tiles(inputs["b_w_o"][0]))] + ffn(1)
    edges = np.cumsum([512, 512, 512, 512, 512, 512, 512, 64, 8, 512, 512])
    for n in range(LAYERS):
        pool_u, pool_z, q, k, v, z, iq, ik, iw, mq, mz, gates = np.split(inputs["w_in_2"][n], edges, axis=1)
        iw = np.concatenate([iw, np.zeros((D, P - iw.shape[1]), iw.dtype)], axis=1)
        single = [iq, np.concatenate([ik, ik], axis=1), iw, q, k, v, z]
        stream += [blocks(tiles(w)) for w in single]
        stream += [blocks(woven(tiles(mq), tiles(mz))), blocks(tiles(inputs["w_mem_kv_2"][n]))]
        stream += [blocks(woven(tiles(pool_u), tiles(pool_z)))]
        gate_blocks = blocks(tiles(gates)).reshape(3, KD, P, -1)
        branch = np.concatenate([tiles(inputs["w_branch_2"][n, b]) for b in range(3)], axis=1)
        branch_blocks = blocks(branch).reshape(KD, 2, P, -1)
        stream += [np.concatenate([gate_blocks.transpose(1, 0, 2, 3), branch_blocks], axis=1).reshape(5 * KD, P, -1)]
        stream += [blocks(tiles(inputs["w_out_2"][n]))]
    weights = np.concatenate(stream)
    gains = {"kv": inputs["kv_norm_g"], "final": inputs["final_g_2"]}
    for n in range(2):
        gains |= {f"{k}{n}": inputs[f"{k}_g"][n] for k in ("mix_pre", "mix_post", "ffn_pre", "ffn_post")}
        gains |= {f"norm{n}": inputs["norm_g_2"][n], f"mem_norm{n}": inputs["mem_norm_g_2"][n]}
    params = np.zeros((P, N_PARAMS), np.float32)
    for name, at in GAIN_AT.items():
        params[:, at:at + KD] = gains[name].reshape(KD, P).T
    for n in range(2):
        params[:, POOL_SCALE_AT + 4 * n:POOL_SCALE_AT + 4 * n + 4] = inputs["pool_scale_2"][n].reshape(4, P).T
    params[:, SUBLN_AT] = inputs["a_subln_g"][0]
    for n, name in enumerate(("a_lambda_q1", "a_lambda_q2", "a_lambda_k1", "a_lambda_k2")):
        params[:64, LAMBDA_AT + n] = inputs[name][0]
    x_t = inputs["x"][0].T.reshape(KD, P, SEQ)
    rel = np.concatenate([inputs["rel_bias_2"], rel_onehot()], axis=1)
    mem_t = inputs["mem_2"][0].T.reshape(KD, P, MEM)
    pool_w = inputs["pool_w_2"].transpose(0, 2, 1, 3)
    return {"x_t": x_t, "weights": weights, "params": params, "rel": rel, "mem_t": mem_t,
            "pool_w": pool_w} | shape_tables()


def rel_onehot():
    d = P - 1 - np.arange(REL_SPAN)
    n = np.abs(d)
    far = 8 + (np.log(np.maximum(n, 1).astype(np.float32) / np.float32(8)) / np.float32(math.log(1024 / 8))
               * np.float32(8)).astype(np.int32)
    bucket = np.where(d > 0, 16, 0) + np.where(n < 8, n, np.minimum(far, 15))
    return (bucket[None, :] == np.arange(32)[:, None]).astype(np.float32)


def shape_tables():
    t = np.zeros((P, N_TABLES), np.float32)
    t[:, IDENT_AT:IDENT_AT + P] = np.eye(P)
    for head in range(2):
        for d in range(8):
            t[64 * head + d + 8, ROT_AT + 64 * head + d] = -1
            t[64 * head + d, ROT_AT + 64 * head + d + 8] = 1
    q, k = np.arange(P)[:, None], np.arange(P)[None, :]
    t[:, CAUSAL_AT:CAUSAL_AT + P] = np.where(k <= q, 0, NEG)
    t[:, STRICT_AT:STRICT_AT + P] = np.where(k < q, 0, NEG)
    for g in range(POOL_GROUPS):
        at = COUNT_AT + POOL_EDGE * g
        t[:, at:at + POOL_EDGE] = 1 / np.minimum(np.arange(POOL_EDGE) + 1, 2 ** (g + 1))
    freq = np.float32(500000.0) ** (-np.arange(0, 16, 2, dtype=np.float32) / np.float32(16))
    angle = np.arange(SEQ, dtype=np.float32)[:, None] * freq[None, :]
    rope = np.zeros((P, 2, SEQ), np.float32)
    rope[:, 0] = 1
    for start in (0, 8, 64, 72):
        rope[start:start + 8, 0] = np.cos(angle).T
        rope[start:start + 8, 1] = np.sin(angle).T
    return {"tables": t, "rope": rope}


def kernel(**inputs):
    from concourse import bacc
    from concourse.bass_utils import run_bass_kernel_spmd

    arrays = {name: np.ascontiguousarray(a) for name, a in layout({k: np.asarray(v) for k, v in inputs.items()}).items()}
    nc = bacc.Bacc("TRN2", target_bir_lowering=False, num_devices=1)
    ap = {name: nc.dram_tensor(name, a.shape, mybir.dt.from_np(a.dtype), kind="ExternalInput").ap()
          for name, a in arrays.items()}
    ap["out_t"] = nc.dram_tensor("out_t", (KD, P, SEQ), F32, kind="ExternalOutput").ap()
    build(nc, ap)
    result = run_bass_kernel_spmd(nc, [arrays], core_ids=[0])
    return result.results[0]["out_t"].reshape(D, SEQ).T[None]
```

```python
import math

import numpy as np

import concourse.bass as bass
from concourse import mybir
from concourse.alu_op_type import AluOpType as ALU

F32 = mybir.dt.float32
F32R = mybir.dt.float32r
ACT = mybir.ActivationFunctionType
AX = mybir.AxisListType

P = 128
SEQ = 512
D = 1024
KD = D // P
QT = SEQ // P
D_FF = 2816
FF_TILES = D_FF // P
A_PAIRS = 8
NEG = -1e30
EPS = 1e-6
LAMBDA_INIT = 0.8 - 0.6 * math.exp(-0.3 * 0)
BLOCK_TILES = 8
DOWN_SHARES = (7, 7, 8)
MERGE_SHARES = (7, 7, 7, 7, 8)
RAW_SLOTS = 4
W_SLOTS = 2

GAINS = ["mix_pre0", "mix_post0", "ffn_pre0", "ffn_post0", "kv", "mix_pre1", "mix_post1", "ffn_pre1", "ffn_post1",
         "norm0", "norm1", "mem_norm0", "mem_norm1", "final"]
GAIN_AT = {name: KD * n for n, name in enumerate(GAINS)}
POOL_SCALE_AT = KD * len(GAINS)
SUBLN_AT = POOL_SCALE_AT + 2 * 4
LAMBDA_AT = SUBLN_AT + 1
N_PARAMS = LAMBDA_AT + 4

IDENT_AT, ROT_AT, CAUSAL_AT, STRICT_AT = 0, P, 2 * P, 3 * P
N_TABLES = 4 * P
MASKED = -2.0 ** 100
POOL_EDGE = 16
POOL_GROUPS = 4

LAYERS = 2
H_TILES = 4
IDX_PAIRS = 4
TOPK = 128
CHUNK = 64
MEM = 256
MEM_CHUNKS = MEM // P
TAKEN = -3e38
IDX_SCALE = 64 ** -0.5 * 8 ** -0.5
MEM_SCALE = 128 ** -0.5
MEM_ORDER = [("z", 0), ("z", 1), ("k", 0), ("z", 2), ("k", 1), ("z", 3), ("k", 2), ("k", 3)] + [
    ("v", f) for f in range(4)]
REL_SPAN = SEQ + P
N_REL_HEADS = 8


class Tally:

    def __init__(self, n=0):
        self.n, self.turn, self.per = n, None, 0

    def at(self, ahead=0):
        if self.turn is None:
            return self.n + ahead
        return self.turn * self.per + (self.n + ahead)

    def next(self):
        self.n += 1
        return self.at()


class Turns:

    def __init__(self, eng, n, grow):
        self.eng, self.n, self.grow = eng, n, grow

    def __enter__(self):
        self.loop = self.eng.Fori(0, self.n)
        i = self.loop.__enter__()
        self.start = [(t, t.n) for t, _ in self.grow]
        for t, per in self.grow:
            t.turn, t.per = i, per
        return i

    def __exit__(self, *error):
        self.loop.__exit__(*error)
        if error[0] is None:
            grown = [t.n - n for t, n in self.start]
            assert grown == [per for _, per in self.grow], (grown, [per for _, per in self.grow])
            for (t, n), (_, per) in zip(self.start, self.grow):
                t.n, t.turn = n + per * self.n, None


def build(nc, ap):
    w_stream, n_blocks = ap["weights"], ap["weights"].shape[0]
    place = {"at": 16512}

    def region(start):
        place["at"] = start

    def sb(name, shape, dt=F32):
        size = 4 * int(np.prod(shape[1:]))
        t = nc.alloc_sbuf_tensor_at(name, shape, dt, offset=place["at"])
        place["at"] += size + (-size) % 32
        return t

    x = sb("x", [P, KD, SEQ])
    h_hi, h_lo = sb("h_hi", [P, KD, SEQ], F32R), sb("h_lo", [P, KD, SEQ], F32R)
    raw = sb("raw", [P, RAW_SLOTS, BLOCK_TILES * P])
    w_hi, w_lo = (sb(n, [P, W_SLOTS, BLOCK_TILES, P], F32R) for n in ("w_hi", "w_lo"))
    params = sb("params", [P, N_PARAMS])
    tables = sb("tables", [P, N_TABLES], F32R)
    inverse_counts = sb("inverse_counts", [P, POOL_GROUPS, POOL_EDGE])
    ones = sb("ones", [P, P])
    eps = sb("eps", [P, 1])
    rstd, rstd_m = sb("rstd", [P, SEQ]), sb("rstd_m", [P, SEQ])
    negmax, rowsum, rinv = sb("negmax", [P, 2, 2]), sb("rowsum", [P, 2, 2]), sb("rinv", [P, 2])
    lam_prod, lam_exp, neg_lam = sb("lam_prod", [64, 2]), sb("lam_exp", [P, 2]), sb("neg_lam", [P, 1])
    sub_gain = sb("sub_gain", [P, 1])
    ident_r, causal_r, strict_r = (tables[:, at:at + P] for at in (IDENT_AT, CAUSAL_AT, STRICT_AT))
    squares = sb("squares", [P, 2, SEQ])
    sum_at = place["at"]
    square_sum = sb("square_sum", [P, SEQ])
    region(sum_at)
    o_raw = sb("o_raw", [P, SEQ])
    stage_at = place["at"]

    plain, rot_sin = sb("plain", [P, 2, SEQ]), sb("rot_sin", [P, SEQ])
    o_sq, o_rstd = sb("o_sq", [P, SEQ]), sb("o_rstd", [P, SEQ])
    rope = sb("rope", [P, 2, SEQ])
    rel = sb("rel", [32, N_REL_HEADS + REL_SPAN])
    rel_rows = sb("rel_rows", [N_REL_HEADS, REL_SPAN])
    region(stage_at)
    g_hi, g_lo = sb("g_hi", [P, KD, SEQ], F32R), sb("g_lo", [P, KD, SEQ], F32R)
    q_now, k_now = sb("q_now", [P, 2, SEQ]), sb("k_now", [P, 2, SEQ])
    v_t = sb("v_t", [P, SEQ])
    v_now = sb("v_now", [P, 2, QT, P])
    probs = sb("probs", [P, 2, 2, SEQ])
    a_t = sb("a_t", [P, 2, QT, SEQ])
    decay = [sb(f"decay{t}", [P, 2, P * (t + 1)]) for t in range(QT)]
    softplus = squares
    o_hi, o_lo = sb("o_hi", [P, KD, SEQ], F32R), sb("o_lo", [P, KD, SEQ], F32R)
    end_a = place["at"]
    region(stage_at)
    m_attn = sb("m_attn", [P, KD, SEQ])
    region(stage_at)
    act_hi, act_lo = sb("act_hi", [P, FF_TILES, SEQ], F32R), sb("act_lo", [P, FF_TILES, SEQ], F32R)
    m_ffn = sb("m_ffn", [P, KD, SEQ])
    gate_s, up_s = sb("gate_s", [P, 2, SEQ]), sb("up_s", [P, 2, SEQ])
    region(stage_at)
    bias = sb("bias", [P, N_REL_HEADS, SEQ])
    y_attn = sb("y_attn_hi", [P, H_TILES, SEQ], F32R), sb("y_attn_lo", [P, H_TILES, SEQ], F32R)
    work_at = place["at"]
    aq, ak = sb("aq", [P, H_TILES, SEQ]), sb("ak", [P, H_TILES, SEQ])
    av = sb("av", [P, QT, H_TILES * P])
    iq, ik = sb("iq", [P, H_TILES, SEQ]), sb("ik", [P, SEQ])
    turn_in = sb("turn_in", [P, SEQ])
    chosen = sb("chosen", [P, QT, SEQ])
    az = sb("az", [P, H_TILES, SEQ])
    iw = sb("iw", [P, QT, 8])
    sparse_w = [None] * QT
    sparse_w[1] = sb("sparse_w1", [P, 2, 2 * P])
    assert place["at"] <= work_at + 56 * 1024
    region(work_at + 56 * 1024)
    for t in (3, 2, 0):
        sparse_w[t] = sb(f"sparse_w{t}", [P, 2, P * (t + 1)])
    a2_at = place["at"]
    a2_t = sb("a2_t", [P, 2, QT, SEQ])
    y_now = sb("y_now", [P, SEQ])
    top8 = sb("top8", [P, 8])
    end_d = place["at"]
    region(a2_at)
    relu_s, index = sb("relu_s", [P, 2, 2, SEQ]), sb("index", [P, SEQ])
    region(work_at)
    y_mem = sb("y_mem_hi", [P, H_TILES, SEQ], F32R), sb("y_mem_lo", [P, H_TILES, SEQ], F32R)
    mem_hi = sb("mem_hi", [P, KD, MEM], F32R)
    mq = sb("mq", [P, H_TILES, SEQ])
    mem_lo = sb("mem_lo", [P, KD, MEM], F32R)
    mem = sb("mem", [P, KD, MEM])
    mk, mv = sb("mk", [P, H_TILES, MEM]), sb("mv", [P, MEM_CHUNKS, H_TILES * P])
    assert place["at"] <= work_at + 56 * 1024
    region(work_at + 56 * 1024)
    mem_w = sb("mem_w", [P, QT, 2, MEM])
    mem_v_t = mem_w[:, 0, 0, :]
    mem_a = sb("mem_a", [P, 2, MEM_CHUNKS, SEQ])
    mz = sb("mz", [P, H_TILES, SEQ])
    region(work_at + 16384)
    y_pool = sb("y_pool_hi", [P, H_TILES, SEQ], F32R), sb("y_pool_lo", [P, H_TILES, SEQ], F32R)
    pool_w = sb("pool_w", [P, POOL_GROUPS, P])
    pool_u, pool_a, pool_b = (sb(n, [P, POOL_EDGE + SEQ]) for n in ("pool_u", "pool_a", "pool_b"))
    pooled, pool_z = sb("pooled", [P, SEQ]), sb("pool_z", [P, SEQ])
    edge = sb("edge", [P, POOL_EDGE])
    region(work_at + 32768)
    sum_hi, sum_lo = sb("sum_hi", [P, KD, SEQ], F32R), sb("sum_lo", [P, KD, SEQ], F32R)
    gates, merged = sb("gates", [P, 2, 3, SEQ]), sb("merged", [P, 2, SEQ])
    part = sb("part", [P, SEQ])
    end_m = place["at"]
    assert max(end_d, end_m) <= nc.sbuf_usable_end, (end_d, end_m)
    region(work_at)
    result = sb("result", [P, KD, SEQ])

    lin = nc.alloc_psum_tensor("lin", [P, 2, SEQ], F32)
    score = nc.alloc_psum_tensor("score", [P, 2, 2, SEQ], F32)
    turn = nc.alloc_psum_tensor("turn", [P, SEQ], F32)
    outp = nc.alloc_psum_tensor("outp", [P, SEQ], F32)

    SPARE = [score[:, slot, e, :] for slot in range(2) for e in range(2)]

    ident = ident_r.bitcast(F32)
    rot = tables[:, ROT_AT:ROT_AT + P].bitcast(F32)
    cos, sin = rope[:, 0, :], rope[:, 1, :]

    def gain(name, f):
        return params[:, GAIN_AT[name] + f:GAIN_AT[name] + f + 1]

    def sem(name):
        return nc.alloc_semaphore(name)

    raw_loaded = [sem(f"raw_loaded{i}") for i in range(RAW_SLOTS)]
    x_loaded, params_loaded, out_stored = sem("x_loaded"), sem("params_loaded"), sem("out_stored")
    hi_split, w_split, hi_used, lo_used = sem("hi_split"), sem("w_split"), sem("hi_used"), sem("lo_used")
    lin_written, lin_read = sem("lin_written"), sem("lin_read")
    score_copied = sem("score_copied")
    score_written, exp_done, mixed = sem("score_written"), sem("exp_done"), sem("mixed")
    negmax_done, qk_ready = sem("negmax_done"), sem("qk_ready")
    turn_written, turn_read = sem("turn_written"), sem("turn_read")
    out_written, out_read = sem("out_written"), sem("out_read")
    logs_done, sticks_done, weights_done = sem("logs_done"), sem("sticks_done"), sem("weights_done")
    sub_rstd, sub_scaled, hi_done, lo_done = sem("sub_rstd"), sem("sub_scaled"), sem("hi_done"), sem("lo_done")
    silu_done, act_ready = sem("silu_done"), sem("act_ready")
    square_done = sem("square_done")
    stat_written, rstd_done = sem("stat_written"), sem("rstd_done")
    x_ready, h_ready = sem("x_ready"), sem("h_ready")
    const_done, sum_added = sem("const_done"), sem("sum_added")
    rel_written, rel_copied, rel_stored, bias_loaded = (
        sem(n) for n in ("rel_written", "rel_copied", "rel_stored", "bias_loaded"))
    relu_done, index_done, biased = sem("relu_done"), sem("index_done"), sem("biased")
    y_ready, mem_loaded, mem_exp, pool_ready = sem("y_ready"), sem("mem_loaded"), sem("mem_exp"), sem("pool_ready")
    gated, pool_loaded = sem("gated"), sem("pool_loaded")
    lam_ready, lam_summed, lam_done = sem("lam_ready"), sem("lam_summed"), sem("lam_done")
    v_step, a_step = sem("v_step"), sem("a_step")

    rel_tensor = nc.dram_tensor("rel_rows_dram", [N_REL_HEADS, REL_SPAN], F32)
    rel_dram = rel_tensor.ap()
    toeplitz = bass.AP(tensor=rel_dram.tensor, offset=0, ap=[[1, P], [REL_SPAN, N_REL_HEADS], [1, SEQ]])

    block = nc.Block()
    block.__enter__()

    @block.sync
    def _(sp):
        sp.dma_start(x[:], ap["x_t"].rearrange("c p n -> p c n")).then_inc(x_loaded, 16)
        sp.dma_start(params[:], ap["params"]).then_inc(params_loaded, 16)
        sp.dma_start(a_t[:, 0, 0, :], ap["tables"]).then_inc(params_loaded, 16)
        sp.dma_start(inverse_counts[:], ap["inverse_counts"]).then_inc(params_loaded, 16)
        sp.dma_start(rope[:], ap["rope"]).then_inc(params_loaded, 16)
        sp.dma_start(rel[:], ap["rel"]).then_inc(params_loaded, 16)

        def load(b, slot, count):
            sp.dma_start(raw[:, slot, :], w_stream[bass.ds(b, 1)].rearrange("a p n -> (a p) n")).then_inc(
                raw_loaded[slot], 16)

        for b in range(RAW_SLOTS):
            load(b, b, 16)
        with sp.Fori(1, n_blocks // RAW_SLOTS) as i:
            for slot in range(RAW_SLOTS):
                sp.wait_ge(w_split, RAW_SLOTS * i + (slot - RAW_SLOTS + 1))
                load(RAW_SLOTS * i + slot, slot, 16)
        for f in range(KD):
            sp.wait_ge(x_ready, KD * 4 + f + 1)
            sp.dma_start(ap["out_t"][f], result[:, f, :]).then_inc(out_stored, 16)
        sp.wait_ge(out_stored, 16 * KD)

    @block.gpsimd
    def _(pool):
        one = ones[:, 0:1].broadcast_to([P, BLOCK_TILES * P])
        pool.wait_ge(const_done, 1)
        with pool.Fori(0, n_blocks // RAW_SLOTS) as i:
            for slot in range(RAW_SLOTS):
                pool.wait_ge(raw_loaded[slot], 16 * i + 16)
                pool.wait_ge(hi_used, RAW_SLOTS * i + (slot + 1))
                hi = w_hi[:, slot % W_SLOTS].rearrange("p c n -> p (c n)")
                lo = w_lo[:, slot % W_SLOTS].rearrange("p c n -> p (c n)")
                pool.tensor_tensor(hi, raw[:, slot, :], one, ALU.mult).then_inc(hi_split, 1)
                pool.wait_ge(hi_split, RAW_SLOTS * i + (slot + 1))
                pool.wait_ge(lo_used, RAW_SLOTS * i + (slot + 1))
                pool.tensor_tensor(lo, raw[:, slot, :], hi.bitcast(F32), ALU.subtract).then_inc(w_split, 1)


    @block.tensor
    def _(pe):
        blocks, tiles = Tally(), Tally()
        lin_freed = Tally(0)
        scores_free, probs_in, turns_done, outs = Tally(), Tally(), Tally(), Tally()
        h_seen = {"n": 0}
        stats = Tally()
        pe.sem_inc(hi_used, W_SLOTS)
        pe.sem_inc(lo_used, W_SLOTS - 1)
        pe.wait_ge(params_loaded, 80)
        pe.wait_ge(const_done, 3)

        def passes(out, slot, tile, hi, lo, first, last, block_first, block_last):
            mm = pe.matmul(out, w_hi[:, slot, tile, :], hi, start=first, stop=False)
            if block_first:
                mm.then_inc(lo_used, 1)
            mm = pe.matmul(out, w_hi[:, slot, tile, :], lo, start=False, stop=False)
            if block_last:
                mm.then_inc(hi_used, 1)
            return pe.matmul(out, w_lo[:, slot, tile, :], hi, start=False, stop=last)

        stream = {"taken": BLOCK_TILES, "of": BLOCK_TILES, "shares": (BLOCK_TILES,), "turn": 0}

        def shares(pattern):
            assert stream["taken"] == stream["of"]
            stream["shares"], stream["turn"] = pattern, 0

        def next_tile():
            first = stream["taken"] == stream["of"]
            if first:
                stream["of"] = stream["shares"][stream["turn"] % len(stream["shares"])]
                stream["turn"] += 1
                stream["taken"] = 0
                pe.wait_ge(w_split, blocks.next())
            stream["taken"] += 1
            return (blocks.n - 1) % W_SLOTS, stream["taken"] - 1, first, stream["taken"] == stream["of"]

        def linear(hi, lo, chunks, ready=None, width=SEQ, piece=None, spare=None, late=0):
            first, end = piece or (0, chunks)
            if first == 0 and spare is None:
                pe.wait_ge(lin_read, tiles.at(1 - late))
            out = lin[:, tiles.n % 2, 0:width] if spare is None else spare
            for c in range(first, end):
                slot, tile, *edges = next_tile()
                if ready is not None:
                    pe.wait_ge(h_ready, h_base["n"] + ready * (c + 1))
                mm = passes(out, slot, tile, hi[:, c, :], lo[:, c, :], c == 0, c == chunks - 1,
                            *edges)
            if end == chunks:
                mm.then_inc(lin_written, 1)
                tiles.next()

        def rotate(which):
            pe.wait_ge(lin_read, tiles.at(2))
            bank = tiles.n % 2
            pe.matmul(lin[:, bank, :], rot, plain[:, which, :], start=True, stop=True).then_inc(lin_written, 1)
            tiles.next()

        def turn_v(parity):
            pe.wait_ge(lin_read, tiles.at(2))
            pe.wait_ge(turn_read, turns_done.at(1))
            for t in range(QT):
                mm = pe.transpose(turn[:, t * P:(t + 1) * P], v_t[:, t * P:(t + 1) * P], ident)
            mm.then_inc(turn_written, 1)
            turns_done.next()

        def scores(parity, t, free, mask):
            n = P * (t + 1)
            pe.wait_ge(free, scores_free.at(1))
            for e in range(2):
                half = slice(64 * e, 64 * e + 64)
                out = score[:, scores_free.n % 2, e, 0:n]
                pe.matmul(out, q_now[half, parity, t * P:(t + 1) * P], k_now[half, parity, 0:n], start=True,
                          stop=True)
                mm = pe.matmul(out[:, n - P:n], ident_r, mask, start=False, stop=True,
                               skip_group_check=True)
            mm.then_inc(score_written, 1)
            scores_free.next()

        def turn_probs(t, e, ready):
            pe.wait_ge(ready, probs_in.at(1))
            pe.wait_ge(turn_read, turns_done.at(1))
            for c in range(t + 1):
                mm = pe.transpose(turn[:, c * P:(c + 1) * P], probs[:, t % 2, e, c * P:(c + 1) * P], ident)
            mm.then_inc(turn_written, 1)
            turns_done.next()

        def stat(source, ready, count):
            pe.wait_ge(ready, count)
            pe.wait_ge(out_read, outs.at(1))
            pe.matmul(outp[:], ones[:], source, start=True, stop=True).then_inc(out_written, 1)
            outs.next()

        qk = Tally()

        def a_period(parity, prev=True, cur=True, nxt=True):
            other = 1 - parity
            if cur:
                qk.n += 2
                pe.wait_ge(qk_ready, qk.at())
                scores(parity, 3, exp_done, causal_r)
            if prev:
                turn_probs(0, 0, mixed)
                probs_in.next()
            if nxt:
                linear(h_hi, h_lo, KD)
            if prev:
                a_values(other)
            if cur:
                scores(parity, 2, exp_done, causal_r)
                turn_probs(3, 0, mixed)
                probs_in.next()
            if nxt:
                rotate(0)
                linear(h_hi, h_lo, KD)
            if prev:
                pe.wait_ge(out_read, outs.at(1))
                pe.matmul(outp[:], ones[:], o_sq[:], start=True, stop=True).then_inc(out_written, 1)
                outs.next()
            if cur:
                scores(parity, 1, exp_done, causal_r)
                turn_probs(2, 0, mixed)
                probs_in.next()
            if nxt:
                rotate(1)
                linear(h_hi, h_lo, KD)
            if cur:
                scores(parity, 0, exp_done, causal_r)
                turn_probs(1, 0, mixed)
                probs_in.next()
            if nxt:
                turn_v(other)

        def a_values(parity):
            pe.wait_ge(turn_read, turns_done.at(1))
            pe.wait_ge(out_read, outs.at(1))
            for c in range(QT):
                mm = pe.matmul(outp[:, c * P:SEQ], v_now[:, parity, c, :], a_t[:, 0, c, c * P:SEQ], start=(c == 0),
                               stop=(c == QT - 1), skip_group_check=True)
            mm.then_inc(out_written, 1)
            outs.next()

        def b_values(parity):
            pe.wait_ge(turn_read, turns_done.at(1))
            pe.wait_ge(out_read, outs.at(1))
            for e in range(2):
                half = slice(64 * e, 64 * e + 64)
                for c in range(QT):
                    mm = pe.matmul(outp[half, c * P:SEQ], v_now[:, parity, c, half], a_t[:, e, c, c * P:SEQ],
                                   start=(c == 0), stop=(c == QT - 1), skip_group_check=True)
            mm.then_inc(out_written, 1)
            outs.next()

        def turn_sticks(t, e=None):
            pe.wait_ge(turn_read, turns_done.at(1))
            heads = (0, 1) if e is None else (e,)
            for n, head in enumerate(heads):
                for c in range(t + 1):
                    at = (n * (t + 1) + c) * P
                    mm = pe.transpose(turn[:, at:at + P], decay[t][:, head, c * P:(c + 1) * P], ident)
            mm.then_inc(turn_written, 1)
            turns_done.next()

        def b_period(parity, prev=True, cur=True, nxt=True):
            other = 1 - parity
            if cur:
                pe.wait_ge(lin_read, tiles.at(1))
                scores(parity, 3, score_copied, strict_r)
            if prev:
                pe.wait_ge(weights_done, probs_in.next())
                turn_sticks(1)
            if nxt:
                linear(h_hi, h_lo, KD, piece=(0, 4))
            if cur:
                turn_v(parity)
            if nxt and cur:
                linear(h_hi, h_lo, KD, piece=(4, 8))

            if cur:
                scores(parity, 2, score_copied, strict_r)
            if prev:
                pe.wait_ge(weights_done, probs_in.next())
                turn_sticks(0)
            if nxt:
                linear(g_hi, g_lo, KD)

            if cur:
                scores(parity, 1, score_copied, strict_r)
            if nxt:
                linear(g_hi, g_lo, KD, piece=(0, 3))
            if prev:
                b_values(other)
            if cur:
                pe.wait_ge(weights_done, probs_in.next())
                turn_sticks(3, 0)
            if nxt:
                linear(g_hi, g_lo, KD, piece=(3, 5))
            if cur:
                turn_sticks(3, 1)

            if cur:
                scores(parity, 0, score_copied, strict_r)
                pe.wait_ge(weights_done, probs_in.next())
                turn_sticks(2, 0)
            if nxt:
                linear(g_hi, g_lo, KD, piece=(5, 8))
            if cur:
                turn_sticks(2, 1)

        h_base, sums = {"n": 0}, Tally(2)

        def first_tiles(sources, spares, copies=1):
            pe.wait_ge(lin_read, tiles.at(2))
            outs_ = [lin[:, 0, :], lin[:, 1, :]] + spares
            assert tiles.n % 2 == 0
            for c in range(KD):
                pe.wait_ge(h_ready, h_base["n"] + copies * (c + 1))
                for (hi, lo), out in zip(sources, outs_):
                    slot, tile, *edges = next_tile()
                    mm = passes(out, slot, tile, hi[:, c, :], lo[:, c, :], c == 0, c == KD - 1, *edges)
                    if c == KD - 1:
                        mm.then_inc(lin_written, 1)
            tiles.n += len(sources)
            h_base["n"] += copies * KD
            norm_stats()

        def norm_stats(width=SEQ):
            sums.n += KD
            pe.wait_ge(sum_added, sums.at())
            pe.wait_ge(out_read, outs.at(1))
            pe.matmul(outp[:, 0:width], ones[:], square_sum[:, 0:width], start=True, stop=True).then_inc(
                out_written, 1)
            outs.next()

        def ffn():
            def both():
                linear(h_hi, h_lo, KD)
                linear(h_hi, h_lo, KD)

            first_tiles([(h_hi, h_lo)] * 4, SPARE[0:2])
            linear(h_hi, h_lo, KD, spare=SPARE[2])
            linear(h_hi, h_lo, KD, spare=SPARE[3])
            linear(h_hi, h_lo, KD, late=4)
            linear(h_hi, h_lo, KD, late=4)
            with Turns(pe, FF_TILES // 2 - 2, [(blocks, 4), (tiles, 4)]) as i:
                for u in range(2):
                    both()
            pe.wait_ge(lo_done, lo_base["n"] + FF_TILES)
            lo_base["n"] += FF_TILES
            shares(DOWN_SHARES)
            with Turns(pe, KD // 2, [(blocks, 6), (tiles, 2)]):
                for u in range(2):
                    linear(act_hi, act_lo, FF_TILES)
            shares((BLOCK_TILES,))

        lo_base = {"n": 0}

        def project_out():
            pe.wait_ge(lo_done, lo_base["n"] + KD)
            lo_base["n"] += KD
            with Turns(pe, KD // 2, [(blocks, 2), (tiles, 2)]):
                for u in range(2):
                    linear(o_hi, o_lo, KD)

        for half in range(2):
            mm = pe.matmul(score[0:N_REL_HEADS, 1, half, 0:REL_SPAN // 2], rel[:, 0:N_REL_HEADS],
                           rel[:, N_REL_HEADS + half * (REL_SPAN // 2):N_REL_HEADS + (half + 1) * (REL_SPAN // 2)],
                           start=True, stop=True)
        mm.then_inc(rel_written, 1)
        pe.wait_ge(rel_copied, 1)
        pe.wait_ge(lam_ready, 1)
        pe.matmul(score[:, 0, 0, 0:2], ones[0:64, :], lam_prod[:], start=True, stop=True).then_inc(lam_summed, 1)
        pe.wait_ge(lam_done, 1)
        first_tiles([(h_hi, h_lo)] * 3, SPARE[3:])
        rotate(0)
        rotate(1)
        turn_v(0)
        a_period(0, False, True, True)
        with Turns(pe, 3, [(blocks, 6), (tiles, 10), (scores_free, 8), (probs_in, 8), (turns_done, 10), (outs, 4),
                           (qk, 4)]):
            a_period(1)
            a_period(0)
        a_period(1, True, True, False)
        a_period(0, True, False, False)
        project_out()
        norm_stats()
        ffn()
        norm_stats()
        scores_free.n = probs_in.n = 0
        pe.wait_ge(exp_done, 2 + QT * A_PAIRS)
        first_tiles([(h_hi, h_lo), (g_hi, g_lo), (g_hi, g_lo)], SPARE[3:], 2)
        b_period(0, False, True, True)
        with Turns(pe, 3, [(blocks, 6), (tiles, 6), (scores_free, 8), (probs_in, 8), (turns_done, 14), (outs, 2)]):
            b_period(1)
            b_period(0)
        b_period(1, True, True, False)
        b_period(0, True, False, False)
        project_out()
        norm_stats()
        ffn()
        norm_stats()

        relus, biases, mem_exps, mixes, ys = Tally(), Tally(), Tally(), Tally(QT * A_PAIRS), Tally(lo_base["n"])

        def turn_tile(source, chunks):
            pe.wait_ge(lin_read, tiles.at(2))
            pe.wait_ge(turn_read, turns_done.at(1))
            for t in range(chunks):
                mm = pe.transpose(turn[:, t * P:(t + 1) * P], source[:, t * P:(t + 1) * P], ident)
            mm.then_inc(turn_written, 1)
            turns_done.next()

        def index_scores(t):
            n = P * (t + 1)
            for pair in range(IDX_PAIRS):
                pe.wait_ge(relu_done, relus.at(1))
                for e in range(2):
                    half = slice(64 * e, 64 * e + 64)
                    mm = pe.matmul(score[:, relus.n % 2, e, 0:n], iq[half, pair, t * P:(t + 1) * P], ik[half, 0:n],
                                   start=True, stop=True)
                mm.then_inc(score_written, 1)
                relus.next()

        def sparse_scores(pair, t):
            n = P * (t + 1)
            pe.wait_ge(biased, biases.at(1))
            for e in range(2):
                half = slice(64 * e, 64 * e + 64)
                mm = pe.matmul(score[:, biases.n % 2, e, 0:n], aq[half, pair, t * P:(t + 1) * P], ak[half, pair, 0:n],
                               start=True, stop=True)
            mm.then_inc(score_written, 1)
            biases.next()

        def turn_both(t, weights, chunks):
            pe.wait_ge(mixed, mixes.next())
            pe.wait_ge(turn_read, turns_done.at(1))
            for e in range(2):
                for c in range(chunks):
                    at = (chunks * e + c) * P
                    mm = pe.transpose(turn[:, at:at + P], weights[:, e, c * P:(c + 1) * P], ident)
            mm.then_inc(turn_written, 1)
            turns_done.next()

        def turn_one(t, e):
            if e == 0:
                pe.wait_ge(mixed, mixes.next())
            pe.wait_ge(turn_read, turns_done.at(1))
            for c in range(t + 1):
                mm = pe.transpose(turn[:, c * P:(c + 1) * P], sparse_w[t][:, e, c * P:(c + 1) * P], ident)
            mm.then_inc(turn_written, 1)
            turns_done.next()

        def sparse_values(pair):
            pe.wait_ge(turn_read, turns_done.at(1))
            pe.wait_ge(out_read, outs.at(1))
            for e in range(2):
                half = slice(64 * e, 64 * e + 64)
                for c in range(QT):
                    mm = pe.matmul(outp[half, c * P:SEQ], av[:, c, pair * P + 64 * e:pair * P + 64 * e + 64],
                                   a2_t[:, e, c, c * P:SEQ], start=(c == 0), stop=(c == QT - 1),
                                   skip_group_check=True)
            mm.then_inc(out_written, 1)
            outs.next()

        def mem_scores(pair, t):
            pe.wait_ge(mem_exp, mem_exps.at(1))
            for e in range(2):
                head = 2 * pair + e
                mm = pe.matmul(score[:, mem_exps.n % 2, e, 0:MEM], mq[:, head, t * P:(t + 1) * P], mk[:, head, :],
                               start=True, stop=True)
            mm.then_inc(score_written, 1)
            mem_exps.next()

        def mem_values(pair):
            pe.wait_ge(turn_read, turns_done.at(1))
            for e in range(2):
                pe.wait_ge(out_read, outs.at(1))
                for c in range(MEM_CHUNKS):
                    mm = pe.matmul(outp[:], mv[:, c, (2 * pair + e) * P:(2 * pair + e + 1) * P], mem_a[:, e, c, :],
                                   start=(c == 0), stop=(c == MEM_CHUNKS - 1))
                mm.then_inc(out_written, 1)
                outs.next()

        def two_layer():
            first_tiles([(h_hi, h_lo)] * H_TILES, SPARE[0:2])
            for spare in SPARE[2:]:
                linear(h_hi, h_lo, KD, spare=spare)
            turn_tile(turn_in, QT)
            for t, source in ((3, None), (2, None), (1, turn_in)):
                index_scores(t)
                if source is None:
                    with Turns(pe, H_TILES // 2, [(blocks, 2), (tiles, 2)]):
                        for u in range(2):
                            linear(h_hi, h_lo, KD)
                else:
                    for u in range(H_TILES):
                        linear(h_hi, h_lo, KD)
                        turn_tile(turn_in, QT)
            with Turns(pe, H_TILES // 2, [(blocks, 2), (tiles, 2)]):
                for u in range(2):
                    linear(h_hi, h_lo, KD)
            pe.wait_ge(lin_read, tiles.at(2))
            pe.wait_ge(relu_done, relus.at(2))
            for pair in range(H_TILES + 1):
                cur, prev = pair < H_TILES, pair > 0
                if cur:
                    sparse_scores(pair, 3)
                if prev:
                    turn_both(1, sparse_w[1], 2)
                if cur:
                    linear(h_hi, h_lo, KD, piece=(0, 3))
                    sparse_scores(pair, 2)
                if prev:
                    turn_both(0, sparse_w[0], 1)
                if cur:
                    linear(h_hi, h_lo, KD, piece=(3, 5))
                    sparse_scores(pair, 1)
                if prev:
                    sparse_values(pair - 1)
                if cur:
                    turn_one(3, 0)
                    linear(h_hi, h_lo, KD, piece=(5, 6))
                    turn_one(3, 1)
                    sparse_scores(pair, 0)
                    turn_one(2, 0)
                    linear(h_hi, h_lo, KD, piece=(6, 8))
                    turn_one(2, 1)
            for n, (kind, f) in enumerate(MEM_ORDER):
                if kind == "z":
                    linear(h_hi, h_lo, KD)
                else:
                    first = (kind, f) == ("k", 0)
                    linear(mem_hi, mem_lo, KD, 1 if first else None, MEM)
                    if first:
                        h_base["n"] += KD
                        norm_stats(MEM)
                if kind == "v":
                    turn_tile(mem_v_t, MEM_CHUNKS)
            pe.wait_ge(lin_read, tiles.at(2))
            pe.wait_ge(biased, biases.at(2))
            steps = [(pair, t) for pair in range(H_TILES // 2) for t in (3, 2, 1, 0)]
            for n in range(len(steps) + 2):
                if n < len(steps):
                    mem_scores(*steps[n])
                if n > 4 and steps[n - 2][1] == 3:
                    mem_values(steps[n - 2][0] - 1)
                if n > 1:
                    turn_both(steps[n - 2][1], mem_w[:, steps[n - 2][1]], MEM_CHUNKS)
            mem_values(H_TILES // 2 - 1)
            pe.wait_ge(pool_loaded, pool_loads.next() * 16)
            for g in range(POOL_GROUPS):
                linear(h_hi, h_lo, KD)
                linear(h_hi, h_lo, KD)
                pe.wait_ge(pool_ready, pools.next())
                pe.wait_ge(lin_read, tiles.at(1))
                pe.matmul(lin[:, tiles.n % 2, :], pool_w[:, g, :], pooled[:], start=True, stop=True).then_inc(
                    lin_written, 1)
                tiles.next()
            ys.n += 3 * H_TILES
            pe.wait_ge(lo_done, ys.at())
            shares(MERGE_SHARES)
            with Turns(pe, KD // 2, [(blocks, 10), (tiles, 12)]):
                for u in range(2):
                    for b in range(3):
                        linear(h_hi, h_lo, KD)
                    for y in (y_pool, y_attn, y_mem):
                        linear(*y, H_TILES)
            shares((BLOCK_TILES,))
            ys.n += KD
            pe.wait_ge(lo_done, ys.at())
            with Turns(pe, KD // 2, [(blocks, 2), (tiles, 2)]):
                for u in range(2):
                    linear(sum_hi, sum_lo, KD)

        pools, pool_loads = Tally(), Tally()
        for layer in range(LAYERS):
            two_layer()
        norm_stats()

    @block.scalar
    def _(act):
        step = Tally()
        act.sem_inc(turn_read, 1)
        act.sem_inc(out_read, 1)
        act.sem_inc(exp_done, 2)
        turned, outs, negs, exps = Tally(), Tally(), Tally(), Tally()
        scored, sticks, subs, lins = Tally(), Tally(), Tally(), Tally()
        sq_in, his = Tally(), Tally()

        def then_wait(ins):
            ins.then_inc(a_step, 1)
            act.wait_ge(a_step, step.next())

        def soft_exp(t):
            n = P * (t + 1)
            act.wait_ge(negmax_done, negs.next())
            slot = (negs.n - 1) % 2
            for e in range(2):
                i = act.activation(probs[:, t % 2, e, 0:n], score[:, slot, e, 0:n], ACT.Exp,
                                   bias=negmax[:, slot, e:e + 1], accum_out=rowsum[:, slot, e:e + 1])
            i.then_inc(exp_done, 1)

        def keep_turned(t, e):
            act.wait_ge(turn_written, turned.next())
            act.activation(a_t[:, e, 0:t + 1, t * P:(t + 1) * P],
                           turn[:, 0:(t + 1) * P].rearrange("p (c n) -> p c n", n=P), ACT.Copy).then_inc(turn_read, 1)

        def keep_values(parity):
            act.wait_ge(turn_written, turned.next())
            act.activation(v_now[:, parity].rearrange("p c n -> p (c n)"), turn[:], ACT.Copy).then_inc(turn_read, 1)

        def to_rstd(out, width, signal, tally_out):
            act.wait_ge(out_written, tally_out.next())
            act.activation(out, outp[:, 0:out.shape[1]], ACT.Ln, bias=eps[:, 0:1], scale=1.0 / width).then_inc(out_read, 1)
            act.wait_ge(out_read, tally_out.at(1))
            act.activation(out, out, ACT.Exp, scale=-0.5).then_inc(signal, 1)

        def a_period(parity, pair, prev=True, cur=True, nxt=True):
            other = 1 - parity
            if cur:
                soft_exp(3)
            if prev:
                keep_turned(0, 0)
                act.wait_ge(out_written, outs.next())
                act.activation(o_raw[:], outp[:], ACT.Copy)
                act.activation(o_sq[:], outp[:], ACT.Square).then_inc(out_read, 1)
            if cur:
                soft_exp(2)
                keep_turned(3, 0)
            if prev:
                to_rstd(o_rstd[:], P, sub_rstd, outs)
            if cur:
                soft_exp(1)
                keep_turned(2, 0)
            if prev:
                act.wait_ge(sub_scaled, subs.next())
                act.activation(o_hi[:, bass.ds(pair - 1, 1), :], o_sq[:], ACT.Copy,
                               scale=sub_gain[:, 0:1]).then_inc(hi_done, 1)
            if cur:
                soft_exp(0)
                keep_turned(1, 0)
            if nxt:
                keep_values(other)

        def b_logs(t, meanwhile=()):
            n = P * (t + 1)
            act.wait_ge(score_written, scored.next())
            slot = (scored.n - 1) % 2
            out = decay[t][:]
            act.activation(out, score[:, slot, :, 0:n], ACT.Abs)
            act.activation(probs[:, slot, :, 0:n], score[:, slot, :, 0:n], ACT.Copy).then_inc(score_copied, 1)
            for job in meanwhile:
                job()
            act.wait_ge(score_copied, copied.next())
            then_wait(act.activation(out, out, ACT.Exp, scale=-1.0))
            act.activation(out, out, ACT.Ln, bias=ones[:, 0:1]).then_inc(logs_done, 1)

        copied = Tally(2)

        def b_weights(t):
            act.wait_ge(sticks_done, sticks.next())
            act.activation(decay[t][:], decay[t][:], ACT.Exp).then_inc(weights_done, 1)

        def keep_both(t):
            act.wait_ge(turn_written, turned.next())
            act.activation(a_t[:, :, 0:t + 1, t * P:(t + 1) * P],
                           turn[:, 0:2 * (t + 1) * P].rearrange("p (e c n) -> p e c n", e=2, n=P),
                           ACT.Copy).then_inc(turn_read, 1)

        def b_period(parity, pair, prev=True, cur=True, nxt=True):
            if cur:
                b_logs(3, [lambda: keep_both(1)] if prev else [])
            elif prev:
                keep_both(1)
            if prev:
                b_weights(0)
            if cur:
                keep_values(parity)

            if cur:
                b_logs(2, [lambda: keep_both(0)] if prev else [])
                b_weights(3)
            elif prev:
                keep_both(0)

            if cur:
                b_logs(1)
                b_weights(2)
            if prev:
                act.wait_ge(out_written, outs.next())
                act.activation(o_hi[:, bass.ds(pair - 1, 1), :], outp[:], ACT.Copy).then_inc(hi_done, 1)
                act.activation(o_raw[:], outp[:], ACT.Copy).then_inc(out_read, 1)
            if cur:
                keep_turned(3, 0)
                keep_turned(3, 1)

            if cur:
                b_logs(0, [lambda: keep_turned(2, 0)])
                b_weights(1)
                keep_turned(2, 1)

        sq = Tally()

        def out_squares(m):
            def one(f, k):
                act.wait_ge(lin_read, lins.next())
                act.wait_ge(sum_added, sq.at(1))
                act.activation(squares[:, k, :], m[:, bass.ds(f, 1), :], ACT.Square).then_inc(square_done, 1)
                sq.next()

            with Turns(act, KD // 2, [(lins, 2), (sq, 2)]) as i:
                for k in range(2):
                    one(2 * i + k, k)

        xs = Tally()

        def norm_in(names, ready=x_ready, counts=None, source=x, width=SEQ):
            counts = xs if counts is None else counts
            for f in range(KD):
                if ready is not None:
                    act.wait_ge(ready, counts.next())
                act.wait_ge(sum_added, sq.at(1))
                act.activation(squares[:, f % 2, 0:width], source[:, f, :], ACT.Square).then_inc(square_done, 1)
                sq.next()
                for name, hi in names:
                    act.activation(hi[:, f, :], source[:, f, :], ACT.Copy, scale=gain(name, f)).then_inc(hi_done, 1)

        def ffn():
            def one(j, u, first):
                act.wait_ge(lin_read, lins.next())
                act.activation(gate_s[:, u, :], gate_s[:, u, :], ACT.Silu).then_inc(silu_done, 1)
                lins.next()
                act.wait_ge(act_ready, acts.next())
                act.activation(act_hi[:, bass.ds(j, 1), :], up_s[:, u, :], ACT.Copy).then_inc(hi_done, 1)

            for u in range(2):
                one(u, u, True)
            with Turns(act, FF_TILES // 2 - 1, [(lins, 4), (acts, 2)]) as i:
                for u in range(2):
                    one(2 * i + (u + 2), u, False)

        acts = Tally()

        act.sem_inc(sum_added, 2)
        act.wait_ge(const_done, 2)
        act.wait_ge(params_loaded, 80)
        act.wait_ge(rel_written, 1)
        for half in range(2):
            i = act.activation(rel_rows[:, half * (REL_SPAN // 2):(half + 1) * (REL_SPAN // 2)],
                               score[0:N_REL_HEADS, 1, half, 0:REL_SPAN // 2], ACT.Copy)
        i.then_inc(rel_copied, 1)
        act.wait_ge(rel_copied, 1)
        act.dma_start(rel_dram, rel_rows[:]).then_inc(rel_stored, 16)
        act.wait_ge(lam_summed, 1)
        act.activation(lam_exp[:], score[:, 0, 0, 0:2], ACT.Exp).then_inc(lam_done, 1)
        act.wait_ge(x_loaded, 16)
        norm_in([("mix_pre0", h_hi)], ready=None)
        to_rstd(rstd[:], D, rstd_done, outs)
        lins.n = 2
        keep_values(0)
        a_period(0, 0, False, True, True)
        with Turns(act, 3, [(negs, 8), (turned, 10), (outs, 4), (subs, 2)]) as i:
            a_period(1, 2 * i + 1)
            a_period(0, 2 * i + 2)
        a_period(1, 7, True, True, False)
        a_period(0, 8, True, False, False)
        lins.n += 5 * A_PAIRS
        act.wait_ge(rel_stored, 16)
        out_squares(m_attn)
        to_rstd(rstd_m[:], D, rstd_done, outs)
        norm_in([("ffn_pre0", h_hi)])
        to_rstd(rstd[:], D, rstd_done, outs)
        ffn()
        out_squares(m_ffn)
        to_rstd(rstd_m[:], D, rstd_done, outs)
        norm_in([("mix_pre1", h_hi), ("kv", g_hi)])
        to_rstd(rstd[:], D, rstd_done, outs)
        scored.n = QT * A_PAIRS
        act.sem_inc(score_copied, 2)
        b_period(0, 0, False, True, True)
        with Turns(act, 3, [(step, 8), (copied, 8), (scored, 8), (sticks, 8), (turned, 14), (outs, 2)]) as i:
            b_period(1, 2 * i + 1)
            b_period(0, 2 * i + 2)
        b_period(1, 7, True, True, False)
        b_period(0, 8, True, False, False)
        lins.n += 3 * A_PAIRS
        out_squares(m_attn)
        to_rstd(rstd_m[:], D, rstd_done, outs)
        norm_in([("ffn_pre1", h_hi)])
        to_rstd(rstd[:], D, rstd_done, outs)
        ffn()
        out_squares(m_ffn)
        to_rstd(rstd_m[:], D, rstd_done, outs)
        act.sem_inc(relu_done, 2)
        act.sem_inc(mem_exp, 2)
        act.dma_start(bias[:], toeplitz).then_inc(bias_loaded, 16)
        norm_in([("norm0", h_hi)])
        to_rstd(rstd[:], D, rstd_done, outs)
        scored.n = 2 * QT * A_PAIRS
        ready_y = Tally()

        def index_relu(t):
            n = P * (t + 1)
            for pair in range(IDX_PAIRS):
                act.wait_ge(score_written, scored.next())
                act.wait_ge(index_done, relued.at(1))
                act.activation(relu_s[:, relued.n % 2, :, 0:n], score[:, relued.n % 2, :, 0:n], ACT.Relu).then_inc(
                    relu_done, 1)
                relued.next()

        relued = Tally()

        def keep(out, chunks, cols=P):
            act.wait_ge(turn_written, turned.next())
            act.activation(out, turn[:, 0:chunks * P].rearrange("p (c n) -> p c n", n=P)[:, :, 0:cols],
                           ACT.Copy).then_inc(turn_read, 1)

        def sparse_exp(t, slot):
            act.wait_ge(negmax_done, negs.next())
            for e in range(2):
                i = act.activation(sparse_w[t][:, e, :], sparse_w[t][:, e, :], ACT.Exp,
                                   bias=negmax[:, slot, e:e + 1], accum_out=rowsum[:, slot, e:e + 1])
            i.then_inc(exp_done, 1)

        def sparse_keep(t):
            if t > 1:
                for e in range(2):
                    keep(a2_t[:, e, 0:t + 1, t * P:(t + 1) * P], t + 1)
            else:
                keep_two(a2_t, t, t + 1)

        def keep_two(out, t, chunks):
            act.wait_ge(turn_written, turned.next())
            act.activation(out[:, :, 0:chunks, t * P:(t + 1) * P],
                           turn[:, 0:2 * chunks * P].rearrange("p (e c n) -> p e c n", e=2, n=P),
                           ACT.Copy).then_inc(turn_read, 1)

        def take_out():
            act.wait_ge(out_written, outs.next())
            act.activation(o_raw[:], outp[:], ACT.Copy).then_inc(out_read, 1)

        def y_hi(y, f):
            act.wait_ge(y_ready, ready_y.next())
            act.activation(y[0][:, f, :], y_now[:], ACT.Copy).then_inc(hi_done, 1)

        def mem_soft(t, slot):
            act.wait_ge(negmax_done, negs.next())
            for e in range(2):
                i = act.activation(mem_w[:, t, e, :], score[:, slot, e, 0:MEM], ACT.Exp,
                                   bias=negmax[:, slot, e:e + 1], accum_out=rowsum[:, slot, e:e + 1])
            i.then_inc(mem_exp, 1)

        def two_layer(layer):
            lins.n += H_TILES + 2
            keep(iw[:], QT, 8)
            for t in (3, 2, 1):
                index_relu(t)
                lins.n += H_TILES
                if t == 1:
                    for f in range(H_TILES):
                        keep(av[:, :, f * P:(f + 1) * P], QT)
            for f in range(H_TILES):
                act.wait_ge(lin_read, lins.next())
                act.activation(az[:, f, :], az[:, f, :], ACT.Silu).then_inc(silu_done, 1)
            steps = [(pair, t) for pair in range(H_TILES) for t in (3, 2, 1, 0)]
            for n, (pair, t) in enumerate(steps):
                sparse_exp(t, n % 2)
                if n > 4 and t == 1:
                    take_out()
                if n > 1:
                    sparse_keep(steps[n - 2][1])
                if n > 4 and t == 0:
                    y_hi(y_attn, pair - 1)
            sparse_keep(1)
            sparse_keep(0)
            take_out()
            y_hi(y_attn, H_TILES - 1)
            lins.n += H_TILES
            scored.n += QT * H_TILES
            act.dma_start(mem[:], ap["mem_t"].rearrange("c p n -> p c n")).then_inc(mem_loaded, 16)
            act.wait_ge(mem_loaded, 16 * (layer + 1))
            norm_in([(f"mem_norm{layer}", mem_hi)], None, None, mem, MEM)
            return

        def two_layer_rest(layer):
            to_rstd(rstd_m[:, 0:MEM], D, rstd_done, outs)
            for kind, f in MEM_ORDER:
                lins.next()
                if kind == "z":
                    act.wait_ge(lin_read, lins.at())
                    act.activation(mz[:, f, :], mz[:, f, :], ACT.Silu).then_inc(silu_done, 1)
                if kind == "v":
                    keep(mv[:, :, f * P:(f + 1) * P], MEM_CHUNKS)
            steps = [(pair, t) for pair in range(H_TILES // 2) for t in (3, 2, 1, 0)]
            for n in range(len(steps) + 2):
                if n < len(steps):
                    mem_soft(steps[n][1], n % 2)
                if n > 4 and steps[n - 2][1] == 3:
                    for e in range(2):
                        take_out()
                        y_hi(y_mem, 2 * (steps[n - 2][0] - 1) + e)
                if n > 1:
                    keep_two(mem_a, steps[n - 2][1], MEM_CHUNKS)
            for e in range(2):
                take_out()
                y_hi(y_mem, H_TILES - 2 + e)
            scored.n += QT * H_TILES // 2
            act.dma_start(pool_w[:], ap["pool_w"][layer]).then_inc(pool_loaded, 16)
            for g in range(POOL_GROUPS):
                lins.next()
                act.wait_ge(lin_read, lins.next())
                act.activation(pool_z[:], pool_z[:], ACT.Silu).then_inc(silu_done, 1)
                act.wait_ge(lin_read, lins.next())
                act.activation(y_pool[0][:, g, :], y_now[:], ACT.Copy).then_inc(hi_done, 1)
            def merge(f, u):
                for b in range(3):
                    act.wait_ge(lin_read, lins.next())
                    act.activation(gates[:, u, b, :], gates[:, u, b, :], ACT.Sigmoid).then_inc(silu_done, 1)
                lins.n += 3
                act.wait_ge(gated, ready_sum.next())
                act.activation(sum_hi[:, bass.ds(f, 1), :], merged[:, u, :], ACT.Copy).then_inc(hi_done, 1)

            with Turns(act, KD // 2, [(lins, 12), (ready_sum, 2)]) as i:
                for u in range(2):
                    merge(2 * i + u, u)
            norm_in([(f"norm{layer + 1}", h_hi)] if layer + 1 < LAYERS else [], lin_read, lins)
            to_rstd(rstd[:], D, rstd_done, outs)

        ready_sum = Tally()
        for layer in range(LAYERS):
            two_layer(layer)
            two_layer_rest(layer)

    @block.vector
    def _(dve):
        step = Tally()
        dve.sem_inc(lin_read, 2)

        def do(ins):
            ins.then_inc(v_step, 1)
            step.next()

        def settle():
            dve.wait_ge(v_step, step.at())

        lins, reads = Tally(), Tally(2)
        exps, scored, logs, silus, his, sqs, sums, rs, subs, qks = (Tally() for _ in range(10))

        def evacuate(out, factor, source_scale=1.0, width=SEQ, spare=None):
            dve.wait_ge(lin_written, lins.next())
            bank = lin[:, (lins.n - 1) % 2, 0:width] if spare is None else spare
            dve.scalar_tensor_tensor(out, bank, source_scale, factor, ALU.mult,
                                     ALU.mult).then_inc(lin_read, 1)
            reads.next()

        def rope(which, out):
            dve.wait_ge(lin_written, lins.next())
            bank = (lins.n - 1) % 2
            dve.tensor_tensor(rot_sin[:], lin[:, bank, :], sin, ALU.mult).then_inc(lin_read, 1)
            reads.next()
            do(dve.tensor_tensor(out, plain[:, which, :], cos, ALU.mult))
            dve.wait_ge(lin_read, reads.at())
            settle()
            dve.tensor_tensor(out, out, rot_sin[:], ALU.add).then_inc(qk_ready, 1)

        def maxima(t):
            n = P * (t + 1)
            dve.wait_ge(score_written, scored.next())
            slot = (scored.n - 1) % 2
            dve.tensor_reduce(negmax[:, slot, :], score[:, slot, :, 0:n], AX.X, ALU.max,
                              negate=True).then_inc(negmax_done, 1)

        def combine(t):
            n = P * (t + 1)
            dve.wait_ge(exp_done, exps.next())
            slot = (exps.n - 1) % 2
            do(dve.reciprocal(rinv[:], rowsum[:, slot, :]))
            settle()
            do(dve.tensor_scalar(probs[:, t % 2, 1, 0:n], probs[:, t % 2, 1, 0:n], rinv[:, 1:2], neg_lam[:, 0:1],
                                 ALU.mult, ALU.mult))
            settle()
            dve.scalar_tensor_tensor(probs[:, t % 2, 0, 0:n], probs[:, t % 2, 0, 0:n], rinv[:, 0:1],
                                     probs[:, t % 2, 1, 0:n], ALU.mult, ALU.add).then_inc(mixed, 1)

        def a_period(parity, pair, prev=True, cur=True, nxt=True):
            other = 1 - parity
            if cur:
                maxima(3)
            if nxt:
                evacuate(plain[:, 0, :], rstd[:], 0.125)
            if cur:
                combine(3)
                maxima(2)
            if nxt:
                rope(0, q_now[:, other, :])
                evacuate(plain[:, 1, :], rstd[:])
            if cur:
                combine(2)
            if prev:
                dve.wait_ge(sub_rstd, subs.next())
                dve.tensor_tensor(o_sq[:], o_raw[:], o_rstd[:], ALU.mult).then_inc(sub_scaled, 1)
            if cur:
                maxima(1)
            if nxt:
                rope(1, k_now[:, other, :])
                evacuate(v_t[:], rstd[:])
            if cur:
                combine(1)
            if prev:
                dve.wait_ge(hi_done, his.next())
                dve.scalar_tensor_tensor(o_lo[:, bass.ds(pair - 1, 1), :], o_sq[:], sub_gain[:, 0:1],
                                         o_hi[:, bass.ds(pair - 1, 1), :].bitcast(F32), ALU.mult,
                                         ALU.subtract).then_inc(lo_done, 1)
            if cur:
                maxima(0)
                combine(0)

        def b_sticks(t):
            n = P * (t + 1)
            dve.wait_ge(logs_done, logs.next())
            z = probs[:, (logs.n - 1) % 2, :, 0:n]
            sums_at = decay[t][:]
            do(dve.scalar_tensor_tensor(softplus[:, :, 0:n], z, 0.0, sums_at, ALU.max, ALU.add))
            settle()
            for e in range(2):
                back = softplus[:, e, 0:n][:, ::-1]
                do(dve.tensor_tensor_scan(sums_at[:, e, :][:, ::-1], back, back, 0.0, ALU.add, ALU.bypass))
            settle()
            dve.tensor_tensor(sums_at, z, sums_at, ALU.subtract).then_inc(sticks_done, 1)

        def b_period(parity, pair, prev=True, cur=True, nxt=True):
            other = 1 - parity
            if cur:
                b_sticks(3)
            if nxt:
                evacuate(q_now[:, other, :], rstd[:], 0.125)
            if cur:
                b_sticks(2)
            if nxt:
                evacuate(k_now[:, other, :], rstd[:])
            if cur:
                b_sticks(1)
            if prev:
                dve.wait_ge(hi_done, his.next())
                dve.wait_ge(out_read, outr.next())
                dve.tensor_tensor(o_lo[:, bass.ds(pair - 1, 1), :], o_raw[:],
                                  o_hi[:, bass.ds(pair - 1, 1), :].bitcast(F32), ALU.subtract).then_inc(lo_done, 1)
            if cur:
                b_sticks(0)
            if nxt:
                evacuate(v_t[:], rstd[:])

        outr = Tally()

        def add_square(first, k, width=SEQ):
            dve.wait_ge(square_done, sqs.next())
            total, new = square_sum[:, 0:width], squares[:, k, 0:width]
            if first:
                i = dve.tensor_copy(total, new)
            else:
                i = dve.tensor_tensor(total, total, new, ALU.add)
            i.then_inc(sum_added, 1)
            dve.wait_ge(sum_added, added.next())

        added = Tally(2)

        def out_tiles(m):
            def tile(f, k):
                dve.wait_ge(lin_written, lins.next())
                dve.tensor_copy(m[:, bass.ds(f, 1), :], lin[:, k, :]).then_inc(lin_read, 1)
                reads.next()

            tile(0, 0)
            tile(1, 1)
            add_square(True, 0)
            with Turns(dve, KD // 2 - 1, [(lins, 2), (reads, 2), (sqs, 2), (added, 2)]) as i:
                tile(2 * i + 2, 0)
                add_square(False, 1)
                tile(2 * i + 3, 1)
                add_square(False, 0)
            add_square(False, 1)

        def norm_in(names, m=None, post=None):
            if m is not None:
                dve.wait_ge(rstd_done, rs.next())
            for f in range(KD):
                if m is not None:
                    do(dve.scalar_tensor_tensor(m[:, f, :], m[:, f, :], gain(post, f), rstd_m[:], ALU.mult, ALU.mult))
                    settle()
                    dve.tensor_tensor(x[:, f, :], x[:, f, :], m[:, f, :], ALU.add).then_inc(x_ready, 1)
                    dve.wait_ge(x_ready, xs.next())
                if f:
                    finish(names, f - 1)
            if names:
                finish(names, KD - 1)

        xs = Tally()

        def finish(names, f, source=x, width=SEQ):
            if not names:
                return
            add_square(f == 0, f % 2, width)
            for name, hi, lo in names:
                if name is None:
                    continue
                dve.wait_ge(hi_done, his.next())
                dve.scalar_tensor_tensor(lo[:, f, :], source[:, f, :], gain(name, f), hi[:, f, :].bitcast(F32), ALU.mult,
                                         ALU.subtract).then_inc(h_ready, 1)

        def ffn():
            def one(j, u, lagging, spares=(None, None)):
                evacuate(gate_s[:, u, :], rstd[:], spare=spares[0])
                if lagging:
                    low(j - 1, 1 - u)
                evacuate(up_s[:, u, :], rstd[:], spare=spares[1])
                dve.wait_ge(silu_done, silus.next())
                dve.wait_ge(lin_read, reads.at())
                dve.tensor_tensor(up_s[:, u, :], gate_s[:, u, :], up_s[:, u, :], ALU.mult).then_inc(act_ready, 1)
                dve.wait_ge(act_ready, acts.next())

            def low(j, u):
                dve.wait_ge(hi_done, his.next())
                dve.tensor_tensor(act_lo[:, bass.ds(j, 1), :], up_s[:, u, :],
                                  act_hi[:, bass.ds(j, 1), :].bitcast(F32), ALU.subtract).then_inc(lo_done, 1)

            one(0, 0, False)
            one(1, 1, True, SPARE[0:2])
            one(2, 0, True, SPARE[2:4])
            one(3, 1, True)
            with Turns(dve, FF_TILES // 2 - 2, [(lins, 4), (reads, 4), (silus, 2), (acts, 2), (his, 2)]) as i:
                for u in range(2):
                    one(2 * i + (u + 4), u, True)
            low(FF_TILES - 1, 1)

        acts = Tally()
        dve.memset(ones[:], 1.0).then_inc(const_done, 1)
        dve.memset(eps[:], EPS).then_inc(const_done, 1)
        dve.wait_ge(params_loaded, 80)
        dve.tensor_copy(tables[:], a_t[:, 0, 0, :]).then_inc(const_done, 1)
        lam = params[0:64, LAMBDA_AT:LAMBDA_AT + 4]
        dve.tensor_tensor(lam_prod[:], lam[:, 0:2], lam[:, 2:4], ALU.mult).then_inc(lam_ready, 1)
        dve.wait_ge(lam_done, 1)
        do(dve.tensor_tensor(neg_lam[:], lam_exp[:, 1:2], lam_exp[:, 0:1], ALU.subtract))
        settle()
        do(dve.tensor_scalar(neg_lam[:], neg_lam[:], -LAMBDA_INIT, None, ALU.add))
        do(dve.tensor_scalar(sub_gain[:], params[:, SUBLN_AT:SUBLN_AT + 1], 1.0 - LAMBDA_INIT, None, ALU.mult))
        dve.wait_ge(x_loaded, 16)
        norm_in([("mix_pre0", h_hi, h_lo)])
        dve.wait_ge(rstd_done, rs.next())
        evacuate(plain[:, 0, :], rstd[:], 0.125)
        evacuate(plain[:, 1, :], rstd[:])
        evacuate(v_t[:], rstd[:], spare=SPARE[3])
        rope(0, q_now[:, 0, :])
        dve.wait_ge(qk_ready, 1)
        rope(1, k_now[:, 0, :])
        exps.n = 2
        a_period(0, 0, False, True, True)
        with Turns(dve, 3, [(step, 20), (lins, 10), (reads, 10), (exps, 8), (scored, 8), (subs, 2), (his, 2)]) as i:
            a_period(1, 2 * i + 1)
            a_period(0, 2 * i + 2)
        a_period(1, 7, True, True, False)
        a_period(0, 8, True, False, False)
        out_tiles(m_attn)
        norm_in([("ffn_pre0", h_hi, h_lo)], m_attn, "mix_post0")
        dve.wait_ge(rstd_done, rs.next())
        ffn()
        out_tiles(m_ffn)
        norm_in([("mix_pre1", h_hi, h_lo), ("kv", g_hi, g_lo)], m_ffn, "ffn_post0")
        dve.wait_ge(rstd_done, rs.next())
        outr.n = 1 + 1 + 2 * A_PAIRS + 4
        evacuate(q_now[:, 0, :], rstd[:], 0.125)
        evacuate(k_now[:, 0, :], rstd[:])
        evacuate(v_t[:], rstd[:], spare=SPARE[3])
        b_period(0, 0, False, True, True)
        with Turns(dve, 3, [(step, 24), (lins, 6), (reads, 6), (logs, 8), (his, 2), (outr, 2)]) as i:
            b_period(1, 2 * i + 1)
            b_period(0, 2 * i + 2)
        b_period(1, 7, True, True, False)
        b_period(0, 8, True, False, False)
        out_tiles(m_attn)
        norm_in([("ffn_pre1", h_hi, h_lo)], m_attn, "mix_post1")
        dve.wait_ge(rstd_done, rs.next())
        ffn()
        out_tiles(m_ffn)
        norm_in([("norm0", h_hi, h_lo)], m_ffn, "ffn_post1")
        dve.wait_ge(rstd_done, rs.next())
        dve.sem_inc(index_done, 2)
        dve.sem_inc(biased, 2)
        scored.n = 2 * QT * A_PAIRS
        relus, ready_y = Tally(2), Tally()
        mem_exps = Tally(2)
        outr.n += 4

        def index_sum(t):
            n = P * (t + 1)
            for pair in range(IDX_PAIRS):
                dve.wait_ge(relu_done, relus.next())
                slot = (relus.n - 1) % 2
                for e in range(2):
                    head = 2 * pair + e
                    weight = iw[:, t, head:head + 1]
                    if head == 0:
                        i = dve.tensor_scalar(index[:, 0:n], relu_s[:, slot, e, 0:n], weight, None, ALU.mult)
                    else:
                        i = dve.scalar_tensor_tensor(index[:, 0:n], relu_s[:, slot, e, 0:n], weight, index[:, 0:n],
                                                     ALU.mult, ALU.add)
                    if e:
                        i.then_inc(index_done, 1)
                        dve.wait_ge(index_done, indexed.next())
                    else:
                        do(i)
                        settle()
            do(dve.memset(index[0:CHUNK, n - CHUNK:n], NEG))
            settle()

        indexed = Tally(2)

        def top_rounds(t, rounds):
            n = P * (t + 1)
            for _ in range(rounds):
                do(dve.max(top8[:], index[:, 0:n]))
                settle()
                do(dve.match_replace(index[:, 0:n], top8[:], index[:, 0:n], TAKEN))
                settle()

        def choose(t):
            n = P * (t + 1)
            do(dve.tensor_scalar(chosen[:, t, 0:n], index[:, 0:n], TAKEN / 2, NEG, ALU.is_ge, ALU.mult))
            settle()

        def sparse_front(pair, t, slot):
            n, w = P * (t + 1), sparse_w[t][:]
            biases_back = bias[:, 2 * pair:2 * pair + 2, P * t + P - n:P * t + P][:, :, ::-1]
            dve.wait_ge(score_written, scored.next())
            dve.tensor_tensor(w, score[:, slot, :, 0:n], biases_back,
                              ALU.add).then_inc(biased, 1)
            dve.wait_ge(biased, biases.next())
            do(dve.tensor_tensor(w, w, chosen[:, t:t + 1, 0:n].broadcast_to([P, 2, n]), ALU.add))
            settle()
            dve.tensor_reduce(negmax[:, slot, :], w, AX.X, ALU.max, negate=True).then_inc(negmax_done, 1)

        biases = Tally(2)

        mixes = Tally(QT * A_PAIRS)

        def normalise(weights, slot):
            dve.wait_ge(mixed, mixes.at())
            do(dve.reciprocal(rinv[:], rowsum[:, slot, :]))
            settle()
            for e in range(2):
                i = dve.tensor_scalar(weights[:, e, :], weights[:, e, :], rinv[:, e:e + 1], None, ALU.mult)
            i.then_inc(mixed, 1)
            mixes.next()

        def sparse_back(t, slot):
            dve.wait_ge(exp_done, exps.next())
            normalise(sparse_w[t], slot)

        def y_of(factor, y, f):
            dve.wait_ge(out_read, outr.next())
            dve.wait_ge(lo_done, lows.at())
            dve.tensor_tensor(y_now[:], o_raw[:], factor, ALU.mult).then_inc(y_ready, 1)
            y_low(y, f)

        def y_low(y, f):
            dve.wait_ge(hi_done, his.next())
            dve.tensor_tensor(y[1][:, f, :], y_now[:], y[0][:, f, :].bitcast(F32), ALU.subtract).then_inc(lo_done, 1)
            lows.next()

        lows = Tally(2 * (KD + FF_TILES))

        def mem_front(slot):
            dve.wait_ge(score_written, scored.next())
            dve.tensor_reduce(negmax[:, slot, :], score[:, slot, :, 0:MEM], AX.X, ALU.max,
                              negate=True).then_inc(negmax_done, 1)

        def two_layer(layer):
            for f, spare in enumerate((None, None, *SPARE[0:2])):
                evacuate(iq[:, f, :], rstd[:], spare=spare)
            evacuate(ik[:], rstd[:], spare=SPARE[2])
            evacuate(turn_in[:], rstd[:], IDX_SCALE, spare=SPARE[3])
            dve.wait_ge(turn_read, iw_turned[layer])
            for t, out, factor in ((3, aq, 0.125), (2, ak, 1.0)):
                index_sum(t)
                for f in range(H_TILES):
                    evacuate(out[:, f, :], rstd[:], factor)
                    top_rounds(t, TOPK // 8 // H_TILES)
                choose(t)
            index_sum(1)
            for f in range(H_TILES):
                evacuate(turn_in[:], rstd[:])
                top_rounds(1, TOPK // 8 // H_TILES)
            choose(1)
            do(dve.memset(chosen[:, 0, 0:P], 0.0))
            settle()
            do(dve.memset(chosen[0:CHUNK, 0, P - CHUNK:P], NEG))
            for f in range(H_TILES):
                evacuate(az[:, f, :], rstd[:])
            silus.n += H_TILES
            dve.wait_ge(silu_done, silus.at())
            dve.wait_ge(bias_loaded, 16)
            scored.n += 3 * IDX_PAIRS
            steps = [(pair, t) for pair in range(H_TILES) for t in (3, 2, 1, 0)]
            for n, (pair, t) in enumerate(steps):
                sparse_front(pair, t, n % 2)
                if n:
                    sparse_back(steps[n - 1][1], (n - 1) % 2)
                if pair and t == 3:
                    evacuate(mq[:, pair - 1, :], rstd[:], MEM_SCALE)
                if n > 4 and t == 0:
                    y_of(az[:, pair - 1, :], y_attn, pair - 1)
            sparse_back(0, 1)
            evacuate(mq[:, H_TILES - 1, :], rstd[:], MEM_SCALE)
            y_of(az[:, H_TILES - 1, :], y_attn, H_TILES - 1)
            dve.wait_ge(mem_loaded, 16 * (layer + 1))
            for f in range(KD):
                finish([(f"mem_norm{layer}", mem_hi, mem_lo)], f, mem, MEM)
                if f % 4 == 3:
                    evacuate(mz[:, f // 4, :], rstd[:])
            for n, (kind, f) in enumerate(MEM_ORDER[2:]):
                if n == 0:
                    dve.wait_ge(rstd_done, rs.next())
                    outr.n += 1
                if kind == "z":
                    evacuate(mz[:, f, :], rstd[:])
                elif kind == "k":
                    evacuate(mk[:, f, :], rstd_m[:, 0:MEM], 1.0, MEM)
                else:
                    evacuate(mem_v_t, rstd_m[:, 0:MEM], 1.0, MEM)
            silus.n += H_TILES
            dve.wait_ge(silu_done, silus.at())
            steps = [(pair, t) for pair in range(H_TILES // 2) for t in (3, 2, 1, 0)]
            for n in range(len(steps) + 1):
                if n < len(steps):
                    mem_front(n % 2)
                if n:
                    dve.wait_ge(mem_exp, mem_exps.next())
                    normalise(mem_w[:, steps[n - 1][1]], (n - 1) % 2)
                if n > 5 and steps[n - 2][1] == 3:
                    for e in range(2):
                        y_of(mz[:, 2 * (steps[n - 2][0] - 1) + e, :], y_mem, 2 * (steps[n - 2][0] - 1) + e)
            for e in range(2):
                y_of(mz[:, H_TILES - 2 + e, :], y_mem, H_TILES - 2 + e)
            for t in (pool_u, pool_a, pool_b):
                do(dve.memset(t[:, 0:POOL_EDGE], 0.0))
            settle()
            body = slice(POOL_EDGE, POOL_EDGE + SEQ)
            for g in range(POOL_GROUPS):
                evacuate(pool_u[:, body], rstd[:])
                dve.wait_ge(lin_read, reads.at())
                source = pool_u
                for level in range(g + 1):
                    out = pool_b if source is pool_a else pool_a
                    back = slice(POOL_EDGE - 2 ** level, POOL_EDGE + SEQ - 2 ** level)
                    do(dve.tensor_tensor(out[:, body], source[:, body], source[:, back], ALU.add))
                    settle()
                    source = out
                inverse = inverse_counts[:, g, :]
                do(dve.tensor_tensor(edge[:], source[:, POOL_EDGE:2 * POOL_EDGE], inverse, ALU.mult))
                do(dve.scalar_tensor_tensor(pooled[:], source[:, body], 0.5 ** (g + 1), pool_u[:, body], ALU.mult,
                                            ALU.subtract))
                settle()
                dve.tensor_tensor(pooled[:, 0:POOL_EDGE], edge[:], pool_u[:, POOL_EDGE:2 * POOL_EDGE],
                                  ALU.subtract).then_inc(pool_ready, 1)
                evacuate(pool_z[:], rstd[:])
                dve.wait_ge(silu_done, silus.next())
                dve.wait_ge(lin_written, lins.next())
                dve.wait_ge(lo_done, lows.at())
                scale_at = POOL_SCALE_AT + POOL_GROUPS * layer + g
                dve.scalar_tensor_tensor(y_now[:], lin[:, (lins.n - 1) % 2, :], params[:, scale_at:scale_at + 1],
                                         pool_z[:], ALU.mult, ALU.mult).then_inc(lin_read, 1)
                reads.next()
                y_low(y_pool, g)

            def merge(f, u):
                for b in range(3):
                    evacuate(gates[:, u, b, :], rstd[:])
                for b in range(3):
                    dve.wait_ge(silu_done, silus.next())
                    dve.wait_ge(lin_written, lins.next())
                    out = merged[:, u, :] if b == 0 else part[:]
                    dve.tensor_tensor(out, lin[:, (lins.n - 1) % 2, :], gates[:, u, b, :], ALU.mult).then_inc(
                        lin_read, 1)
                    dve.wait_ge(lin_read, reads.next())
                    if b:
                        i = dve.tensor_tensor(merged[:, u, :], merged[:, u, :], part[:], ALU.add)
                        if b == 1:
                            do(i)
                            settle()
                        else:
                            i.then_inc(gated, 1)
                            dve.wait_ge(gated, gate_n.next())
                dve.wait_ge(hi_done, his.next())
                dve.tensor_tensor(sum_lo[:, bass.ds(f, 1), :], merged[:, u, :],
                                  sum_hi[:, bass.ds(f, 1), :].bitcast(F32), ALU.subtract).then_inc(lo_done, 1)
                lows.next()

            with Turns(dve, KD // 2, [(lins, 12), (reads, 12), (silus, 6), (gate_n, 2), (his, 2), (step, 2),
                                             (lows, 2)]) as i:
                for u in range(2):
                    merge(2 * i + u, u)
            names = [(f"norm{layer + 1}", h_hi, h_lo)] if layer + 1 < LAYERS else [(None, None, None)]
            for f in range(KD):
                dve.wait_ge(lin_written, lins.next())
                dve.tensor_tensor(x[:, f, :], x[:, f, :], lin[:, (lins.n - 1) % 2, :], ALU.add).then_inc(lin_read, 1)
                dve.wait_ge(lin_read, reads.next())
                if f:
                    finish(names, f - 1)
            finish(names, KD - 1)
            dve.wait_ge(rstd_done, rs.next())
            outr.n += 1

        gate_n = Tally()
        turns_at = 1 + 5 * A_PAIRS + 7 * A_PAIRS
        per_layer = 1 + H_TILES + 6 * H_TILES + H_TILES + QT * H_TILES // 2
        iw_turned = [turns_at + 1 + per_layer * layer for layer in range(LAYERS)]
        for layer in range(LAYERS):
            two_layer(layer)
        for f in range(KD):
            dve.scalar_tensor_tensor(result[:, f, :], x[:, f, :], gain("final", f), rstd[:], ALU.mult,
                                     ALU.mult).then_inc(x_ready, 1)

    block.__exit__(None, None, None)


def layout(inputs):
    def tiles(w):
        k, n = w.shape
        return w.reshape(k // P, P, n // P, P).transpose(2, 0, 1, 3)

    def blocks(t, shares=(BLOCK_TILES,)):
        full = np.zeros((t.shape[0], len(shares), P, BLOCK_TILES, P), t.dtype)
        for n, share in enumerate(shares):
            at = sum(shares[:n])
            full[:, n, :, :share] = t[:, at:at + share].transpose(0, 2, 1, 3)
        return full.reshape(-1, P, BLOCK_TILES * P)

    def woven(*parts):
        return np.stack(parts, axis=1).reshape(-1, *parts[0].shape[1:])

    def first_grouped(t, n):
        return [blocks(t[:n].swapaxes(0, 1).reshape(n, KD, P, P)), blocks(t[n:])]

    def ffn(layer):
        both = tiles(inputs["ffn_w_gate_up"][layer])
        return first_grouped(woven(both[:FF_TILES], both[FF_TILES:]), 4) + [blocks(tiles(inputs["ffn_w_down"][layer]), DOWN_SHARES)]

    qkv = tiles(inputs["a_w_qkv"][0])
    kv = tiles(inputs["kv_w"])
    stream = first_grouped(woven(qkv[0:8], qkv[8:16], qkv[16:24]), 3) + [blocks(tiles(inputs["a_w_o"][0]))] + ffn(0)
    stream += first_grouped(woven(tiles(inputs["b_w_q"][0]), kv[0:8], kv[8:16]), 3)
    stream += [blocks(tiles(inputs["b_w_o"][0]))] + ffn(1)
    edges = np.cumsum([512, 512, 512, 512, 512, 512, 512, 64, 8, 512, 512])
    for n in range(LAYERS):
        pool_u, pool_z, q, k, v, z, iq, ik, iw, mq, mz, gates = np.split(inputs["w_in_2"][n], edges, axis=1)
        iw = np.concatenate([iw, np.zeros((D, P - iw.shape[1]), iw.dtype)], axis=1)
        single = [np.concatenate([ik, ik], axis=1), iw, q, k, v, z]
        stream += [first_grouped(tiles(iq), H_TILES)[0]] + [blocks(tiles(w)) for w in single]
        stream += [blocks(tiles(mq))]
        mem_kv = tiles(inputs["w_mem_kv_2"][n])
        kinds = {"z": tiles(mz), "k": mem_kv[:H_TILES], "v": mem_kv[H_TILES:]}
        stream += [blocks(np.stack([kinds[kind][f] for kind, f in MEM_ORDER]))]
        stream += [blocks(woven(tiles(pool_u), tiles(pool_z)))]
        gate_tiles = tiles(gates).reshape(3, KD, KD, P, P)
        branch_tiles = [tiles(inputs["w_branch_2"][n, b]) for b in range(3)]
        stream += [blocks(np.concatenate([*gate_tiles, *branch_tiles], axis=1), MERGE_SHARES)]
        stream += [blocks(tiles(inputs["w_out_2"][n]))]
    weights = np.concatenate(stream)
    gains = {"kv": inputs["kv_norm_g"], "final": inputs["final_g_2"]}
    for n in range(2):
        gains |= {f"{k}{n}": inputs[f"{k}_g"][n] for k in ("mix_pre", "mix_post", "ffn_pre", "ffn_post")}
        gains |= {f"norm{n}": inputs["norm_g_2"][n], f"mem_norm{n}": inputs["mem_norm_g_2"][n]}
    params = np.zeros((P, N_PARAMS), np.float32)
    for name, at in GAIN_AT.items():
        params[:, at:at + KD] = gains[name].reshape(KD, P).T
    for n in range(2):
        params[:, POOL_SCALE_AT + 4 * n:POOL_SCALE_AT + 4 * n + 4] = inputs["pool_scale_2"][n].reshape(4, P).T
    params[:, SUBLN_AT] = inputs["a_subln_g"][0]
    for n, name in enumerate(("a_lambda_q1", "a_lambda_q2", "a_lambda_k1", "a_lambda_k2")):
        params[:64, LAMBDA_AT + n] = inputs[name][0]
    x_t = inputs["x"][0].T.reshape(KD, P, SEQ)
    rel = np.concatenate([inputs["rel_bias_2"], rel_onehot()], axis=1)
    mem_t = inputs["mem_2"][0].T.reshape(KD, P, MEM)
    pool_w = inputs["pool_w_2"].transpose(0, 2, 1, 3)
    return {"x_t": x_t, "weights": weights, "params": params, "rel": rel, "mem_t": mem_t,
            "pool_w": pool_w} | shape_tables()


def rel_onehot():
    d = P - 1 - np.arange(REL_SPAN)
    n = np.abs(d)
    far = 8 + (np.log(np.maximum(n, 1).astype(np.float32) / np.float32(8)) / np.float32(math.log(1024 / 8))
               * np.float32(8)).astype(np.int32)
    bucket = np.where(d > 0, 16, 0) + np.where(n < 8, n, np.minimum(far, 15))
    return (bucket[None, :] == np.arange(32)[:, None]).astype(np.float32)


def shape_tables():
    t = np.zeros((P, N_TABLES), np.float32)
    t[:, IDENT_AT:IDENT_AT + P] = np.eye(P)
    for head in range(2):
        for d in range(8):
            t[64 * head + d + 8, ROT_AT + 64 * head + d] = -1
            t[64 * head + d, ROT_AT + 64 * head + d + 8] = 1
    q, k = np.arange(P)[:, None], np.arange(P)[None, :]
    t[:, CAUSAL_AT:CAUSAL_AT + P] = np.where(k <= q, 0, MASKED)
    t[:, STRICT_AT:STRICT_AT + P] = np.where(k < q, 0, MASKED)
    counts = np.zeros((P, POOL_GROUPS, POOL_EDGE), np.float32)
    for g in range(POOL_GROUPS):
        counts[:, g] = 1 / np.minimum(np.arange(POOL_EDGE) + 1, 2 ** (g + 1))
    freq = np.float32(500000.0) ** (-np.arange(0, 16, 2, dtype=np.float32) / np.float32(16))
    angle = np.arange(SEQ, dtype=np.float32)[:, None] * freq[None, :]
    rope = np.zeros((P, 2, SEQ), np.float32)
    rope[:, 0] = 1
    for start in (0, 8, 64, 72):
        rope[start:start + 8, 0] = np.cos(angle).T
        rope[start:start + 8, 1] = np.sin(angle).T
    return {"tables": t, "inverse_counts": counts, "rope": rope}


def kernel(**inputs):
    from concourse import bacc
    from concourse.bass_utils import run_bass_kernel_spmd

    arrays = {name: np.ascontiguousarray(a) for name, a in layout({k: np.asarray(v) for k, v in inputs.items()}).items()}
    nc = bacc.Bacc("TRN2", target_bir_lowering=False, num_devices=1)
    ap = {name: nc.dram_tensor(name, a.shape, mybir.dt.from_np(a.dtype), kind="ExternalInput").ap()
          for name, a in arrays.items()}
    ap["out_t"] = nc.dram_tensor("out_t", (KD, P, SEQ), F32, kind="ExternalOutput").ap()
    build(nc, ap)
    result = run_bass_kernel_spmd(nc, [arrays], core_ids=[0])
    return result.results[0]["out_t"].reshape(D, SEQ).T[None]
```

```python
import math

import numpy as np

import concourse.bass as bass
from concourse import mybir
from concourse.alu_op_type import AluOpType as ALU

F32 = mybir.dt.float32
F32R = mybir.dt.float32r
ACT = mybir.ActivationFunctionType
AX = mybir.AxisListType

P = 128
SEQ = 512
D = 1024
KD = D // P
QT = SEQ // P
D_FF = 2816
FF_TILES = D_FF // P
A_PAIRS = 8
NEG = -1e30
EPS = 1e-6
LAMBDA_INIT = 0.8 - 0.6 * math.exp(-0.3 * 0)
BLOCK_TILES = 8
DOWN_SHARES = (7, 7, 8)
MERGE_SHARES = (7, 7, 7, 7, 8)
RAW_SLOTS = 4
W_SLOTS = 2
X_PARTS = 4

GAINS = ["mix_pre0", "mix_post0", "ffn_pre0", "ffn_post0", "kv", "mix_pre1", "mix_post1", "ffn_pre1", "ffn_post1",
         "norm0", "norm1", "mem_norm0", "mem_norm1", "final"]
GAIN_AT = {name: KD * n for n, name in enumerate(GAINS)}
POOL_SCALE_AT = KD * len(GAINS)
SUBLN_AT = POOL_SCALE_AT + 2 * 4
LAMBDA_AT = SUBLN_AT + 1
N_PARAMS = LAMBDA_AT + 4

IDENT_AT, ROT_AT, CAUSAL_AT, STRICT_AT = 0, P, 2 * P, 3 * P
N_TABLES = 4 * P
MASKED = -2.0 ** 100
POOL_EDGE = 16
POOL_GROUPS = 4

LAYERS = 2
H_TILES = 4
IDX_PAIRS = 4
TOPK = 128
CHUNK = 64
MEM = 256
MEM_CHUNKS = MEM // P
TAKEN = -3e38
IDX_SCALE = 64 ** -0.5 * 8 ** -0.5
MEM_SCALE = 128 ** -0.5
MEM_LAG = 2
SPARSE_ORDER = (3, 0, 2, 1)
SPARSE_PIECES = (0, 5, 6, 7, 8)
MEM_ORDER = [("z", 0), ("z", 1), ("k", 0), ("k", 1), ("z", 2), ("k", 2), ("k", 3), ("z", 3)] + [
    ("v", f) for f in range(4)]
REL_SPAN = SEQ + P
N_REL_HEADS = 8


class Tally:

    def __init__(self, n=0):
        self.n, self.turn, self.per = n, None, 0

    def at(self, ahead=0):
        if self.turn is None:
            return self.n + ahead
        return self.turn * self.per + (self.n + ahead)

    def next(self):
        self.n += 1
        return self.at()


class Turns:

    def __init__(self, eng, n, grow):
        self.eng, self.n, self.grow = eng, n, grow

    def __enter__(self):
        self.loop = self.eng.Fori(0, self.n)
        i = self.loop.__enter__()
        self.start = [(t, t.n) for t, _ in self.grow]
        for t, per in self.grow:
            t.turn, t.per = i, per
        return i

    def __exit__(self, *error):
        self.loop.__exit__(*error)
        if error[0] is None:
            grown = [t.n - n for t, n in self.start]
            assert grown == [per for _, per in self.grow], (grown, [per for _, per in self.grow])
            for (t, n), (_, per) in zip(self.start, self.grow):
                t.n, t.turn = n + per * self.n, None


def build(nc, ap):
    w_stream, n_blocks = ap["weights"], ap["weights"].shape[0]
    place = {"at": 16512}

    def region(start):
        place["at"] = start

    def sb(name, shape, dt=F32):
        size = 4 * int(np.prod(shape[1:]))
        t = nc.alloc_sbuf_tensor_at(name, shape, dt, offset=place["at"])
        place["at"] += size + (-size) % 32
        return t

    x = sb("x", [P, KD, SEQ])
    h_hi, h_lo = sb("h_hi", [P, KD, SEQ], F32R), sb("h_lo", [P, KD, SEQ], F32R)
    raw = sb("raw", [P, RAW_SLOTS, BLOCK_TILES * P])
    w_hi, w_lo = (sb(n, [P, W_SLOTS, BLOCK_TILES, P], F32R) for n in ("w_hi", "w_lo"))
    params = sb("params", [P, N_PARAMS])
    tables = sb("tables", [P, N_TABLES], F32R)
    inverse_counts = sb("inverse_counts", [P, POOL_GROUPS, POOL_EDGE])
    ones = sb("ones", [P, P])
    eps = sb("eps", [P, 1])
    rstd, rstd_m = sb("rstd", [P, SEQ]), sb("rstd_m", [P, SEQ])
    negmax, rowsum, rinv = sb("negmax", [P, 2, 2]), sb("rowsum", [P, 2, 2]), sb("rinv", [P, 2])
    lam_prod, lam_exp, neg_lam = sb("lam_prod", [64, 2]), sb("lam_exp", [P, 2]), sb("neg_lam", [P, 1])
    sub_gain = sb("sub_gain", [P, 1])
    ident_r, causal_r, strict_r = (tables[:, at:at + P] for at in (IDENT_AT, CAUSAL_AT, STRICT_AT))
    squares = sb("squares", [P, 2, SEQ])
    sum_at = place["at"]
    square_sum = sb("square_sum", [P, SEQ])
    region(sum_at)
    o_raw = sb("o_raw", [P, SEQ])
    stage_at = place["at"]

    plain, rot_sin = sb("plain", [P, 2, SEQ]), sb("rot_sin", [P, SEQ])
    o_sq, o_rstd = sb("o_sq", [P, SEQ]), sb("o_rstd", [P, SEQ])
    rope = sb("rope", [P, 2, SEQ])
    rel = sb("rel", [32, N_REL_HEADS + REL_SPAN])
    rel_rows = sb("rel_rows", [N_REL_HEADS, REL_SPAN])
    region(stage_at)
    g_hi, g_lo = sb("g_hi", [P, KD, SEQ], F32R), sb("g_lo", [P, KD, SEQ], F32R)
    q_now, k_now = sb("q_now", [P, 2, SEQ]), sb("k_now", [P, 2, SEQ])
    v_t = sb("v_t", [P, SEQ])
    v_now = sb("v_now", [P, 2, QT, P])
    probs = sb("probs", [P, 2, 2, SEQ])
    a_t = sb("a_t", [P, 2, QT, SEQ])
    pair_w = [sb(f"pair_w{t}", [P, 2, P * (t + 1)]) for t in range(QT)]
    softplus = squares
    o_hi, o_lo = sb("o_hi", [P, KD, SEQ], F32R), sb("o_lo", [P, KD, SEQ], F32R)
    assert place["at"] <= nc.sbuf_usable_end
    region(stage_at)
    m_attn = sb("m_attn", [P, KD, SEQ])
    region(stage_at)
    act_hi, act_lo = sb("act_hi", [P, FF_TILES, SEQ], F32R), sb("act_lo", [P, FF_TILES, SEQ], F32R)
    m_ffn = sb("m_ffn", [P, KD, SEQ])
    gate_s, up_s = sb("gate_s", [P, 2, SEQ]), sb("up_s", [P, 2, SEQ])
    region(stage_at)
    bias = sb("bias", [P, N_REL_HEADS, SEQ])
    y_attn = sb("y_attn_hi", [P, H_TILES, SEQ], F32R), sb("y_attn_lo", [P, H_TILES, SEQ], F32R)
    work_at = place["at"]
    aq, ak = sb("aq", [P, H_TILES, SEQ]), sb("ak", [P, H_TILES, SEQ])
    av = sb("av", [P, QT, H_TILES * P])
    iq, ik = sb("iq", [P, H_TILES, SEQ]), sb("ik", [P, SEQ])
    turn_in = sb("turn_in", [P, SEQ])
    chosen = sb("chosen", [P, QT, SEQ])
    az = sb("az", [P, H_TILES, SEQ])
    iw = sb("iw", [P, QT, 8])
    sparse_w = [None] * QT
    sparse_w[1] = sb("sparse_w1", [P, 2, 2 * P])
    assert place["at"] <= work_at + 56 * 1024
    region(work_at + 56 * 1024)
    for t in (3, 2, 0):
        sparse_w[t] = sb(f"sparse_w{t}", [P, 2, P * (t + 1)])
    a2_at = place["at"]
    a2_t = sb("a2_t", [P, 2, QT, SEQ])
    y_now = sb("y_now", [P, SEQ])
    top8 = sb("top8", [P, 8])
    v_turn_in = turn_in, y_now
    end_d = place["at"]
    region(a2_at)
    relu_s = sb("relu_s", [P, 2, 2, SEQ])
    index = [None] + [sb(f"index{t}", [P, P * (t + 1)]) for t in (1, 2, 3)]
    region(work_at)
    y_mem = sb("y_mem_hi", [P, H_TILES, SEQ], F32R), sb("y_mem_lo", [P, H_TILES, SEQ], F32R)
    mem_hi = sb("mem_hi", [P, KD, MEM], F32R)
    mq = sb("mq", [P, H_TILES, SEQ])
    mem_lo = sb("mem_lo", [P, KD, MEM], F32R)
    mem = sb("mem", [P, KD, MEM])
    mk, mv = sb("mk", [P, H_TILES, MEM]), sb("mv", [P, MEM_CHUNKS, H_TILES * P])
    assert place["at"] <= work_at + 56 * 1024
    region(work_at + 56 * 1024)
    mem_w = sb("mem_w", [P, QT, 2, MEM])
    mem_v_t = [mem_w[:, k, 0, :] for k in range(2)]
    mem_a = sb("mem_a", [P, 2, MEM_CHUNKS, SEQ])
    mz = sb("mz", [P, H_TILES, SEQ])
    region(work_at + 16384)
    y_pool = sb("y_pool_hi", [P, H_TILES, SEQ], F32R), sb("y_pool_lo", [P, H_TILES, SEQ], F32R)
    pool_w = sb("pool_w", [P, POOL_GROUPS, P])
    pool_u, pool_a, pool_b = (sb(n, [P, POOL_EDGE + SEQ]) for n in ("pool_u", "pool_a", "pool_b"))
    pooled, pool_z = sb("pooled", [P, SEQ]), sb("pool_z", [P, SEQ])
    edge = sb("edge", [P, POOL_EDGE])
    region(work_at + 32768)
    sum_hi, sum_lo = sb("sum_hi", [P, KD, SEQ], F32R), sb("sum_lo", [P, KD, SEQ], F32R)
    gates, merged = sb("gates", [P, 2, 3, SEQ]), sb("merged", [P, 2, SEQ])
    part = sb("part", [P, SEQ])
    end_m = place["at"]
    assert max(end_d, end_m) <= nc.sbuf_usable_end, (end_d, end_m)
    region(work_at)
    result = sb("result", [P, KD, SEQ])

    lin = nc.alloc_psum_tensor("lin", [P, 2, SEQ], F32)
    score = nc.alloc_psum_tensor("score", [P, 2, 2, SEQ], F32)
    turn = nc.alloc_psum_tensor("turn", [P, SEQ], F32)
    outp = nc.alloc_psum_tensor("outp", [P, SEQ], F32)

    SPARE = [score[:, slot, e, :] for slot in range(2) for e in range(2)]

    ident = ident_r.bitcast(F32)
    rot = tables[:, ROT_AT:ROT_AT + P].bitcast(F32)
    cos, sin = rope[:, 0, :], rope[:, 1, :]

    def gain(name, f):
        return params[:, GAIN_AT[name] + f:GAIN_AT[name] + f + 1]

    def sem(name):
        return nc.alloc_semaphore(name)

    raw_loaded = [sem(f"raw_loaded{i}") for i in range(RAW_SLOTS)]
    hi_split, w_split, hi_used, lo_used = sem("hi_split"), sem("w_split"), sem("hi_used"), sem("lo_used")
    x_loaded = [sem(f"x_loaded{n}") for n in range(X_PARTS)]
    params_loaded, tables_loaded, out_stored = sem("params_loaded"), sem("tables_loaded"), sem("out_stored")
    const_done, lam_ready, lam_summed, lam_done = (
        sem(n) for n in ("const_done", "lam_ready", "lam_summed", "lam_done"))
    rel_written, rel_copied, rel_stored, bias_loaded = (
        sem(n) for n in ("rel_written", "rel_copied", "rel_stored", "bias_loaded"))
    lin_written, lin_read = sem("lin_written"), sem("lin_read")
    score_written, score_copied = sem("score_written"), sem("score_copied")
    turn_written, turn_read = sem("turn_written"), sem("turn_read")
    out_written, out_read = sem("out_written"), sem("out_read")
    x_ready, h_ready, square_done, sum_added, rstd_done = (
        sem(n) for n in ("x_ready", "h_ready", "square_done", "sum_added", "rstd_done"))
    hi_done, lo_done = sem("hi_done"), sem("lo_done")
    negmax_done, exp_done, mixed = sem("negmax_done"), sem("exp_done"), sem("mixed")
    qk_ready, sub_rstd, sub_scaled = sem("qk_ready"), sem("sub_rstd"), sem("sub_scaled")
    logs_done, sticks_done, weights_done = sem("logs_done"), sem("sticks_done"), sem("weights_done")
    silu_done, act_ready, y_ready, gated = (sem(n) for n in ("silu_done", "act_ready", "y_ready", "gated"))
    relu_done, index_done, biased, mem_exp = (sem(n) for n in ("relu_done", "index_done", "biased", "mem_exp"))
    mem_loaded, pool_loaded, pool_ready = sem("mem_loaded"), sem("pool_loaded"), sem("pool_ready")
    v_step, a_step = sem("v_step"), sem("a_step")

    rel_tensor = nc.dram_tensor("rel_rows_dram", [N_REL_HEADS, REL_SPAN], F32)
    rel_dram = rel_tensor.ap()
    toeplitz = bass.AP(tensor=rel_dram.tensor, offset=0, ap=[[1, P], [REL_SPAN, N_REL_HEADS], [1, SEQ]])

    block = nc.Block()
    block.__enter__()

    @block.sync
    def _(sp):
        def load(b, slot):
            sp.dma_start(raw[:, slot, :], w_stream[bass.ds(b, 1)].rearrange("a p n -> (a p) n")).then_inc(
                raw_loaded[slot], 16)

        sp.dma_start(params[:], ap["params"]).then_inc(params_loaded, 16)
        per = KD // X_PARTS
        for n in range(X_PARTS):
            load(n, n)
            part = slice(n * per, (n + 1) * per)
            sp.dma_start(x[:, part, :], ap["x_t"][part].rearrange("c p n -> p c n")).then_inc(x_loaded[n], 16)

        def reload(i, slot):
            sp.wait_ge(w_split, RAW_SLOTS * i + (slot - RAW_SLOTS + 1))
            load(RAW_SLOTS * i + slot, slot)

        with sp.Fori(1, n_blocks // RAW_SLOTS) as i:
            for slot in range(RAW_SLOTS):
                reload(i, slot)
        for slot in range(n_blocks % RAW_SLOTS):
            reload(n_blocks // RAW_SLOTS, slot)
        for f in range(KD):
            sp.wait_ge(x_ready, KD * 4 + f + 1)
            sp.dma_start(ap["out_t"][f], result[:, f, :]).then_inc(out_stored, 16)
        sp.wait_ge(out_stored, 16 * KD)

    @block.gpsimd
    def _(pool):
        one = ones[:, 0:1].broadcast_to([P, BLOCK_TILES * P])
        pool.wait_ge(const_done, 1)

        def split(i, slot):
            pool.wait_ge(raw_loaded[slot], 16 * i + 16)
            pool.wait_ge(hi_used, RAW_SLOTS * i + (slot + 1))
            hi = w_hi[:, slot % W_SLOTS].rearrange("p c n -> p (c n)")
            lo = w_lo[:, slot % W_SLOTS].rearrange("p c n -> p (c n)")
            pool.tensor_tensor(hi, raw[:, slot, :], one, ALU.mult).then_inc(hi_split, 1)
            pool.wait_ge(hi_split, RAW_SLOTS * i + (slot + 1))
            pool.wait_ge(lo_used, RAW_SLOTS * i + (slot + 1))
            pool.tensor_tensor(lo, raw[:, slot, :], hi.bitcast(F32), ALU.subtract).then_inc(w_split, 1)

        with pool.Fori(0, n_blocks // RAW_SLOTS) as i:
            for slot in range(RAW_SLOTS):
                split(i, slot)
        for slot in range(n_blocks % RAW_SLOTS):
            split(n_blocks // RAW_SLOTS, slot)

    @block.tensor
    def _(pe):
        blocks, tiles = Tally(), Tally()
        scores_free, probs_in, turns_done, outs = Tally(), Tally(), Tally(), Tally()
        pe.sem_inc(hi_used, W_SLOTS)
        pe.sem_inc(lo_used, W_SLOTS - 1)
        pe.wait_ge(const_done, 2)

        def passes(out, slot, tile, hi, lo, first, last, block_first, block_last):
            mm = pe.matmul(out, w_hi[:, slot, tile, :], hi, start=first, stop=False)
            if block_first:
                mm.then_inc(lo_used, 1)
            mm = pe.matmul(out, w_hi[:, slot, tile, :], lo, start=False, stop=False)
            if block_last:
                mm.then_inc(hi_used, 1)
            return pe.matmul(out, w_lo[:, slot, tile, :], hi, start=False, stop=last)

        stream = {"taken": BLOCK_TILES, "of": BLOCK_TILES, "shares": (BLOCK_TILES,), "turn": 0}

        def shares(pattern):
            assert stream["taken"] == stream["of"]
            stream["shares"], stream["turn"] = pattern, 0

        def next_tile():
            first = stream["taken"] == stream["of"]
            if first:
                stream["of"] = stream["shares"][stream["turn"] % len(stream["shares"])]
                stream["turn"] += 1
                stream["taken"] = 0
                pe.wait_ge(w_split, blocks.next())
            stream["taken"] += 1
            return (blocks.n - 1) % W_SLOTS, stream["taken"] - 1, first, stream["taken"] == stream["of"]

        def linear(hi, lo, chunks, ready=None, width=SEQ, piece=None, spare=None, late=0,
                   lows=None):
            first, end = piece or (0, chunks)
            if first == 0 and spare is None:
                pe.wait_ge(lin_read, tiles.at(1 - late))
            out = lin[:, tiles.n % 2, 0:width] if spare is None else spare
            for c in range(first, end):
                slot, tile, *edges = next_tile()
                if ready is not None:
                    pe.wait_ge(h_ready, h_base["n"] + ready * (c + 1))
                if lows is not None:
                    pe.wait_ge(lo_done, lows + c + 1)
                mm = passes(out, slot, tile, hi[:, c, :], lo[:, c, :], c == 0, c == chunks - 1,
                            *edges)
            if end == chunks:
                mm.then_inc(lin_written, 1)
                tiles.next()

        def rotate(which):
            pe.wait_ge(lin_read, tiles.at(1))
            bank = tiles.n % 2
            pe.matmul(lin[:, bank, :], rot, plain[:, which, :], start=True, stop=True).then_inc(lin_written, 1)
            tiles.next()

        def turn_v(parity):
            pe.wait_ge(lin_read, tiles.at(2))
            pe.wait_ge(turn_read, turns_done.at(1))
            for t in range(QT):
                mm = pe.transpose(turn[:, t * P:(t + 1) * P], v_t[:, t * P:(t + 1) * P], ident)
            mm.then_inc(turn_written, 1)
            turns_done.next()

        def scores(parity, t, free, mask):
            n = P * (t + 1)
            pe.wait_ge(free, scores_free.at(1))
            for e in range(2):
                half = slice(64 * e, 64 * e + 64)
                out = score[:, scores_free.n % 2, e, 0:n]
                pe.matmul(out, q_now[half, parity, t * P:(t + 1) * P], k_now[half, parity, 0:n], start=True,
                          stop=True)
                mm = pe.matmul(out[:, n - P:n], ident_r, mask, start=False, stop=True,
                               skip_group_check=True)
            mm.then_inc(score_written, 1)
            scores_free.next()

        def turn_probs(t):
            pe.wait_ge(mixed, probs_in.next())
            pe.wait_ge(turn_read, turns_done.at(1))
            for c in range(t + 1):
                mm = pe.transpose(turn[:, c * P:(c + 1) * P], pair_w[t][:, 0, c * P:(c + 1) * P], ident)
            mm.then_inc(turn_written, 1)
            turns_done.next()

        qk = Tally()

        def a_period(parity, prev=True, cur=True, nxt=True, fill=False):
            other = 1 - parity
            if nxt:
                linear(h_hi, h_lo, KD, piece=(0, 2))
            if cur:
                qk.n += 2
                pe.wait_ge(qk_ready, qk.at())
                scores(parity, 3, exp_done, causal_r)
            if prev:
                turn_probs(1)
            if nxt:
                linear(h_hi, h_lo, KD, piece=(2, 5))
            if fill:
                project_chunk(2)
            if cur:
                turn_v(parity)
            if prev:
                a_values(other, 3)
            if nxt:
                linear(h_hi, h_lo, KD, piece=(5, 8))
            if prev:
                a_values(other, 2)

            if cur:
                scores(parity, 2, exp_done, causal_r)
            if prev:
                turn_probs(0)
            if nxt:
                linear(h_hi, h_lo, KD)
            if fill and cur:
                project_chunk(2)
            if prev:
                a_values(other, 1)

            if cur:
                scores(parity, 1, exp_done, causal_r)
            if nxt:
                rotate(0)
            if cur:
                turn_probs(3)
            elif prev:
                pe.wait_ge(turn_read, turns_done.at(1))
            if nxt:
                linear(h_hi, h_lo, KD, piece=(0, 5))
            if prev:
                a_values(other, 0)
            if nxt:
                linear(h_hi, h_lo, KD, piece=(5, 8))
            if fill and cur:
                project_chunk(2)

            if cur:
                scores(parity, 0, exp_done, causal_r)
            if nxt:
                rotate(1)
            if cur:
                turn_probs(2)
            if prev:
                pe.wait_ge(out_read, outs.at(1))
                pe.matmul(outp[:], ones[:], o_sq[:], start=True, stop=True).then_inc(out_written, 1)
                outs.next()

        def a_values(parity, t):
            if t == QT - 1:
                pe.wait_ge(out_read, outs.at(1))
            for c in range(t + 1):
                mm = pe.matmul(outp[:, t * P:(t + 1) * P], v_now[:, parity, c, :], a_t[:, 0, c, t * P:(t + 1) * P],
                               start=(c == 0), stop=(c == t), skip_group_check=True)
            if t == 0:
                mm.then_inc(out_written, 1)
                outs.next()

        def b_values(parity, t):
            if t == QT - 1:
                pe.wait_ge(out_read, outs.at(1))
            for e in range(2):
                half = slice(64 * e, 64 * e + 64)
                for c in range(t + 1):
                    mm = pe.matmul(outp[half, t * P:(t + 1) * P], v_now[:, parity, c, half],
                                   a_t[:, e, c, t * P:(t + 1) * P], start=(c == 0), stop=(c == t),
                                   skip_group_check=True)
            if t == 0:
                mm.then_inc(out_written, 1)
                outs.next()

        projected = Tally()

        def project_chunk(count):
            for _ in range(count):
                c = projected.n
                pe.wait_ge(lo_done, lo_base["n"] + c + 1)
                if c == 0:
                    pe.wait_ge(lin_read, tiles.at(2))
                for out in (lin[:, 0, :], lin[:, 1, :]):
                    slot, tile, *edges = next_tile()
                    mm = passes(out, slot, tile, o_hi[:, c, :], o_lo[:, c, :], c == 0, c == KD - 1, *edges)
                    if c == KD - 1:
                        mm.then_inc(lin_written, 1)
                projected.next()

        def turn_sticks(t, e=None):
            pe.wait_ge(turn_read, turns_done.at(1))
            heads = (0, 1) if e is None else (e,)
            for n, head in enumerate(heads):
                for c in range(t + 1):
                    at = (n * (t + 1) + c) * P
                    mm = pe.transpose(turn[:, at:at + P], pair_w[t][:, head, c * P:(c + 1) * P], ident)
            mm.then_inc(turn_written, 1)
            turns_done.next()

        def b_period(parity, prev=True, cur=True, nxt=True, fill=False):
            other = 1 - parity
            if cur:
                pe.wait_ge(lin_read, tiles.at(1))
                scores(parity, 3, score_copied, strict_r)
            if prev:
                pe.wait_ge(weights_done, probs_in.next())
                turn_sticks(1)
            if nxt:
                linear(h_hi, h_lo, KD, piece=(0, 4))
            if fill:
                project_chunk(2)
            if prev:
                b_values(other, 3)
            if cur:
                turn_v(parity)
            if nxt:
                linear(h_hi, h_lo, KD, piece=(4, 8))

            if cur:
                scores(parity, 2, score_copied, strict_r)
            if prev:
                pe.wait_ge(weights_done, probs_in.next())
                turn_sticks(0)
            if nxt:
                linear(g_hi, g_lo, KD, piece=(0, 4))
            if prev:
                b_values(other, 2)
            if nxt:
                linear(g_hi, g_lo, KD, piece=(4, 8))
            if fill and cur:
                project_chunk(2)

            if cur:
                scores(parity, 1, score_copied, strict_r)
            if cur:
                pe.wait_ge(weights_done, probs_in.next())
                turn_sticks(3, 0)
            if prev:
                b_values(other, 1)
            if nxt:
                linear(g_hi, g_lo, KD, piece=(0, 3))
            if fill and cur:
                project_chunk(1)
            if cur:
                turn_sticks(3, 1)
            elif prev:
                pe.wait_ge(turn_read, turns_done.at(1))
            if prev:
                b_values(other, 0)

            if cur:
                scores(parity, 0, score_copied, strict_r)
            if nxt:
                linear(g_hi, g_lo, KD, piece=(3, 6))
            if cur:
                pe.wait_ge(weights_done, probs_in.next())
                turn_sticks(2, 0)
            if nxt:
                linear(g_hi, g_lo, KD, piece=(6, 7))
            if fill and cur:
                project_chunk(1)
            if cur:
                turn_sticks(2, 1)
            if nxt:
                linear(g_hi, g_lo, KD, piece=(7, 8))

        h_base, sums = {"n": 0}, Tally(2)

        def first_tiles(sources, spares, copies=1):
            pe.wait_ge(lin_read, tiles.at(2))
            banks = [lin[:, 0, :], lin[:, 1, :]] + spares
            assert tiles.n % 2 == 0
            for c in range(KD):
                pe.wait_ge(h_ready, h_base["n"] + copies * (c + 1))
                for (hi, lo), out in zip(sources, banks):
                    slot, tile, *edges = next_tile()
                    mm = passes(out, slot, tile, hi[:, c, :], lo[:, c, :], c == 0, c == KD - 1, *edges)
                    if c == KD - 1:
                        mm.then_inc(lin_written, 1)
            tiles.n += len(sources)
            h_base["n"] += copies * KD
            norm_stats()

        def norm_stats(width=SEQ):
            sums.n += KD
            pe.wait_ge(sum_added, sums.at())
            pe.wait_ge(out_read, outs.at(1))
            pe.matmul(outp[:, 0:width], ones[:], square_sum[:, 0:width], start=True, stop=True).then_inc(
                out_written, 1)
            outs.next()

        def ffn():
            def both():
                linear(h_hi, h_lo, KD)
                linear(h_hi, h_lo, KD)

            first_tiles([(h_hi, h_lo)] * 4, SPARE[0:2])
            linear(h_hi, h_lo, KD, spare=SPARE[2])
            linear(h_hi, h_lo, KD, spare=SPARE[3])
            linear(h_hi, h_lo, KD, late=4)
            linear(h_hi, h_lo, KD, late=4)
            with Turns(pe, FF_TILES // 2 - 2, [(blocks, 4), (tiles, 4)]) as i:
                for u in range(2):
                    both()
            shares(DOWN_SHARES)
            linear(act_hi, act_lo, FF_TILES, lows=lo_base["n"])
            lo_base["n"] += FF_TILES
            linear(act_hi, act_lo, FF_TILES)
            with Turns(pe, KD // 2 - 1, [(blocks, 6), (tiles, 2)]):
                for u in range(2):
                    linear(act_hi, act_lo, FF_TILES)
            shares((BLOCK_TILES,))

        lo_base = {"n": 0}

        def project_out():
            project_chunk(KD - projected.n)
            projected.n = 0
            tiles.n += 2
            lo_base["n"] += KD
            with Turns(pe, KD // 2 - 1, [(blocks, 2), (tiles, 2)]):
                for u in range(2):
                    linear(o_hi, o_lo, KD)

        first_tiles([(h_hi, h_lo)] * 3, SPARE[3:])
        pe.wait_ge(tables_loaded, 64)
        for half in range(2):
            mm = pe.matmul(score[0:N_REL_HEADS, 0, half, 0:REL_SPAN // 2], rel[:, 0:N_REL_HEADS],
                           rel[:, N_REL_HEADS + half * (REL_SPAN // 2):N_REL_HEADS + (half + 1) * (REL_SPAN // 2)],
                           start=True, stop=True)
        mm.then_inc(rel_written, 1)
        pe.wait_ge(lam_ready, 1)
        pe.matmul(score[:, 1, 0, 0:2], ones[0:64, :], lam_prod[:], start=True, stop=True).then_inc(lam_summed, 1)
        pe.wait_ge(const_done, 3)
        rotate(0)
        rotate(1)
        pe.wait_ge(rel_copied, 1)
        pe.wait_ge(lam_done, 1)
        a_period(0, False, True, True)
        with Turns(pe, 3, [(blocks, 6), (tiles, 10), (scores_free, 8), (probs_in, 8), (turns_done, 10), (outs, 4),
                           (qk, 4)]):
            a_period(1)
            a_period(0)
        a_period(1, True, True, False, True)
        a_period(0, True, False, False)
        project_out()
        norm_stats()
        ffn()
        norm_stats()
        scores_free.n = probs_in.n = 0
        pe.wait_ge(exp_done, 2 + QT * A_PAIRS)
        first_tiles([(h_hi, h_lo), (g_hi, g_lo), (g_hi, g_lo)], SPARE[3:], 2)
        b_period(0, False, True, True)
        with Turns(pe, 3, [(blocks, 6), (tiles, 6), (scores_free, 8), (probs_in, 8), (turns_done, 14), (outs, 2)]):
            b_period(1)
            b_period(0)
        b_period(1, True, True, False, True)
        b_period(0, True, False, False)
        project_out()
        norm_stats()
        ffn()
        norm_stats()

        relus, biases, mem_exps, mixes, ys = Tally(), Tally(), Tally(), Tally(QT * A_PAIRS), Tally(lo_base["n"])

        def turn_tile(source, chunks, later=0):
            pe.wait_ge(lin_read, tiles.at(2 - later))
            pe.wait_ge(turn_read, turns_done.at(1))
            for t in range(chunks):
                mm = pe.transpose(turn[:, t * P:(t + 1) * P], source[:, t * P:(t + 1) * P], ident)
            mm.then_inc(turn_written, 1)
            turns_done.next()

        def index_scores(t):
            n = P * (t + 1)
            for pair in range(IDX_PAIRS):
                pe.wait_ge(relu_done, relus.at(1))
                for e in range(2):
                    half = slice(64 * e, 64 * e + 64)
                    mm = pe.matmul(score[:, relus.n % 2, e, 0:n], iq[half, pair, t * P:(t + 1) * P], ik[half, 0:n],
                                   start=True, stop=True)
                mm.then_inc(score_written, 1)
                relus.next()

        def sparse_scores(pair, t):
            n = P * (t + 1)
            pe.wait_ge(biased, biases.at(1))
            for e in range(2):
                half = slice(64 * e, 64 * e + 64)
                mm = pe.matmul(score[:, biases.n % 2, e, 0:n], aq[half, pair, t * P:(t + 1) * P], ak[half, pair, 0:n],
                               start=True, stop=True)
            mm.then_inc(score_written, 1)
            biases.next()

        def turn_both(t, weights, chunks):
            pe.wait_ge(mixed, mixes.next())
            pe.wait_ge(turn_read, turns_done.at(1))
            for e in range(2):
                for c in range(chunks):
                    at = (chunks * e + c) * P
                    mm = pe.transpose(turn[:, at:at + P], weights[:, e, c * P:(c + 1) * P], ident)
            mm.then_inc(turn_written, 1)
            turns_done.next()

        def turn_one(t, e):
            if e == 0:
                pe.wait_ge(mixed, mixes.next())
            pe.wait_ge(turn_read, turns_done.at(1))
            for c in range(t + 1):
                mm = pe.transpose(turn[:, c * P:(c + 1) * P], sparse_w[t][:, e, c * P:(c + 1) * P], ident)
            mm.then_inc(turn_written, 1)
            turns_done.next()

        def sparse_values(pair, t):
            if t == SPARSE_ORDER[0]:
                pe.wait_ge(out_read, outs.at(1))
            for e in range(2):
                half = slice(64 * e, 64 * e + 64)
                for c in range(t + 1):
                    mm = pe.matmul(outp[half, t * P:(t + 1) * P], av[:, c, pair * P + 64 * e:pair * P + 64 * e + 64],
                                   a2_t[:, e, c, t * P:(t + 1) * P], start=(c == 0), stop=(c == t),
                                   skip_group_check=True)
            if t == SPARSE_ORDER[-1]:
                mm.then_inc(out_written, 1)
                outs.next()

        def mem_scores(pair, t):
            pe.wait_ge(mem_exp, mem_exps.at(1))
            for e in range(2):
                head = 2 * pair + e
                mm = pe.matmul(score[:, mem_exps.n % 2, e, 0:MEM], mq[:, head, t * P:(t + 1) * P], mk[:, head, :],
                               start=True, stop=True)
            mm.then_inc(score_written, 1)
            mem_exps.next()

        def mem_values(pair):
            pe.wait_ge(turn_read, turns_done.at(1))
            for e in range(2):
                pe.wait_ge(out_read, outs.at(1))
                for c in range(MEM_CHUNKS):
                    mm = pe.matmul(outp[:], mv[:, c, (2 * pair + e) * P:(2 * pair + e + 1) * P], mem_a[:, e, c, :],
                                   start=(c == 0), stop=(c == MEM_CHUNKS - 1))
                mm.then_inc(out_written, 1)
                outs.next()

        def two_layer():
            first_tiles([(h_hi, h_lo)] * H_TILES, SPARE[0:2])
            for spare in SPARE[2:]:
                linear(h_hi, h_lo, KD, spare=spare)
            turn_tile(ik, QT, 1)
            pe.wait_ge(lin_read, tiles.at(1))
            pe.matmul(lin[64:128, tiles.n % 2, :], ident[0:64, 0:64], ik[0:64, :], start=True,
                      stop=True).then_inc(lin_written, 1)
            tiles.next()
            linear(h_hi, h_lo, KD)
            pe.wait_ge(lin_read, tiles.at(1))
            for t in (3, 2, 1):
                index_scores(t)
                if t == 3:
                    for u in range(2, H_TILES):
                        linear(h_hi, h_lo, KD)
                elif t == 2:
                    with Turns(pe, H_TILES // 2, [(blocks, 2), (tiles, 2)]):
                        for u in range(2):
                            linear(h_hi, h_lo, KD)
                else:
                    for u in range(H_TILES):
                        linear(h_hi, h_lo, KD)
                        if u:
                            turn_tile(v_turn_in[(u - 1) % 2], QT, 1)
            linear(h_hi, h_lo, KD)
            turn_tile(v_turn_in[(H_TILES - 1) % 2], QT, 1)
            for u in range(1, H_TILES):
                linear(h_hi, h_lo, KD)
            pe.wait_ge(lin_read, tiles.at(1))
            pe.wait_ge(relu_done, relus.at(2))
            steps = [(pair, t) for pair in range(H_TILES) for t in SPARSE_ORDER]
            for n in range(len(steps) + 3):
                cur = n < len(steps)
                piece = SPARSE_PIECES[n % 4:n % 4 + 2]
                if cur:
                    sparse_scores(*steps[n])
                if 2 <= n < len(steps) + 2:
                    t = steps[n - 2][1]
                    if t > 1:
                        turn_one(t, 0)
                        if cur:
                            linear(h_hi, h_lo, KD, piece=piece)
                        turn_one(t, 1)
                    else:
                        turn_both(t, sparse_w[t], t + 1)
                        if cur:
                            linear(h_hi, h_lo, KD, piece=piece)
                elif cur:
                    linear(h_hi, h_lo, KD, piece=piece)
                else:
                    pe.wait_ge(turn_read, turns_done.at(1))
                if n >= 3:
                    sparse_values(*steps[n - 3])
            for n, (kind, f) in enumerate(MEM_ORDER):
                if kind == "z":
                    linear(h_hi, h_lo, KD)
                else:
                    first = (kind, f) == ("k", 0)
                    linear(mem_hi, mem_lo, KD, 1 if first else None, MEM)
                    if first:
                        h_base["n"] += KD
                        norm_stats(MEM)
                if kind == "v" and f:
                    turn_tile(mem_v_t[(f - 1) % 2], MEM_CHUNKS, 1)
            turn_tile(mem_v_t[(H_TILES - 1) % 2], MEM_CHUNKS)
            pe.wait_ge(biased, biases.at(2))
            steps = [(pair, t) for pair in range(H_TILES // 2) for t in (3, 2, 1, 0)]
            for n in range(len(steps) + MEM_LAG):
                if n < len(steps):
                    mem_scores(*steps[n])
                    linear(h_hi, h_lo, KD, piece=(2 * (n % 4), 2 * (n % 4) + 2))
                if n >= MEM_LAG:
                    pair, t = steps[n - MEM_LAG]
                    if pair and t == 3:
                        mem_values(pair - 1)
                    turn_both(t, mem_w[:, t], MEM_CHUNKS)
            mem_values(H_TILES // 2 - 1)
            pe.wait_ge(pool_loaded, pool_loads.next() * 16)
            for g in range(POOL_GROUPS):
                if g:
                    linear(h_hi, h_lo, KD)
                    linear(h_hi, h_lo, KD)
                pe.wait_ge(pool_ready, pools.next())
                pe.wait_ge(lin_read, tiles.at(1))
                pe.matmul(lin[:, tiles.n % 2, :], pool_w[:, g, :], pooled[:], start=True, stop=True).then_inc(
                    lin_written, 1)
                tiles.next()
            ys.n += 3 * H_TILES
            shares(MERGE_SHARES)
            with Turns(pe, KD // 2, [(blocks, 10), (tiles, 12)]):
                for u in range(2):
                    for b in range(3):
                        linear(h_hi, h_lo, KD)
                    if u == 0:
                        pe.wait_ge(lo_done, ys.at())
                    for y in (y_pool, y_attn, y_mem):
                        linear(*y, H_TILES)
            shares((BLOCK_TILES,))
            linear(sum_hi, sum_lo, KD, lows=ys.at())
            ys.n += KD
            linear(sum_hi, sum_lo, KD)
            with Turns(pe, KD // 2 - 1, [(blocks, 2), (tiles, 2)]):
                for u in range(2):
                    linear(sum_hi, sum_lo, KD)

        pools, pool_loads = Tally(), Tally()
        for layer in range(LAYERS):
            two_layer()
        norm_stats()

    @block.scalar
    def _(act):
        step = Tally()
        act.sem_inc(turn_read, 1)
        act.sem_inc(out_read, 1)
        act.sem_inc(exp_done, 2)
        turned, outs, negs, exps = Tally(), Tally(), Tally(), Tally()
        scored, sticks, subs, lins = Tally(), Tally(), Tally(), Tally()

        def then_wait(ins):
            ins.then_inc(a_step, 1)
            act.wait_ge(a_step, step.next())

        def soft_exp(t):
            n = P * (t + 1)
            act.wait_ge(negmax_done, negs.next())
            slot = (negs.n - 1) % 2
            for e in range(2):
                i = act.activation(pair_w[t][:, e, :], score[:, slot, e, 0:n], ACT.Exp,
                                   bias=negmax[:, slot, e:e + 1], accum_out=rowsum[:, slot, e:e + 1])
            i.then_inc(exp_done, 1)

        def keep_turned(t, e):
            act.wait_ge(turn_written, turned.next())
            act.activation(a_t[:, e, 0:t + 1, t * P:(t + 1) * P],
                           turn[:, 0:(t + 1) * P].rearrange("p (c n) -> p c n", n=P), ACT.Copy).then_inc(turn_read, 1)

        def keep_values(parity):
            act.wait_ge(turn_written, turned.next())
            act.activation(v_now[:, parity].rearrange("p c n -> p (c n)"), turn[:], ACT.Copy).then_inc(turn_read, 1)

        def to_rstd(out, width, signal, tally_out):
            act.wait_ge(out_written, tally_out.next())
            act.activation(out, outp[:, 0:out.shape[1]], ACT.Ln, bias=eps[:, 0:1], scale=1.0 / width).then_inc(out_read, 1)
            act.wait_ge(out_read, tally_out.at(1))
            act.activation(out, out, ACT.Exp, scale=-0.5).then_inc(signal, 1)

        def a_period(parity, pair, prev=True, cur=True, nxt=True):
            if prev:
                keep_turned(1, 0)
            if cur:
                soft_exp(3)
                keep_values(parity)

            if prev:
                keep_turned(0, 0)
            if cur:
                soft_exp(2)

            if cur:
                keep_turned(3, 0)
                soft_exp(1)
            if prev:
                act.wait_ge(out_written, outs.next())
                act.activation(o_raw[:], outp[:], ACT.Copy)
                act.activation(o_sq[:], outp[:], ACT.Square).then_inc(out_read, 1)

            if cur:
                soft_exp(0)
                keep_turned(2, 0)
            if prev:
                to_rstd(o_rstd[:], P, sub_rstd, outs)
                act.wait_ge(sub_scaled, subs.next())
                act.activation(o_hi[:, bass.ds(pair - 1, 1), :], o_sq[:], ACT.Copy,
                               scale=sub_gain[:, 0:1]).then_inc(hi_done, 1)

        def b_sizes(t):
            n = P * (t + 1)
            act.wait_ge(score_written, scored.next())
            slot = (scored.n - 1) % 2
            out = pair_w[t][:]
            act.activation(out, score[:, slot, :, 0:n], ACT.Abs)
            act.activation(probs[:, slot, :, 0:n], score[:, slot, :, 0:n], ACT.Copy).then_inc(score_copied, 1)

        def b_logs(t):
            out = pair_w[t][:]
            act.wait_ge(score_copied, copied.next())
            then_wait(act.activation(out, out, ACT.Exp, scale=-1.0))
            act.activation(out, out, ACT.Ln, bias=ones[:, 0:1]).then_inc(logs_done, 1)

        copied = Tally(2)
        b_lows = Tally(KD + FF_TILES)

        def b_weights(t):
            act.wait_ge(sticks_done, sticks.next())
            act.activation(pair_w[t][:], pair_w[t][:], ACT.Exp).then_inc(weights_done, 1)

        def keep_both(t):
            act.wait_ge(turn_written, turned.next())
            act.activation(a_t[:, :, 0:t + 1, t * P:(t + 1) * P],
                           turn[:, 0:2 * (t + 1) * P].rearrange("p (e c n) -> p e c n", e=2, n=P),
                           ACT.Copy).then_inc(turn_read, 1)

        def b_period(parity, pair, prev=True, cur=True, nxt=True):
            if cur:
                b_sizes(3)
            if prev:
                keep_both(1)
            if cur:
                b_logs(3)
            if prev:
                b_weights(0)
            if cur:
                keep_values(parity)

            if cur:
                b_sizes(2)
            if prev:
                keep_both(0)
            if cur:
                b_logs(2)
                b_weights(3)

            if cur:
                b_sizes(1)
                keep_turned(3, 0)
                b_logs(1)
                keep_turned(3, 1)
                b_weights(2)

            if cur:
                b_sizes(0)
                keep_turned(2, 0)
                b_logs(0)
                b_weights(1)
                keep_turned(2, 1)
            if prev:
                act.wait_ge(out_written, outs.next())
                act.activation(o_hi[:, bass.ds(pair - 1, 1), :], outp[:], ACT.Copy).then_inc(hi_done, 1)
                act.wait_ge(lo_done, b_lows.at())
                act.activation(o_raw[:], outp[:], ACT.Copy).then_inc(out_read, 1)
                b_lows.next()

        sq = Tally()

        def out_squares(m):
            def one(f, k):
                act.wait_ge(lin_read, lins.next())
                act.wait_ge(sum_added, sq.at(1))
                act.activation(squares[:, k, :], m[:, bass.ds(f, 1), :], ACT.Square).then_inc(square_done, 1)
                sq.next()

            with Turns(act, KD // 2, [(lins, 2), (sq, 2)]) as i:
                for k in range(2):
                    one(2 * i + k, k)

        xs = Tally()

        def norm_in(names, ready=x_ready, counts=None, source=x, width=SEQ, arrivals=None):
            counts = xs if counts is None else counts
            for f in range(KD):
                if ready is not None:
                    act.wait_ge(ready, counts.next())
                if arrivals and f % (KD // X_PARTS) == 0:
                    act.wait_ge(arrivals[f // (KD // X_PARTS)], 16)
                for name, hi in names:
                    act.activation(hi[:, f, :], source[:, f, :], ACT.Copy, scale=gain(name, f)).then_inc(hi_done, 1)
                act.wait_ge(sum_added, sq.at(1))
                act.activation(squares[:, f % 2, 0:width], source[:, f, :], ACT.Square).then_inc(square_done, 1)
                sq.next()

        def ffn():
            def one(j, u):
                act.wait_ge(lin_read, lins.next())
                act.activation(gate_s[:, u, :], gate_s[:, u, :], ACT.Silu).then_inc(silu_done, 1)
                lins.next()
                act.wait_ge(act_ready, acts.next())
                act.activation(act_hi[:, bass.ds(j, 1), :], up_s[:, u, :], ACT.Copy).then_inc(hi_done, 1)

            for u in range(2):
                one(u, u)
            with Turns(act, FF_TILES // 2 - 1, [(lins, 4), (acts, 2)]) as i:
                for u in range(2):
                    one(2 * i + (u + 2), u)

        acts = Tally()

        act.sem_inc(sum_added, 2)
        act.wait_ge(const_done, 2)
        act.dma_start(a_t[:, 0, 0, :], ap["tables"]).then_inc(tables_loaded, 16)
        act.dma_start(inverse_counts[:], ap["inverse_counts"]).then_inc(tables_loaded, 16)
        act.dma_start(rope[:], ap["rope"]).then_inc(tables_loaded, 16)
        act.dma_start(rel[:], ap["rel"]).then_inc(tables_loaded, 16)
        act.wait_ge(params_loaded, 16)
        norm_in([("mix_pre0", h_hi)], ready=None, arrivals=x_loaded)
        to_rstd(rstd[:], D, rstd_done, outs)
        act.wait_ge(rel_written, 1)
        for half in range(2):
            i = act.activation(rel_rows[:, half * (REL_SPAN // 2):(half + 1) * (REL_SPAN // 2)],
                               score[0:N_REL_HEADS, 0, half, 0:REL_SPAN // 2], ACT.Copy)
        i.then_inc(rel_copied, 1)
        act.wait_ge(rel_copied, 1)
        act.dma_start(rel_dram, rel_rows[:]).then_inc(rel_stored, 16)
        act.wait_ge(lam_summed, 1)
        act.activation(lam_exp[:], score[:, 1, 0, 0:2], ACT.Exp).then_inc(lam_done, 1)
        lins.n = 2
        a_period(0, 0, False, True, True)
        with Turns(act, 3, [(negs, 8), (turned, 10), (outs, 4), (subs, 2)]) as i:
            a_period(1, 2 * i + 1)
            a_period(0, 2 * i + 2)
        a_period(1, 7, True, True, False)
        a_period(0, 8, True, False, False)
        lins.n += 5 * A_PAIRS
        act.wait_ge(rel_stored, 16)
        out_squares(m_attn)
        to_rstd(rstd_m[:], D, rstd_done, outs)
        norm_in([("ffn_pre0", h_hi)])
        to_rstd(rstd[:], D, rstd_done, outs)
        ffn()
        out_squares(m_ffn)
        to_rstd(rstd_m[:], D, rstd_done, outs)
        norm_in([("mix_pre1", h_hi), ("kv", g_hi)])
        to_rstd(rstd[:], D, rstd_done, outs)
        scored.n = QT * A_PAIRS
        act.sem_inc(score_copied, 2)
        b_period(0, 0, False, True, True)
        with Turns(act, 3, [(step, 8), (copied, 8), (scored, 8), (sticks, 8), (turned, 14), (outs, 2), (b_lows, 2)]) as i:
            b_period(1, 2 * i + 1)
            b_period(0, 2 * i + 2)
        b_period(1, 7, True, True, False)
        b_period(0, 8, True, False, False)
        lins.n += 3 * A_PAIRS
        out_squares(m_attn)
        to_rstd(rstd_m[:], D, rstd_done, outs)
        norm_in([("ffn_pre1", h_hi)])
        to_rstd(rstd[:], D, rstd_done, outs)
        ffn()
        out_squares(m_ffn)
        to_rstd(rstd_m[:], D, rstd_done, outs)
        act.sem_inc(relu_done, 2)
        act.sem_inc(mem_exp, 2)
        act.dma_start(bias[:], toeplitz).then_inc(bias_loaded, 16)
        norm_in([("norm0", h_hi)])
        to_rstd(rstd[:], D, rstd_done, outs)
        scored.n = 2 * QT * A_PAIRS
        ready_y = Tally()

        def index_relu(t):
            n = P * (t + 1)
            for pair in range(IDX_PAIRS):
                act.wait_ge(score_written, scored.next())
                act.wait_ge(index_done, relued.at(1))
                act.activation(relu_s[:, relued.n % 2, :, 0:n], score[:, relued.n % 2, :, 0:n], ACT.Relu).then_inc(
                    relu_done, 1)
                relued.next()

        relued = Tally()

        def keep(out, chunks):
            act.wait_ge(turn_written, turned.next())
            act.activation(out, turn[:, 0:chunks * P].rearrange("p (c n) -> p c n", n=P),
                           ACT.Copy).then_inc(turn_read, 1)

        def sparse_exp(t, slot):
            act.wait_ge(negmax_done, negs.next())
            for e in range(2):
                i = act.activation(sparse_w[t][:, e, :], sparse_w[t][:, e, :], ACT.Exp,
                                   bias=negmax[:, slot, e:e + 1], accum_out=rowsum[:, slot, e:e + 1])
            i.then_inc(exp_done, 1)

        def sparse_keep(t):
            if t > 1:
                for e in range(2):
                    keep(a2_t[:, e, 0:t + 1, t * P:(t + 1) * P], t + 1)
            else:
                keep_two(a2_t, t, t + 1)

        def keep_two(out, t, chunks):
            act.wait_ge(turn_written, turned.next())
            act.activation(out[:, :, 0:chunks, t * P:(t + 1) * P],
                           turn[:, 0:2 * chunks * P].rearrange("p (e c n) -> p e c n", e=2, n=P),
                           ACT.Copy).then_inc(turn_read, 1)

        def take_out():
            act.wait_ge(out_written, outs.next())
            act.activation(o_raw[:], outp[:], ACT.Copy).then_inc(out_read, 1)

        def y_hi(y, f):
            act.wait_ge(y_ready, ready_y.next())
            act.activation(y[0][:, f, :], y_now[:], ACT.Copy).then_inc(hi_done, 1)

        def mem_soft(t, slot):
            act.wait_ge(negmax_done, negs.next())
            for e in range(2):
                i = act.activation(mem_w[:, t, e, :], score[:, slot, e, 0:MEM], ACT.Exp,
                                   bias=negmax[:, slot, e:e + 1], accum_out=rowsum[:, slot, e:e + 1])
            i.then_inc(mem_exp, 1)

        def two_layer(layer):
            lins.n += H_TILES + 2
            act.wait_ge(turn_written, turned.next())
            act.activation(iw[:], turn[:].rearrange("p (c n) -> p c n", n=P)[:, :, 64:72], ACT.Copy,
                           scale=IDX_SCALE).then_inc(turn_read, 1)
            for t in (3, 2, 1):
                index_relu(t)
                lins.n += H_TILES
                if t == 1:
                    for f in range(H_TILES):
                        keep(av[:, :, f * P:(f + 1) * P], QT)
            for f in range(H_TILES):
                act.wait_ge(lin_read, lins.next())
                act.activation(az[:, f, :], az[:, f, :], ACT.Silu).then_inc(silu_done, 1)
            steps = [(pair, t) for pair in range(H_TILES) for t in SPARSE_ORDER]
            for n in range(len(steps) + 2):
                if n > 4 and n % 4 == 3:
                    take_out()
                if n > 1:
                    sparse_keep(steps[n - 2][1])
                if n < len(steps):
                    sparse_exp(steps[n][1], n % 2)
                if n > 4 and n % 4 == 3:
                    y_hi(y_attn, n // 4 - 1)
            take_out()
            y_hi(y_attn, H_TILES - 1)
            lins.n += H_TILES
            scored.n += QT * H_TILES
            act.dma_start(mem[:], ap["mem_t"].rearrange("c p n -> p c n")).then_inc(mem_loaded, 16)
            act.wait_ge(mem_loaded, 16 * (layer + 1))
            norm_in([(f"mem_norm{layer}", mem_hi)], None, None, mem, MEM)
            to_rstd(rstd_m[:, 0:MEM], D, rstd_done, outs)
            for kind, f in MEM_ORDER:
                lins.next()
                if kind == "z":
                    act.wait_ge(lin_read, lins.at())
                    act.activation(mz[:, f, :], mz[:, f, :], ACT.Silu).then_inc(silu_done, 1)
                if kind == "v":
                    keep(mv[:, :, f * P:(f + 1) * P], MEM_CHUNKS)
            act.dma_start(pool_w[:], ap["pool_w"][layer]).then_inc(pool_loaded, 16)
            steps = [(pair, t) for pair in range(H_TILES // 2) for t in (3, 2, 1, 0)]
            for n in range(len(steps) + MEM_LAG):
                if n < len(steps):
                    mem_soft(steps[n][1], n % 2)
                if n >= MEM_LAG:
                    pair, t = steps[n - MEM_LAG]
                    if pair and t == 3:
                        for e in range(2):
                            take_out()
                            y_hi(y_mem, 2 * (pair - 1) + e)
                    keep_two(mem_a, t, MEM_CHUNKS)
            for e in range(2):
                take_out()
                y_hi(y_mem, H_TILES - 2 + e)
            scored.n += QT * H_TILES // 2
            for g in range(POOL_GROUPS):
                lins.next()
                act.wait_ge(lin_read, lins.next())
                act.activation(pool_z[:], pool_z[:], ACT.Silu).then_inc(silu_done, 1)
                act.wait_ge(lin_read, lins.next())
                act.activation(y_pool[0][:, g, :], y_now[:], ACT.Copy).then_inc(hi_done, 1)
            def merge(f, u):
                for b in range(3):
                    act.wait_ge(lin_read, lins.next())
                    act.activation(gates[:, u, b, :], gates[:, u, b, :], ACT.Sigmoid).then_inc(silu_done, 1)
                lins.n += 3
                act.wait_ge(gated, ready_sum.next())
                act.activation(sum_hi[:, bass.ds(f, 1), :], merged[:, u, :], ACT.Copy).then_inc(hi_done, 1)

            with Turns(act, KD // 2, [(lins, 12), (ready_sum, 2)]) as i:
                for u in range(2):
                    merge(2 * i + u, u)
            norm_in([(f"norm{layer + 1}", h_hi)] if layer + 1 < LAYERS else [], lin_read, lins)
            to_rstd(rstd[:], D, rstd_done, outs)

        ready_sum = Tally()
        for layer in range(LAYERS):
            two_layer(layer)

    @block.vector
    def _(dve):
        step = Tally()
        dve.sem_inc(lin_read, 2)

        def do(ins):
            ins.then_inc(v_step, 1)
            step.next()

        def settle():
            dve.wait_ge(v_step, step.at())

        lins, reads = Tally(), Tally(2)
        exps, scored, logs, silus, his, sqs, rs, subs = (Tally() for _ in range(8))

        def evacuate(out, factor, source_scale=1.0, width=SEQ, spare=None):
            dve.wait_ge(lin_written, lins.next())
            bank = lin[:, (lins.n - 1) % 2, 0:width] if spare is None else spare
            dve.scalar_tensor_tensor(out, bank, source_scale, factor, ALU.mult,
                                     ALU.mult).then_inc(lin_read, 1)
            reads.next()

        def rope(which, out):
            dve.wait_ge(lin_written, lins.next())
            bank = (lins.n - 1) % 2
            dve.tensor_tensor(rot_sin[:], lin[:, bank, :], sin, ALU.mult).then_inc(lin_read, 1)
            reads.next()
            do(dve.tensor_tensor(out, plain[:, which, :], cos, ALU.mult))
            dve.wait_ge(lin_read, reads.at())
            settle()
            dve.tensor_tensor(out, out, rot_sin[:], ALU.add).then_inc(qk_ready, 1)

        def maxima(t):
            n = P * (t + 1)
            dve.wait_ge(score_written, scored.next())
            slot = (scored.n - 1) % 2
            dve.tensor_reduce(negmax[:, slot, :], score[:, slot, :, 0:n], AX.X, ALU.max,
                              negate=True).then_inc(negmax_done, 1)

        combined = Tally()

        def combine(t):
            w = pair_w[t]
            dve.wait_ge(exp_done, exps.next())
            slot = (exps.n - 1) % 2
            if combined.turn is not None or combined.n:
                dve.wait_ge(mixed, combined.at())
            do(dve.reciprocal(rinv[:], rowsum[:, slot, :]))
            settle()
            do(dve.tensor_scalar(w[:, 1, :], w[:, 1, :], rinv[:, 1:2], neg_lam[:, 0:1], ALU.mult, ALU.mult))
            settle()
            dve.scalar_tensor_tensor(w[:, 0, :], w[:, 0, :], rinv[:, 0:1], w[:, 1, :], ALU.mult,
                                     ALU.add).then_inc(mixed, 1)
            combined.next()

        def a_period(parity, pair, prev=True, cur=True, nxt=True):
            other = 1 - parity
            if cur:
                maxima(3)
            if prev:
                combine(0)

            if nxt:
                evacuate(plain[:, 0, :], rstd[:], 0.125)
            if cur:
                maxima(2)
                combine(3)

            if nxt:
                evacuate(plain[:, 1, :], rstd[:])
            if cur:
                maxima(1)
                combine(2)
            if nxt:
                rope(0, q_now[:, other, :])
                evacuate(v_t[:], rstd[:])

            if cur:
                maxima(0)
                combine(1)
            if nxt:
                rope(1, k_now[:, other, :])
            if prev:
                dve.wait_ge(sub_rstd, subs.next())
                dve.tensor_tensor(o_sq[:], o_raw[:], o_rstd[:], ALU.mult).then_inc(sub_scaled, 1)
                dve.wait_ge(hi_done, his.next())
                dve.scalar_tensor_tensor(o_lo[:, bass.ds(pair - 1, 1), :], o_sq[:], sub_gain[:, 0:1],
                                         o_hi[:, bass.ds(pair - 1, 1), :].bitcast(F32), ALU.mult,
                                         ALU.subtract).then_inc(lo_done, 1)

        def b_sticks(t):
            n = P * (t + 1)
            dve.wait_ge(logs_done, logs.next())
            z = probs[:, (logs.n - 1) % 2, :, 0:n]
            sums_at = pair_w[t][:]
            do(dve.scalar_tensor_tensor(softplus[:, :, 0:n], z, 0.0, sums_at, ALU.max, ALU.add))
            settle()
            for e in range(2):
                back = softplus[:, e, 0:n][:, ::-1]
                do(dve.tensor_tensor_scan(sums_at[:, e, :][:, ::-1], back, back, 0.0, ALU.add, ALU.bypass))
            settle()
            dve.tensor_tensor(sums_at, z, sums_at, ALU.subtract).then_inc(sticks_done, 1)

        def b_period(parity, pair, prev=True, cur=True, nxt=True):
            other = 1 - parity
            if cur:
                b_sticks(3)
            if nxt:
                evacuate(q_now[:, other, :], rstd[:], 0.125)
            if cur:
                b_sticks(2)
            if nxt:
                evacuate(k_now[:, other, :], rstd[:])
            if cur:
                b_sticks(1)
                b_sticks(0)
            if nxt:
                evacuate(v_t[:], rstd[:])
            if prev:
                dve.wait_ge(hi_done, his.next())
                dve.wait_ge(out_read, outr.next())
                dve.tensor_tensor(o_lo[:, bass.ds(pair - 1, 1), :], o_raw[:],
                                  o_hi[:, bass.ds(pair - 1, 1), :].bitcast(F32), ALU.subtract).then_inc(lo_done, 1)

        outr = Tally()

        def add_square(first, k, width=SEQ):
            dve.wait_ge(square_done, sqs.next())
            total, new = square_sum[:, 0:width], squares[:, k, 0:width]
            if first:
                i = dve.tensor_copy(total, new)
            else:
                i = dve.tensor_tensor(total, total, new, ALU.add)
            i.then_inc(sum_added, 1)
            dve.wait_ge(sum_added, added.next())

        added = Tally(2)

        def out_tiles(m):
            def tile(f, k):
                dve.wait_ge(lin_written, lins.next())
                dve.tensor_copy(m[:, bass.ds(f, 1), :], lin[:, k, :]).then_inc(lin_read, 1)
                reads.next()

            tile(0, 0)
            tile(1, 1)
            add_square(True, 0)
            with Turns(dve, KD // 2 - 1, [(lins, 2), (reads, 2), (sqs, 2), (added, 2)]) as i:
                tile(2 * i + 2, 0)
                add_square(False, 1)
                tile(2 * i + 3, 1)
                add_square(False, 0)
            add_square(False, 1)

        def norm_in(names, m=None, post=None):
            if m is not None:
                dve.wait_ge(rstd_done, rs.next())
            for f in range(KD):
                if m is not None:
                    do(dve.scalar_tensor_tensor(m[:, f, :], m[:, f, :], gain(post, f), rstd_m[:], ALU.mult, ALU.mult))
                if f:
                    low_parts(names, f - 1)
                if m is not None:
                    settle()
                    dve.tensor_tensor(x[:, f, :], x[:, f, :], m[:, f, :], ALU.add).then_inc(x_ready, 1)
                    xs.next()
                if f:
                    add_square(f == 1, (f - 1) % 2)
                if m is not None:
                    dve.wait_ge(x_ready, xs.at())
            finish(names, KD - 1)

        xs = Tally()

        def low_parts(names, f, source=x):
            for name, hi, lo in names:
                dve.wait_ge(hi_done, his.next())
                dve.scalar_tensor_tensor(lo[:, f, :], source[:, f, :], gain(name, f), hi[:, f, :].bitcast(F32), ALU.mult,
                                         ALU.subtract).then_inc(h_ready, 1)

        def finish(names, f, source=x, width=SEQ):
            low_parts(names, f, source)
            add_square(f == 0, f % 2, width)

        def ffn():
            def one(j, u, lagging, spares=(None, None)):
                evacuate(gate_s[:, u, :], rstd[:], spare=spares[0])
                if lagging:
                    low(j - 1, 1 - u)
                evacuate(up_s[:, u, :], rstd[:], spare=spares[1])
                dve.wait_ge(silu_done, silus.next())
                dve.wait_ge(lin_read, reads.at())
                dve.tensor_tensor(up_s[:, u, :], gate_s[:, u, :], up_s[:, u, :], ALU.mult).then_inc(act_ready, 1)
                dve.wait_ge(act_ready, acts.next())

            def low(j, u):
                dve.wait_ge(hi_done, his.next())
                dve.tensor_tensor(act_lo[:, bass.ds(j, 1), :], up_s[:, u, :],
                                  act_hi[:, bass.ds(j, 1), :].bitcast(F32), ALU.subtract).then_inc(lo_done, 1)

            one(0, 0, False)
            one(1, 1, True, SPARE[0:2])
            one(2, 0, True, SPARE[2:4])
            one(3, 1, True)
            with Turns(dve, FF_TILES // 2 - 2, [(lins, 4), (reads, 4), (silus, 2), (acts, 2), (his, 2)]) as i:
                for u in range(2):
                    one(2 * i + (u + 4), u, True)
            low(FF_TILES - 1, 1)

        acts = Tally()
        dve.memset(ones[:], 1.0).then_inc(const_done, 1)
        dve.memset(eps[:], EPS).then_inc(const_done, 1)
        dve.wait_ge(params_loaded, 16)
        lam = params[0:64, LAMBDA_AT:LAMBDA_AT + 4]
        dve.tensor_tensor(lam_prod[:], lam[:, 0:2], lam[:, 2:4], ALU.mult).then_inc(lam_ready, 1)
        do(dve.tensor_scalar(sub_gain[:], params[:, SUBLN_AT:SUBLN_AT + 1], 1.0 - LAMBDA_INIT, None, ALU.mult))
        norm_in([("mix_pre0", h_hi, h_lo)])
        dve.wait_ge(tables_loaded, 64)
        dve.tensor_copy(tables[:], a_t[:, 0, 0, :]).then_inc(const_done, 1)
        dve.wait_ge(rstd_done, rs.next())
        evacuate(plain[:, 0, :], rstd[:], 0.125)
        evacuate(plain[:, 1, :], rstd[:])
        evacuate(v_t[:], rstd[:], spare=SPARE[3])
        rope(0, q_now[:, 0, :])
        dve.wait_ge(qk_ready, 1)
        rope(1, k_now[:, 0, :])
        dve.wait_ge(lam_done, 1)
        do(dve.tensor_tensor(neg_lam[:], lam_exp[:, 1:2], lam_exp[:, 0:1], ALU.subtract))
        settle()
        do(dve.tensor_scalar(neg_lam[:], neg_lam[:], -LAMBDA_INIT, None, ALU.add))
        exps.n = 2
        a_period(0, 0, False, True, True)
        with Turns(dve, 3, [(step, 20), (lins, 10), (reads, 10), (exps, 8), (scored, 8), (subs, 2), (his, 2),
                            (combined, 8)]) as i:
            a_period(1, 2 * i + 1)
            a_period(0, 2 * i + 2)
        a_period(1, 7, True, True, False)
        a_period(0, 8, True, False, False)
        out_tiles(m_attn)
        norm_in([("ffn_pre0", h_hi, h_lo)], m_attn, "mix_post0")
        dve.wait_ge(rstd_done, rs.next())
        ffn()
        out_tiles(m_ffn)
        norm_in([("mix_pre1", h_hi, h_lo), ("kv", g_hi, g_lo)], m_ffn, "ffn_post0")
        dve.wait_ge(rstd_done, rs.next())
        outr.n = 1 + 1 + 2 * A_PAIRS + 4
        evacuate(q_now[:, 0, :], rstd[:], 0.125)
        evacuate(k_now[:, 0, :], rstd[:])
        evacuate(v_t[:], rstd[:], spare=SPARE[3])
        b_period(0, 0, False, True, True)
        with Turns(dve, 3, [(step, 24), (lins, 6), (reads, 6), (logs, 8), (his, 2), (outr, 2)]) as i:
            b_period(1, 2 * i + 1)
            b_period(0, 2 * i + 2)
        b_period(1, 7, True, True, False)
        b_period(0, 8, True, False, False)
        out_tiles(m_attn)
        norm_in([("ffn_pre1", h_hi, h_lo)], m_attn, "mix_post1")
        dve.wait_ge(rstd_done, rs.next())
        ffn()
        out_tiles(m_ffn)
        norm_in([("norm0", h_hi, h_lo)], m_ffn, "ffn_post1")
        dve.wait_ge(rstd_done, rs.next())
        dve.sem_inc(index_done, 2)
        dve.sem_inc(biased, 2)
        scored.n = 2 * QT * A_PAIRS
        relus, ready_y = Tally(2), Tally()
        mem_exps = Tally(2)
        outr.n += 4

        def index_sum(t):
            n = P * (t + 1)
            for pair in range(IDX_PAIRS):
                dve.wait_ge(relu_done, relus.next())
                slot = (relus.n - 1) % 2
                for e in range(2):
                    head = 2 * pair + e
                    weight = iw[:, t, head:head + 1]
                    if head == 0:
                        i = dve.tensor_scalar(index[t][:], relu_s[:, slot, e, 0:n], weight, None, ALU.mult)
                    else:
                        i = dve.scalar_tensor_tensor(index[t][:], relu_s[:, slot, e, 0:n], weight, index[t][:],
                                                     ALU.mult, ALU.add)
                    if e:
                        i.then_inc(index_done, 1)
                        dve.wait_ge(index_done, indexed.next())
                    else:
                        do(i)
                        settle()
            do(dve.memset(index[t][0:CHUNK, n - CHUNK:n], NEG))
            settle()

        indexed = Tally(2)

        def top_round(t):
            do(dve.max(top8[:], index[t][:]))
            settle()
            do(dve.match_replace(index[t][:], top8[:], index[t][:], TAKEN))
            settle()

        def choose(t):
            do(dve.tensor_scalar(chosen[:, t, 0:P * (t + 1)], index[t][:], TAKEN / 2, NEG, ALU.is_ge, ALU.mult))
            settle()

        def top_rounds(first, count):
            per_tile = TOPK // 8
            for n in range(first, first + count):
                t = 3 - n // per_tile
                top_round(t)
                if n % per_tile == per_tile - 1:
                    choose(t)
            return first + count

        def sparse_front(pair, t, slot):
            n, w = P * (t + 1), sparse_w[t][:]
            biases_back = bias[:, 2 * pair:2 * pair + 2, P * t + P - n:P * t + P][:, :, ::-1]
            dve.wait_ge(score_written, scored.next())
            dve.tensor_tensor(w, score[:, slot, :, 0:n], biases_back,
                              ALU.add).then_inc(biased, 1)
            dve.wait_ge(biased, biases.next())
            do(dve.tensor_tensor(w, w, chosen[:, t:t + 1, 0:n].broadcast_to([P, 2, n]), ALU.add))
            settle()
            dve.tensor_reduce(negmax[:, slot, :], w, AX.X, ALU.max, negate=True).then_inc(negmax_done, 1)

        biases = Tally(2)

        mixes = Tally(QT * A_PAIRS)

        def normalise(weights, slot):
            dve.wait_ge(mixed, mixes.at())
            do(dve.reciprocal(rinv[:], rowsum[:, slot, :]))
            settle()
            for e in range(2):
                i = dve.tensor_scalar(weights[:, e, :], weights[:, e, :], rinv[:, e:e + 1], None, ALU.mult)
            i.then_inc(mixed, 1)
            mixes.next()

        def sparse_back(t, slot):
            dve.wait_ge(exp_done, exps.next())
            normalise(sparse_w[t], slot)

        def y_product(factor):
            dve.wait_ge(out_read, outr.next())
            dve.wait_ge(lo_done, lows.at())
            dve.tensor_tensor(y_now[:], o_raw[:], factor, ALU.mult).then_inc(y_ready, 1)

        def y_of(factor, y, f):
            y_product(factor)
            y_low(y, f)

        def y_low(y, f):
            dve.wait_ge(hi_done, his.next())
            dve.tensor_tensor(y[1][:, f, :], y_now[:], y[0][:, f, :].bitcast(F32), ALU.subtract).then_inc(lo_done, 1)
            lows.next()

        lows = Tally(2 * (KD + FF_TILES))

        def mem_front(slot):
            dve.wait_ge(score_written, scored.next())
            dve.tensor_reduce(negmax[:, slot, :], score[:, slot, :, 0:MEM], AX.X, ALU.max,
                              negate=True).then_inc(negmax_done, 1)

        body = slice(POOL_EDGE, POOL_EDGE + SEQ)

        def pool_means(g):
            dve.wait_ge(lin_read, reads.at())
            source = pool_u
            for level in range(g + 1):
                out = pool_b if source is pool_a else pool_a
                back = slice(POOL_EDGE - 2 ** level, POOL_EDGE + SEQ - 2 ** level)
                do(dve.tensor_tensor(out[:, body], source[:, body], source[:, back], ALU.add))
                settle()
                source = out
            inverse = inverse_counts[:, g, :]
            do(dve.tensor_tensor(edge[:], source[:, POOL_EDGE:2 * POOL_EDGE], inverse, ALU.mult))
            do(dve.scalar_tensor_tensor(pooled[:], source[:, body], 0.5 ** (g + 1), pool_u[:, body], ALU.mult,
                                        ALU.subtract))
            settle()
            dve.tensor_tensor(pooled[:, 0:POOL_EDGE], edge[:], pool_u[:, POOL_EDGE:2 * POOL_EDGE],
                              ALU.subtract).then_inc(pool_ready, 1)

        def two_layer(layer):
            for f, spare in enumerate((None, None, *SPARE[0:2])):
                evacuate(iq[:, f, :], rstd[:], spare=spare)
            evacuate(ik[:], rstd[:], spare=SPARE[2])
            evacuate(aq[:, 0, :], rstd[:], 0.125, spare=SPARE[3])
            dve.wait_ge(lin_written, lins.next())
            dve.tensor_copy(ik[64:128, :], lin[64:128, (lins.n - 1) % 2, :]).then_inc(lin_read, 1)
            reads.next()
            evacuate(aq[:, 1, :], rstd[:], 0.125)
            dve.wait_ge(turn_read, iw_turned[layer])
            taken = 0
            for t, out, factor, rounds in ((3, aq, 0.125, (2, 3, 3, 3)), (2, ak, 1.0, (3, 3, 3, 4)),
                                           (1, None, 1.0, (4, 3, 3, 3)), (0, az, 1.0, (3, 3, 3, 2))):
                if t:
                    index_sum(t)
                for f in range(H_TILES):
                    if out is not aq or f > 1:
                        evacuate(v_turn_in[f % 2][:] if out is None else out[:, f, :], rstd[:], factor)
                    taken = top_rounds(taken, rounds[f])
            assert taken == 3 * TOPK // 8
            do(dve.memset(chosen[:, 0, 0:P], 0.0))
            settle()
            do(dve.memset(chosen[0:CHUNK, 0, P - CHUNK:P], NEG))
            silus.n += H_TILES
            dve.wait_ge(silu_done, silus.at())
            dve.wait_ge(bias_loaded, 16)
            scored.n += 3 * IDX_PAIRS
            steps = [(pair, t) for pair in range(H_TILES) for t in SPARSE_ORDER]
            for n, (pair, t) in enumerate(steps):
                sparse_front(pair, t, n % 2)
                if n:
                    sparse_back(steps[n - 1][1], (n - 1) % 2)
                if pair and n % 4 == 0:
                    evacuate(mq[:, pair - 1, :], rstd[:], MEM_SCALE)
                if pair and n % 4 == 3:
                    y_product(az[:, pair - 1, :])
                if pair > 1 and n % 4 == 0:
                    y_low(y_attn, pair - 2)
            sparse_back(SPARSE_ORDER[-1], 1)
            evacuate(mq[:, H_TILES - 1, :], rstd[:], MEM_SCALE)
            y_low(y_attn, H_TILES - 2)
            y_of(az[:, H_TILES - 1, :], y_attn, H_TILES - 1)
            dve.wait_ge(mem_loaded, 16 * (layer + 1))
            for f in range(KD):
                finish([(f"mem_norm{layer}", mem_hi, mem_lo)], f, mem, MEM)
                if f % 4 == 3:
                    evacuate(mz[:, f // 4, :], rstd[:])
            for n, (kind, f) in enumerate(MEM_ORDER[2:]):
                if n == 0:
                    dve.wait_ge(rstd_done, rs.next())
                    outr.n += 1
                if kind == "z":
                    evacuate(mz[:, f, :], rstd[:])
                elif kind == "k":
                    evacuate(mk[:, f, :], rstd_m[:, 0:MEM], 1.0, MEM)
                else:
                    evacuate(mem_v_t[f % 2], rstd_m[:, 0:MEM], 1.0, MEM)
            silus.n += H_TILES
            dve.wait_ge(silu_done, silus.at())
            steps = [(pair, t) for pair in range(H_TILES // 2) for t in (3, 2, 1, 0)]
            for t in (pool_u, pool_a, pool_b):
                do(dve.memset(t[:, 0:POOL_EDGE], 0.0))
            settle()
            for n in range(len(steps) + 1):
                if n < len(steps):
                    mem_front(n % 2)
                if n:
                    dve.wait_ge(mem_exp, mem_exps.next())
                    normalise(mem_w[:, steps[n - 1][1]], (n - 1) % 2)
                if n == QT + 1:
                    evacuate(pool_u[:, body], rstd[:])
                if n == QT + 2:
                    pool_means(0)
                if n == len(steps):
                    evacuate(pool_z[:], rstd[:])
                if n == QT + MEM_LAG:
                    for e in range(2):
                        y_of(mz[:, e, :], y_mem, e)
            for e in range(2):
                y_of(mz[:, H_TILES - 2 + e, :], y_mem, H_TILES - 2 + e)
            for g in range(POOL_GROUPS):
                if g:
                    evacuate(pool_u[:, body], rstd[:])
                    pool_means(g)
                if g:
                    evacuate(pool_z[:], rstd[:])
                dve.wait_ge(silu_done, silus.next())
                dve.wait_ge(lin_written, lins.next())
                dve.wait_ge(lo_done, lows.at())
                scale_at = POOL_SCALE_AT + POOL_GROUPS * layer + g
                dve.scalar_tensor_tensor(y_now[:], lin[:, (lins.n - 1) % 2, :], params[:, scale_at:scale_at + 1],
                                         pool_z[:], ALU.mult, ALU.mult).then_inc(lin_read, 1)
                reads.next()
                y_low(y_pool, g)

            def merge(f, u):
                for b in range(3):
                    evacuate(gates[:, u, b, :], rstd[:])
                for b in range(3):
                    dve.wait_ge(silu_done, silus.next())
                    dve.wait_ge(lin_written, lins.next())
                    out = merged[:, u, :] if b == 0 else part[:]
                    dve.tensor_tensor(out, lin[:, (lins.n - 1) % 2, :], gates[:, u, b, :], ALU.mult).then_inc(
                        lin_read, 1)
                    dve.wait_ge(lin_read, reads.next())
                    if b:
                        i = dve.tensor_tensor(merged[:, u, :], merged[:, u, :], part[:], ALU.add)
                        if b == 1:
                            do(i)
                            settle()
                        else:
                            i.then_inc(gated, 1)
                            dve.wait_ge(gated, gate_n.next())
                dve.wait_ge(hi_done, his.next())
                dve.tensor_tensor(sum_lo[:, bass.ds(f, 1), :], merged[:, u, :],
                                  sum_hi[:, bass.ds(f, 1), :].bitcast(F32), ALU.subtract).then_inc(lo_done, 1)
                lows.next()

            with Turns(dve, KD // 2, [(lins, 12), (reads, 12), (silus, 6), (gate_n, 2), (his, 2), (step, 2),
                                             (lows, 2)]) as i:
                for u in range(2):
                    merge(2 * i + u, u)
            names = [(f"norm{layer + 1}", h_hi, h_lo)] if layer + 1 < LAYERS else []
            for f in range(KD):
                dve.wait_ge(lin_written, lins.next())
                dve.tensor_tensor(x[:, f, :], x[:, f, :], lin[:, (lins.n - 1) % 2, :], ALU.add).then_inc(lin_read, 1)
                dve.wait_ge(lin_read, reads.next())
                if f:
                    finish(names, f - 1)
            finish(names, KD - 1)
            dve.wait_ge(rstd_done, rs.next())
            outr.n += 1

        gate_n = Tally()
        turns_at = 1 + 5 * A_PAIRS + 7 * A_PAIRS
        per_layer = 1 + H_TILES + 6 * H_TILES + H_TILES + QT * H_TILES // 2
        iw_turned = [turns_at + 1 + per_layer * layer for layer in range(LAYERS)]
        for layer in range(LAYERS):
            two_layer(layer)
        for f in range(KD):
            dve.scalar_tensor_tensor(result[:, f, :], x[:, f, :], gain("final", f), rstd[:], ALU.mult,
                                     ALU.mult).then_inc(x_ready, 1)

    block.__exit__(None, None, None)


def layout(inputs):
    def tiles(w):
        k, n = w.shape
        return w.reshape(k // P, P, n // P, P).transpose(2, 0, 1, 3)

    def blocks(t, shares=(BLOCK_TILES,)):
        full = np.zeros((t.shape[0], len(shares), P, BLOCK_TILES, P), t.dtype)
        for n, share in enumerate(shares):
            at = sum(shares[:n])
            full[:, n, :, :share] = t[:, at:at + share].transpose(0, 2, 1, 3)
        return full.reshape(-1, P, BLOCK_TILES * P)

    def woven(*parts):
        return np.stack(parts, axis=1).reshape(-1, *parts[0].shape[1:])

    def first_grouped(t, n):
        return [blocks(t[:n].swapaxes(0, 1).reshape(n, KD, P, P)), blocks(t[n:])]

    def ffn(layer):
        both = tiles(inputs["ffn_w_gate_up"][layer])
        return first_grouped(woven(both[:FF_TILES], both[FF_TILES:]), 4) + [blocks(tiles(inputs["ffn_w_down"][layer]), DOWN_SHARES)]

    qkv = tiles(inputs["a_w_qkv"][0])
    kv = tiles(inputs["kv_w"])
    stream = first_grouped(woven(qkv[0:8], qkv[8:16], qkv[16:24]), 3) 
    stream += first_grouped(tiles(inputs["a_w_o"][0]), 2) + ffn(0)
    stream += first_grouped(woven(tiles(inputs["b_w_q"][0]), kv[0:8], kv[8:16]), 3)
    stream += first_grouped(tiles(inputs["b_w_o"][0]), 2) + ffn(1)
    edges = np.cumsum([512, 512, 512, 512, 512, 512, 512, 64, 8, 512, 512])
    for n in range(LAYERS):
        pool_u, pool_z, q, k, v, z, iq, ik, iw, mq, mz, gates = np.split(inputs["w_in_2"][n], edges, axis=1)
        keys = np.concatenate([ik, iw, np.zeros((D, P - ik.shape[1] - iw.shape[1]), ik.dtype)], axis=1)
        single = [keys, q, k, v, z]
        stream += [first_grouped(tiles(iq), H_TILES)[0]] + [blocks(tiles(w)) for w in single]
        stream += [blocks(tiles(mq))]
        mem_kv = tiles(inputs["w_mem_kv_2"][n])
        kinds = {"z": tiles(mz), "k": mem_kv[:H_TILES], "v": mem_kv[H_TILES:]}
        stream += [blocks(np.stack([kinds[kind][f] for kind, f in MEM_ORDER]))]
        stream += [blocks(woven(tiles(pool_u), tiles(pool_z)))]
        gate_tiles = tiles(gates).reshape(3, KD, KD, P, P)
        branch_tiles = [tiles(inputs["w_branch_2"][n, b]) for b in range(3)]
        stream += [blocks(np.concatenate([*gate_tiles, *branch_tiles], axis=1), MERGE_SHARES)]
        stream += [blocks(tiles(inputs["w_out_2"][n]))]
    weights = np.concatenate(stream)
    gains = {"kv": inputs["kv_norm_g"], "final": inputs["final_g_2"]}
    for n in range(2):
        gains |= {f"{k}{n}": inputs[f"{k}_g"][n] for k in ("mix_pre", "mix_post", "ffn_pre", "ffn_post")}
        gains |= {f"norm{n}": inputs["norm_g_2"][n], f"mem_norm{n}": inputs["mem_norm_g_2"][n]}
    params = np.zeros((P, N_PARAMS), np.float32)
    for name, at in GAIN_AT.items():
        params[:, at:at + KD] = gains[name].reshape(KD, P).T
    for n in range(2):
        params[:, POOL_SCALE_AT + 4 * n:POOL_SCALE_AT + 4 * n + 4] = inputs["pool_scale_2"][n].reshape(4, P).T
    params[:, SUBLN_AT] = inputs["a_subln_g"][0]
    for n, name in enumerate(("a_lambda_q1", "a_lambda_q2", "a_lambda_k1", "a_lambda_k2")):
        params[:64, LAMBDA_AT + n] = inputs[name][0]
    x_t = inputs["x"][0].T.reshape(KD, P, SEQ)
    rel = np.concatenate([inputs["rel_bias_2"], rel_onehot()], axis=1)
    mem_t = inputs["mem_2"][0].T.reshape(KD, P, MEM)
    pool_w = inputs["pool_w_2"].transpose(0, 2, 1, 3)
    return {"x_t": x_t, "weights": weights, "params": params, "rel": rel, "mem_t": mem_t,
            "pool_w": pool_w} | shape_tables()


def rel_onehot():
    d = P - 1 - np.arange(REL_SPAN)
    n = np.abs(d)
    far = 8 + (np.log(np.maximum(n, 1).astype(np.float32) / np.float32(8)) / np.float32(math.log(1024 / 8))
               * np.float32(8)).astype(np.int32)
    bucket = np.where(d > 0, 16, 0) + np.where(n < 8, n, np.minimum(far, 15))
    return (bucket[None, :] == np.arange(32)[:, None]).astype(np.float32)


def shape_tables():
    t = np.zeros((P, N_TABLES), np.float32)
    t[:, IDENT_AT:IDENT_AT + P] = np.eye(P)
    for head in range(2):
        for d in range(8):
            t[64 * head + d + 8, ROT_AT + 64 * head + d] = -1
            t[64 * head + d, ROT_AT + 64 * head + d + 8] = 1
    q, k = np.arange(P)[:, None], np.arange(P)[None, :]
    t[:, CAUSAL_AT:CAUSAL_AT + P] = np.where(k <= q, 0, MASKED)
    t[:, STRICT_AT:STRICT_AT + P] = np.where(k < q, 0, MASKED)
    counts = np.zeros((P, POOL_GROUPS, POOL_EDGE), np.float32)
    for g in range(POOL_GROUPS):
        counts[:, g] = 1 / np.minimum(np.arange(POOL_EDGE) + 1, 2 ** (g + 1))
    freq = np.float32(500000.0) ** (-np.arange(0, 16, 2, dtype=np.float32) / np.float32(16))
    angle = np.arange(SEQ, dtype=np.float32)[:, None] * freq[None, :]
    rope = np.zeros((P, 2, SEQ), np.float32)
    rope[:, 0] = 1
    for start in (0, 8, 64, 72):
        rope[start:start + 8, 0] = np.cos(angle).T
        rope[start:start + 8, 1] = np.sin(angle).T
    return {"tables": t, "inverse_counts": counts, "rope": rope}


def kernel(**inputs):
    from concourse import bacc
    from concourse.bass_utils import run_bass_kernel_spmd

    arrays = {name: np.ascontiguousarray(a) for name, a in layout({k: np.asarray(v) for k, v in inputs.items()}).items()}
    nc = bacc.Bacc("TRN2", target_bir_lowering=False, num_devices=1)
    ap = {name: nc.dram_tensor(name, a.shape, mybir.dt.from_np(a.dtype), kind="ExternalInput").ap()
          for name, a in arrays.items()}
    ap["out_t"] = nc.dram_tensor("out_t", (KD, P, SEQ), F32, kind="ExternalOutput").ap()
    build(nc, ap)
    result = run_bass_kernel_spmd(nc, [arrays], core_ids=[0])
    return result.results[0]["out_t"].reshape(D, SEQ).T[None]
```
